# Optimizing a Trainium2 kernel written in Bass

```python
import jax, jax.numpy as jnp
from jax import lax
import numpy as np

D_MODEL = 1024
BATCH = 1
SEQ = 256
DEPTH = 2

N_META = 16
D_ATTN = D_MODEL // 2
D_RNN = D_MODEL - D_ATTN
N_HEADS = 8
QK_NOPE = 64
QK_ROPE = 32
QK_HEAD = QK_NOPE + QK_ROPE
V_HEAD = D_ATTN // N_HEADS
Q_LORA = 384
KV_LORA = 256
ROPE_BASE = 10000.0
N_RNN_BLOCKS = 8
RNN_BLOCK = D_RNN // N_RNN_BLOCKS
CONV_W = 4
LRU_C = 8.0
D_FF = 2816
N_EXPERTS = 8
TOP_K = 2
D_FF_EXPERT = 1408
Q_BLOCK = 128
EPS = 1e-6
N_DENSE = (DEPTH + 1) // 2
N_MOE = DEPTH // 2
SPLITS = (Q_LORA, Q_LORA + KV_LORA, Q_LORA + KV_LORA + QK_ROPE, Q_LORA + KV_LORA + QK_ROPE + D_RNN)
D_IN = Q_LORA + KV_LORA + QK_ROPE + 2 * D_RNN

kernel_name = "hymba_mla_rglru_moe_trunk"

def rmsnorm(x, g):
    xf = x.astype(jnp.float32)
    y = xf * lax.rsqrt(jnp.mean(xf * xf, axis=-1, keepdims=True) + EPS)
    return (y * g.astype(jnp.float32)).astype(x.dtype)

def rope_tables(pos):
    inv_freq = ROPE_BASE ** (-jnp.arange(0, QK_ROPE, 2, dtype=jnp.float32) / QK_ROPE)
    ang = pos.astype(jnp.float32)[..., None] * inv_freq
    return jnp.cos(ang), jnp.sin(ang)

def apply_rope(x, cos, sin):
    xf = x.astype(jnp.float32)
    x1, x2 = xf[..., : QK_ROPE // 2], xf[..., QK_ROPE // 2:]
    c, s = cos[:, :, None, :], sin[:, :, None, :]
    return jnp.concatenate([x1 * c - x2 * s, x2 * c + x1 * s], axis=-1).astype(x.dtype)

def causal_block_attention(q, k, v):
    T = q.shape[1]
    bounds = sorted(set([0, N_META] + list(range(N_META + Q_BLOCK, T, Q_BLOCK)) + [T]))
    scale = QK_HEAD ** -0.5
    outs = []
    for s, e in zip(bounds[:-1], bounds[1:]):
        sc = jnp.einsum('bqhd,bkhd->bhqk', q[:, s:e], k[:, :e]).astype(jnp.float32) * scale
        mask = jnp.arange(e)[None, :] <= jnp.arange(s, e)[:, None]
        p = jax.nn.softmax(jnp.where(mask, sc, -1e30), axis=-1)
        outs.append(jnp.einsum('bhqk,bkhd->bqhd', p.astype(v.dtype), v[:, :e]))
    return jnp.concatenate(outs, axis=1)

def mla_mixer(cq, ckv, kr, cos, sin, q_norm_g, w_uq, kv_norm_g, w_ukv, q_head_g, k_head_g):
    B, T, _ = cq.shape
    q = (rmsnorm(cq, q_norm_g) @ w_uq).reshape(B, T, N_HEADS, QK_HEAD)
    kv = (rmsnorm(ckv, kv_norm_g) @ w_ukv).reshape(B, T, N_HEADS, QK_NOPE + V_HEAD)
    k_nope, v = kv[..., :QK_NOPE], kv[..., QK_NOPE:]
    k = jnp.concatenate([k_nope, jnp.broadcast_to(kr[:, :, None, :], (B, T, N_HEADS, QK_ROPE))], axis=-1)
    q = rmsnorm(q, q_head_g)
    k = rmsnorm(k, k_head_g)
    q = jnp.concatenate([q[..., :QK_NOPE], apply_rope(q[..., QK_NOPE:], cos, sin)], axis=-1)
    k = jnp.concatenate([k[..., :QK_NOPE], apply_rope(k[..., QK_NOPE:], cos, sin)], axis=-1)
    o = causal_block_attention(q, k, v)
    return o.reshape(B, T, D_ATTN)

def _lin_combine(left, right):
    a_l, b_l = left
    a_r, b_r = right
    return a_l * a_r, a_r * b_l + b_r

def rglru_mixer(xr, gate, conv_w, conv_b, w_a, b_a, w_i, b_i, lam):
    B, T, _ = xr.shape
    xp = jnp.pad(xr, ((0, 0), (CONV_W - 1, 0), (0, 0)))
    xc = conv_b + xp[:, 0:T] * conv_w[0]
    for j in range(1, CONV_W):
        xc = xc + xp[:, j:j + T] * conv_w[j]
    xb = xc.reshape(B, T, N_RNN_BLOCKS, RNN_BLOCK)
    r = jax.nn.sigmoid(jnp.einsum('btnc,ncd->btnd', xb, w_a).reshape(B, T, D_RNN) + b_a)
    i = jax.nn.sigmoid(jnp.einsum('btnc,ncd->btnd', xb, w_i).reshape(B, T, D_RNN) + b_i)
    log_a = -LRU_C * r.astype(jnp.float32) * jax.nn.softplus(-lam.astype(jnp.float32))
    a = jnp.exp(log_a)
    mult = jnp.sqrt(-jnp.expm1(2.0 * log_a))
    b = mult * i.astype(jnp.float32) * xc.astype(jnp.float32)
    _, h = lax.associative_scan(_lin_combine, (a, b), axis=1)
    return h.astype(xr.dtype) * jax.nn.gelu(gate, approximate=True)

def swiglu(x, w_g, w_u, w_d):
    return (jax.nn.silu(x @ w_g) * (x @ w_u)) @ w_d

def moe_swiglu(x, w_router, w_g, w_u, w_d):
    B, T, D = x.shape
    xt = x.reshape(-1, D)
    logits = (xt @ w_router).astype(jnp.float32)
    top_val, top_idx = lax.top_k(logits, TOP_K)
    top_w = jax.nn.softmax(top_val, axis=-1)
    gates = jnp.sum(jax.nn.one_hot(top_idx, N_EXPERTS, dtype=jnp.float32) * top_w[..., None], axis=1)
    gates = gates.astype(x.dtype)
    out = jnp.zeros_like(xt)
    for e in range(N_EXPERTS):
        h = jax.nn.silu(xt @ w_g[e]) * (xt @ w_u[e])
        out = out + (gates[:, e:e + 1] * h) @ w_d[e]
    return out.reshape(B, T, D)

def setup_inputs(seed: int = 0) -> dict:
    key = jax.random.key(seed)
    ks = iter(jax.random.split(key, 40))

    def nrm(shape, fan_in):
        return jax.random.normal(next(ks), shape, jnp.float32) * (fan_in ** -0.5)

    def gain(shape):
        return 1.0 + 0.02 * jax.random.normal(next(ks), shape, jnp.float32)

    def bias(shape):
        return 0.02 * jax.random.normal(next(ks), shape, jnp.float32)

    x = jax.random.normal(next(ks), (BATCH, SEQ, D_MODEL), jnp.float32)
    start = jax.random.randint(next(ks), (BATCH, 1), 0, 1024, dtype=jnp.int32)
    positions = (start + jnp.arange(SEQ, dtype=jnp.int32)[None, :]).astype(jnp.int32)
    meta_tokens = jax.random.normal(next(ks), (N_META, D_MODEL), jnp.float32)
    u = jax.random.uniform(next(ks), (DEPTH, D_RNN), jnp.float32, 0.9, 0.999)
    s = u ** (1.0 / LRU_C)
    lru_lambda = jnp.log(s) - jnp.log1p(-s)
    return {
        "x": x,
        "positions": positions,
        "meta_tokens": meta_tokens,
        "norm_mix_g": gain((DEPTH, D_MODEL)),
        "w_in": nrm((DEPTH, D_MODEL, D_IN), D_MODEL),
        "q_norm_g": gain((DEPTH, Q_LORA)),
        "w_uq": nrm((DEPTH, Q_LORA, N_HEADS * QK_HEAD), Q_LORA),
        "kv_norm_g": gain((DEPTH, KV_LORA)),
        "w_ukv": nrm((DEPTH, KV_LORA, N_HEADS * (QK_NOPE + V_HEAD)), KV_LORA),
        "q_head_g": gain((DEPTH, QK_HEAD)),
        "k_head_g": gain((DEPTH, QK_HEAD)),
        "conv_w": nrm((DEPTH, CONV_W, D_RNN), CONV_W),
        "conv_b": bias((DEPTH, D_RNN)),
        "w_a": nrm((DEPTH, N_RNN_BLOCKS, RNN_BLOCK, RNN_BLOCK), RNN_BLOCK),
        "b_a": bias((DEPTH, D_RNN)),
        "w_i": nrm((DEPTH, N_RNN_BLOCKS, RNN_BLOCK, RNN_BLOCK), RNN_BLOCK),
        "b_i": bias((DEPTH, D_RNN)),
        "lru_lambda": lru_lambda,
        "attn_out_g": gain((DEPTH, D_ATTN)),
        "rnn_out_g": gain((DEPTH, D_RNN)),
        "w_out": nrm((DEPTH, D_MODEL, D_MODEL), D_MODEL),
        "norm_ffn_g": gain((DEPTH, D_MODEL)),
        "ffn_w_gate": nrm((N_DENSE, D_MODEL, D_FF), D_MODEL),
        "ffn_w_up": nrm((N_DENSE, D_MODEL, D_FF), D_MODEL),
        "ffn_w_down": nrm((N_DENSE, D_FF, D_MODEL), D_FF),
        "router_w": nrm((N_MOE, D_MODEL, N_EXPERTS), D_MODEL),
        "moe_w_gate": nrm((N_MOE, N_EXPERTS, D_MODEL, D_FF_EXPERT), D_MODEL),
        "moe_w_up": nrm((N_MOE, N_EXPERTS, D_MODEL, D_FF_EXPERT), D_MODEL),
        "moe_w_down": nrm((N_MOE, N_EXPERTS, D_FF_EXPERT, D_MODEL), D_FF_EXPERT),
    }

def reference(x, positions, meta_tokens, norm_mix_g, w_in, q_norm_g, w_uq, kv_norm_g, w_ukv,
              q_head_g, k_head_g, conv_w, conv_b, w_a, b_a, w_i, b_i, lru_lambda,
              attn_out_g, rnn_out_g, w_out, norm_ffn_g, ffn_w_gate, ffn_w_up, ffn_w_down,
              router_w, moe_w_gate, moe_w_up, moe_w_down):
    B = x.shape[0]
    meta = jnp.broadcast_to(meta_tokens[None].astype(x.dtype), (B, N_META, D_MODEL))
    h = jnp.concatenate([meta, x], axis=1)
    meta_pos = jnp.broadcast_to(jnp.arange(N_META, dtype=jnp.int32)[None, :], (B, N_META))
    pos_full = jnp.concatenate([meta_pos, positions.astype(jnp.int32) + N_META], axis=1)
    cos, sin = rope_tables(pos_full)
    for l in range(DEPTH):
        u = rmsnorm(h, norm_mix_g[l])
        proj = u @ w_in[l]
        cq, ckv, kr, xr, gt = jnp.split(proj, SPLITS, axis=-1)
        att = mla_mixer(cq, ckv, kr, cos, sin, q_norm_g[l], w_uq[l], kv_norm_g[l], w_ukv[l],
                        q_head_g[l], k_head_g[l])
        rnn = rglru_mixer(xr, gt, conv_w[l], conv_b[l], w_a[l], b_a[l], w_i[l], b_i[l], lru_lambda[l])
        mix = jnp.concatenate([rmsnorm(att, attn_out_g[l]), rmsnorm(rnn, rnn_out_g[l])], axis=-1)
        h = h + mix @ w_out[l]
        u = rmsnorm(h, norm_ffn_g[l])
        if l % 2 == 0:
            j = l // 2
            h = h + swiglu(u, ffn_w_gate[j], ffn_w_up[j], ffn_w_down[j])
        else:
            j = l // 2
            h = h + moe_swiglu(u, router_w[j], moe_w_gate[j], moe_w_up[j], moe_w_down[j])
    return h[:, N_META:]


_drawn_inputs = setup_inputs


def setup_inputs(seed=0):
    import zlib

    import numpy as np

    out = dict(_drawn_inputs(seed))
    spreads = {}
    factors = {'q_norm_g': 4.028,
     'q_head_g': 3.503,
     'k_head_g': 3.426,
     'b_a': 8.0,
     'b_i': 6.374,
     'norm_ffn_g': 2.725}
    for name, (base, spread) in spreads.items():
        noise = np.random.default_rng([zlib.crc32(name.encode()), seed]).standard_normal(out[name].shape)
        drawn = base * np.exp(spread * noise) if base else spread * noise
        out[name] = __import__('jax').numpy.asarray(drawn.astype(out[name].dtype))
    for name, factor in factors.items():
        out[name] = (out[name] * factor).astype(out[name].dtype)
    return out
```

```python
import concourse.bass as bass
from concourse import mybir
from concourse.alu_op_type import AluOpType as ALU
from contextlib import ExitStack, contextmanager
import numpy as np

F32 = mybir.dt.float32
F32R = mybir.dt.float32r
I32 = mybir.dt.int32
U32 = mybir.dt.uint32
ACT = mybir.ActivationFunctionType
AX = mybir.AxisListType

P = 128
D = 1024
KD = D // P
SEQ, NMETA = 256, 16
T = SEQ + NMETA
DEPTH = 2
DH2 = D // 2
CH = DH2 // P
NH, NOPE, ROPE = 8, 64, 32
QKH = NOPE + ROPE
VH = DH2 // NH
QL, KVL = 384, 256
QC, KVC = QL // P, KVL // P
D_IN = QL + KVL + ROPE + 2 * DH2
CONV = 4
FF = 2816
FC = FF // P
NE, FE = 8, 1408
FEC = FE // P
EPS = 1e-6
TILES = [(0, NMETA), (NMETA, P), (NMETA + P, P)]

RAW = 4
SPL = 2
SLOT = 3072
GC = 256
HALF_A = 6 * P
HALF_B = FE - HALF_A

C_ID, C_LT = 0, P
C_MASK = 2 * P
C_IOTA = C_MASK + T
C_E8 = C_IOTA + 2 * P
C_ROT = C_E8 + NE
C_FREQ = C_ROT + ROPE
C_ALL = C_FREQ + 1


def constants():
    c = np.zeros((P, C_ALL), np.float32)
    c[:, C_ID:C_ID + P] = np.eye(P)
    c[:, C_LT:C_LT + P] = np.triu(np.ones((P, P)), 1)
    c[:, C_MASK + T - P:C_MASK + T] = np.triu(np.full((P, P), -1e30), 1)
    c[:, C_IOTA:C_IOTA + 2 * P] = np.arange(2 * P)
    c[:, C_E8:C_E8 + NE] = np.arange(NE)
    for m in range(ROPE // 2):
        c[NOPE + m + ROPE // 2, C_ROT + m] = -1.0
        c[NOPE + m, C_ROT + m + ROPE // 2] = 1.0
    freq = np.float32(10000.0) ** (-np.arange(0, ROPE, 2, dtype=np.float32) / np.float32(ROPE))
    c[NOPE:QKH, C_FREQ] = np.concatenate([freq, freq])
    return c


ROWS = {}
_n = 0
for _name, _k in (("norm_mix_g", KD), ("norm_ffn_g", KD), ("q_norm_g", QC), ("kv_norm_g", KVC), ("attn_out_g", CH),
                  ("rnn_out_g", CH), ("conv_w", CONV * CH), ("conv_b", CH), ("b_a", CH), ("b_i", CH),
                  ("lru_lambda", CH), ("q_head_g", 1), ("k_head_g", 1)):
    ROWS[_name] = (_n, _k)
    _n += DEPTH * _k
NROWS = _n


def tiles(l):
    return (0, 1, 2) if l < DEPTH - 1 else (1, 2)


def first_token(l):
    return TILES[tiles(l)[0]][0]


class Block:

    def __init__(self, bank, order, before, per_order=0, per_before=0):
        self.bank, self.order, self.before = bank, order, before
        self.per_order, self.per_before = per_order, per_before

    def ready(self, i=0):
        return self.order + 1 + self.per_order * i

    def emptied(self, i=0):
        return self.before + self.per_before * i


class Plan:

    def __init__(self):
        self.order, self.before, self.blocks, self.turn = 0, [0] * 8, {}, 0

    def add(self, name, bank=None):
        if bank is None:
            bank, self.turn = self.turn % 4, self.turn + 1
        self.blocks[name] = Block(bank, self.order, self.before[bank])
        self.order += 1
        self.before[bank] += 1

    def loop(self, name, banks, times):
        per = [banks.count(b) for b in range(8)]
        for j, b in enumerate(banks):
            self.blocks[name, j] = Block(b, self.order + j, self.before[b] + banks[:j].count(b), len(banks), per[b])
        self.order += len(banks) * times
        for b in range(8):
            self.before[b] += per[b] * times


class Chain:

    def __init__(self, eng, sem):
        self.eng, self.sem, self.base, self.n = eng, sem, 0, 0

    def link(self, ins):
        ins.then_inc(self.sem, 1)
        self.n += 1
        self.eng.wait_ge(self.sem, self.base + self.n)

    @contextmanager
    def loop(self, times, per):
        start = self.base + self.n
        with self.eng.Fori(0, times) as i:
            self.base, self.n = start + per * i, 0
            yield i
            assert self.n == per, self.n
        self.base, self.n = start + per * times, 0


def plan_blocks():
    pl = Plan()
    for c in range(KD):
        pl.add(("x", c))
    pl.add("vec")
    for l in range(DEPTH):
        def add(*name, bank=None):
            pl.add((l, *name), bank)
        add("n1ss", bank=4)
        add("n1bc", bank=4)
        for n, k in (("xr", CH), ("gt", CH), ("q", QC), ("kv", KVC), ("kr", 1)):
            for c in range(k):
                add(n, c)
        add("cqss", bank=4)
        add("cqbc", bank=4)
        add("kvbc", bank=5)
        for n in ("wa", "wi"):
            for c in range(CH):
                add(n, c)
        for h in range(NH):
            add("uq", h)
        for h in range(NH):
            add("kn", h)
        for t in range(3):
            add("v", t)
        add("krr")
        add("qss", bank=4)
        add("kss", bank=4)
        for h in range(NH):
            add("qr", h)
        for h in range(NH):
            add("kbc", h)
        for t in tiles(l):
            for h in range(NH):
                add("s", t, h)
            for h in range(NH):
                add("p", t, h, bank=6 + h % 2)
            add("o", t, bank=5)
            add("ot", t, bank=4)
        add("rnss", bank=4)
        add("rnbc", bank=4)
        for m in range(KD):
            add("wo", m)
        add("n2ss", bank=4)
        add("n2bc", bank=4)
        if l == 0:
            for j, b in enumerate((0, 1, 2, 3)):
                pl.add(("ff0", j), b)
            pl.loop("ff", [4, 5, 6, 7, 0, 1, 2, 3], 5)
            pl.loop("dn", [4, 5, 6, 7], 2)

        else:
            pl.add("lg", 0)
            pl.add("cum", 1)
            for t in range(2):
                for hf in range(2):
                    pl.add(("ut", t, hf))
            for t in range(2):
                for hf in range(2):
                    pl.add(("ht", t, hf))
    return pl


PER_MIX = 12
MIX_SPLIT = 10
W_IN_COLS = [(QL + KVL + ROPE, GC), (QL + KVL + ROPE + GC, GC), (QL + KVL + ROPE + DH2, GC),
             (QL + KVL + ROPE + DH2 + GC, GC), (0, QL), (QL, KVL + ROPE)]
N_FF = 2 * (FF // GC) + KD
MIX0 = [0, PER_MIX + N_FF]
SPLIT0 = [0, MIX_SPLIT + N_FF]
FF0, FFS0 = PER_MIX, MIX_SPLIT
MOE0, MOES0 = MIX0[1] + PER_MIX, SPLIT0[1] + MIX_SPLIT
PER_EXPERT = 12
EXPERT_WIDTH = [4 * HALF_A] * 4 + [4 * HALF_B] * 4 + [3 * D] * 3 + [2 * D]
W0 = 2
XB, XH = (6, 5), (3, 3)

POWERS, SQUARES, _k, _q = {}, {}, 0, 0
for _l in range(DEPTH):
    for _name in ["n1", "lat", "qk"] + [("att", _t) for _t in tiles(_l)] + ["rnn", "n2"]:
        _k += 1
        POWERS[_l, _name] = _k
    for _name, _m in (("n1", KD // 2), ("lat", 2), ("rnn", 1), ("n2", KD // 2)):
        _q += _m
        SQUARES[_l, _name] = _q
MIXHI = [0, CH * (len(tiles(0)) + 1)]


def build(nc, ins, out):
    pl = plan_blocks()
    B = pl.blocks
    x, positions, meta = ins["x"], ins["positions"], ins["meta_tokens"]

    with ExitStack() as ctx:
        def sem(name):
            return ctx.enter_context(nc.semaphore(name))

        def sb(name, shape, dt=F32, to=ctx):
            return to.enter_context(nc.sbuf_tensor(name, shape, dt))

        ps = ctx.enter_context(nc.psum_tensor("ps", [P, 8, 512], F32))
        raw = sb("raw", [P, RAW, SLOT])
        whi = sb("whi", [P, SPL, SLOT], F32R)
        wlo = sb("wlo", [P, SPL, SLOT], F32R)
        con = sb("con", [P, C_ALL])
        vrow = sb("vrow", [P, P])
        vec = sb("vec", [P, P])
        hT = sb("hT", [P, KD, T])
        u32 = sb("u32", [P, KD, T])
        uhi = sb("uhi", [P, KD, T], F32R)
        ulo = sb("ulo", [P, KD, T], F32R)
        one = sb("one", [P, 1])
        mhalf = sb("mhalf", [P, 1])
        cosT = sb("cosT", [P, T])
        sinT = sb("sinT", [P, T])
        rt = sb("rt", [P, 56])
        gdiag = sb("gdiag", [P, 2, CH, P])
        hba = sb("hba", [P, DEPTH * CH])
        hbi = sb("hbi", [P, DEPTH * CH])
        sp2 = sb("sp2", [P, DEPTH * CH])
        spt = sb("spt", [P, 4, DEPTH * CH])
        small = sb("small", [P, 5, NH])
        scr = sb("scr", [P, 1])
        rw = sb("rw", [P, KD, NE])
        mixer = ExitStack()
        xr = sb("xr", [P, CH, T + CONV - 1], to=mixer)
        gt = sb("gt", [P, CH, T], to=mixer)
        xc = sb("xc", [P, CH, T], to=mixer)
        ta = sb("ta", [P, CH, T], to=mixer)
        tb = sb("tb", [P, CH, T], to=mixer)
        cq = sb("cq", [P, QC, T], to=mixer)
        ckv = sb("ckv", [P, KVC, T], to=mixer)
        kr = sb("kr", [P, 2, T], to=mixer)
        qT = sb("qT", [P, NH, T], to=mixer)
        kT = sb("kT", [P, NH, T], to=mixer)
        vt = sb("vt", [P, 3, DH2], to=mixer)
        pT = sb("pT", [P, 2, 3 * P], to=mixer)
        osb = sb("osb", [P, DH2], to=mixer)
        mixer.close()
        dense = ExitStack()
        ahi = sb("ahi", [P, FC, T], F32R, to=dense)
        alo = sb("alo", [P, FC, T], F32R, to=dense)
        aff = sb("aff", [P, 2, T], to=dense)
        tff = sb("tff", [P, 2, T], to=dense)
        dense.close()
        load = ExitStack()
        xin = sb("xin", [P, 3, D], to=load)
        posi = sb("posi", [P, SEQ], I32, to=load)
        rope = sb("rope", [P, 4, T], to=load)
        load.close()
        moe = ExitStack()
        acc = sb("acc", [P, 2, D], to=moe)
        sel = sb("sel", [P, 2, NE + 1], to=moe)
        gate = sb("gate", [P, 2, NE + 1], to=moe)
        pos = sb("pos", [P, 2, NE + 1], to=moe)
        lgt = sb("lgt", [P, 2, NE], to=moe)
        top = sb("top", [P, 2, 8], to=moe)
        topi = sb("topi", [P, 2, 8], U32, to=moe)
        topf = sb("topf", [P, 2, 8], to=moe)
        rtmp = sb("rtmp", [P, 6, NE], to=moe)
        flag = sb("flag", [P, 1], I32, to=moe)
        onehot = sb("onehot", [P, 2, P], F32R, to=moe)
        onehT = sb("onehT", [P, 2, P], F32R, to=moe)
        identr = sb("identr", [P, P], F32R, to=moe)
        xeh = sb("xeh", [P, KD, P], F32R, to=moe)
        xel = sb("xel", [P, KD, P], F32R, to=moe)
        sg = sb("sg", [P, HALF_A], to=moe)
        act1 = sb("act1", [P, HALF_A], to=moe)
        hact = sb("hact", [P, FE], to=moe)
        heh = sb("heh", [P, FEC, P], F32R, to=moe)
        hel = sb("hel", [P, FEC, P], F32R, to=moe)
        yhi = sb("yhi", [P, D], F32R, to=moe)
        ylo = sb("ylo", [P, D], F32R, to=moe)
        moe.close()

        landed = [sem(f"landed{n}") for n in range(RAW)]
        hi_done = sem("hi_done")
        lo_done = sem("lo_done")
        w_used = sem("w_used")
        filled = sem("filled")
        emptied = [sem(f"emptied{b}") for b in range(8)]
        x_in = sem("x_in")
        con_in = sem("con_in")
        vec_in = sem("vec_in")
        pos_in = sem("pos_in")
        rw_in = sem("rw_in")
        gdiag_in = sem("gdiag_in")
        out_done = sem("out_done")
        zeroed = sem("zeroed")
        vec_done = sem("vec_done")
        hba_done = sem("hba_done")
        h_done = sem("h_done")
        squares = sem("squares")
        var_done = sem("var_done")
        rstd_done = sem("rstd_done")
        u_done = sem("u_done")
        uhi_done = sem("uhi_done")
        ulo_done = sem("ulo_done")
        xc_done = sem("xc_done")
        th_done = sem("th_done")
        w2_done = sem("w2_done")
        root_done = sem("root_done")
        b_done = sem("b_done")
        gsq_done = sem("gsq_done")
        ginner = sem("ginner")
        gtanh = sem("gtanh")
        rnn_done = sem("rnn_done")
        lat_done = sem("lat_done")
        krg_done = sem("krg_done")
        qrot_done = sem("qrot_done")
        kfull = sem("kfull")
        qksq = sem("qksq")
        sc_done = sem("sc_done")
        exp_done = sem("exp_done")
        pt_done = sem("pt_done")
        pv_done = sem("pv_done")
        on_done = sem("on_done")
        mixhi = sem("mixhi")
        mixlo = sem("mixlo")
        rg_done = sem("rg_done")
        sgff = sem("sgff")
        aff_done = sem("aff_done")
        ahi_done = sem("ahi_done")
        alo_done = sem("alo_done")
        angle = sem("angle")
        sine = sem("sine")
        splus = sem("splus")
        splus_e = sem("splus_e")
        top_done = sem("top_done")
        topx = sem("topx")
        sel_done = sem("sel_done")
        flag_done = sem("flag_done")
        tok_hi = sem("tok_hi")
        tok_lo = sem("tok_lo")
        ready0 = sem("ready0")
        qsq_done = sem("qsq_done")
        hot_done = sem("hot_done")
        xr_full = [sem(f"x{b}_full") for b in range(2)]
        xr_hi = [sem(f"x{b}_hi") for b in range(2)]
        xr_free = [sem(f"x{b}_free") for b in range(2)]
        sg_done = sem("sg_done")
        hact_done = sem("hact_done")
        yhi_done = sem("yhi_done")
        ylo_done = sem("ylo_done")
        acc_done = sem("acc_done")
        d_link = sem("d_link")
        a_link = sem("a_link")

        block = ctx.enter_context(nc.Block())
        ident = con[:, C_ID:C_ID + P]

        def col(name, l, k=0, rows=slice(0, P)):
            first, per = ROWS[name]
            n = first + l * per + k
            return vec[rows, n:n + 1]

        def fill(eng, b, i=0):
            if b.before or b.per_before:
                if isinstance(b.emptied(i), int) and b.emptied(i) == 0:
                    return
                eng.wait_ge(emptied[b.bank], b.emptied(i))

        def bank(b, rows=slice(0, P), cols=slice(0, T)):
            return ps[rows, b.bank, cols]

        FFB = B["ff0", 0].order

        def chunk_used(s):
            for l in range(DEPTH):
                j = s - SPLIT0[l]
                if 0 <= j < 6:
                    return B[((l, "xr", 1), (l, "xr", 3), (l, "gt", 1), (l, "gt", 3), (l, "q", 2), (l, "kr", 0))[j]].ready()
                if 6 <= j < MIX_SPLIT:
                    return B[l, "wo", 2 * (j - 6) + 1].ready()
            c = s - FFS0
            if c < 22:
                return FFB + 4 * (c // 2) + 2 + 2 * (c % 2)
            return B["dn", 0].order + c - 21

        def matmul3(pe, dst, w, xs, start, stop, swap=False):
            (wh, wl), (xh, xl) = w, xs
            pe.matmul(dst, wh, xh, start=start, stop=False, skip_group_check=True)
            pe.matmul(dst, wh, xl, start=False, stop=False, skip_group_check=True)
            return pe.matmul(dst, wl, xh, start=False, stop=stop, skip_group_check=True)

        def w_in_src(l, n):
            c, k = W_IN_COLS[n]
            return ins["w_in"][l].rearrange("(k p) c -> p k c", p=P)[:, :, c:c + k], KD, k

        def slot_of(n, k, c):
            s = n % RAW
            return raw[:, s, 0:k * c].rearrange("p (k c) -> p k c", k=k)

        @block.sync
        def _(sp):
            def freed(n, need_lo=None, need_filled=None):
                if need_lo is not None:
                    sp.wait_ge(lo_done, need_lo)
                if need_filled is not None:
                    sp.wait_ge(filled, need_filled)

            def mix_split(l, j):
                return SPLIT0[l] + (j + 1 if j < 6 else j - 1)

            def mixer_loads(l):
                for j in range(PER_MIX):
                    n = MIX0[l] + j
                    old = j - RAW
                    if l and old < 0:
                        freed(n, need_lo=SPLIT0[l] + old + 1)
                    elif old >= 0:
                        if old in (6, 7):
                            freed(n, need_filled=B[(l, "uq", NH - 1) if old == 6 else (l, "v", 2)].ready())
                        else:
                            freed(n, need_lo=mix_split(l, old))
                    if j < 6:
                        src, k, c = w_in_src(l, j)
                    elif j == 6:
                        src, k, c = ins["w_uq"][l].rearrange("(k p) c -> p k c", p=P), QC, NH * QKH
                    elif j == 7:
                        src, k, c = ins["w_ukv"][l].rearrange("(k p) c -> p k c", p=P), KVC, NH * (NOPE + VH)
                    else:
                        m = (j - 8) * GC
                        src, k, c = ins["w_out"][l].rearrange("(k p) c -> p k c", p=P)[:, :, m:m + GC], KD, GC
                    sp.dma_start(slot_of(n, k, c), src).then_inc(landed[n % RAW], 16)
                    if j == 5:
                        if l:
                            sp.wait_ge(filled, B[0, "wi", CH - 1].ready())
                        else:
                            sp.wait_ge(zeroed, 1)
                        for kind, name in enumerate(("w_a", "w_i")):
                            for s in range(2):
                                r = slice(64 * s, 64 * s + 64)
                                sp.dma_start(gdiag[r, kind, :, r],
                                             ins[name][l].rearrange("(c s) a b -> s a c b", s=2)[s]).then_inc(gdiag_in, 16)

            gsrc = [ins[n][0].rearrange("(k p) c -> p k c", p=P) for n in ("ffn_w_gate", "ffn_w_up")]
            dsrc = ins["ffn_w_down"][0].rearrange("(k p) c -> p k c", p=P)

            mixer_loads(0)
            sp.dma_start(rw[:, :, :], ins["router_w"][0].rearrange("(k p) e -> p k e", p=P)).then_inc(rw_in, 16)
            for j in range(2):
                n = FF0 + j
                freed(n, need_lo=FFS0 - RAW + j + 1)
                sp.dma_start(slot_of(n, KD, GC), gsrc[j][:, :, 0:GC]).then_inc(landed[n % RAW], 16)
            with sp.Fori(0, 5) as i:
                for j in range(4):
                    n = FF0 + 2 + j
                    freed(n, need_lo=FFS0 + 2 + j - RAW + 1 + 4 * i)
                    sp.dma_start(slot_of(n, KD, GC), gsrc[j % 2][:, :, bass.ds((2 * i + j // 2 + 1) * GC, GC)])\
                      .then_inc(landed[n % RAW], 16)
            with sp.Fori(0, 2) as i:
                for j in range(4):
                    n = FF0 + 22 + j
                    freed(n, need_lo=FFS0 + 22 + j - RAW + 1 + 4 * i)
                    sp.dma_start(slot_of(n, FC, P), dsrc[:, :, bass.ds((4 * i + j) * P, P)])\
                      .then_inc(landed[n % RAW], 16)
            mixer_loads(1)

            eg = [ins[n][0].rearrange("e (k p) c -> e p k c", p=P) for n in ("moe_w_gate", "moe_w_up")]
            ed = ins["moe_w_down"][0].rearrange("e (k p) c -> e p k c", p=P)

            def expert_loads(done):
                with sp.Fori(0, NE) as e:
                    for j in range(PER_EXPERT):
                        n = MOE0 + j
                        freed(n, need_lo=MOES0 + j - RAW + 1 + PER_EXPERT * (e + done))
                        if j < 8:
                            hf, kind, kk = j // 4, j // 2 % 2, j % 2
                            c0, c = (0, HALF_A) if hf == 0 else (HALF_A, HALF_B)
                            src = eg[kind][bass.ds(e, 1), :, 4 * kk:4 * kk + 4, c0:c0 + c]
                            k = 4
                        else:
                            k0, k = ((0, 3), (3, 3), (6, 3), (9, 2))[j - 8]
                            c = D
                            src = ed[bass.ds(e, 1), :, k0:k0 + k, :]
                        sp.dma_start(slot_of(n, k, c), src.rearrange("o p k c -> p (o k) c")).then_inc(landed[n % RAW], 16)

            expert_loads(0)
            sp.wait_ge(flag_done, 1)
            more = sp.value_load(flag[0:1, 0:1], min_val=0, max_val=1)
            with sp.If(more > 0):
                expert_loads(NE)
            with sp.Else():
                sp.nop()
            sp.nop()
            sp.wait_ge(acc_done, 1)
            sp.dma_start(out[0].rearrange("(t p) d -> p t d", p=P), acc[:, :, :]).then_inc(out_done, 16)
            sp.wait_ge(out_done, 16)

        @block.gpsimd
        def _(pool):
            n = [0]

            def power(ap):
                n[0] += 1
                pool.wait_ge(var_done, n[0])
                pool.tensor_tensor(ap, ap, mhalf[0:ap.shape[0], :].to_broadcast(list(ap.shape)), ALU.pow)\
                    .then_inc(rstd_done, 1)

            for l in range(DEPTH):
                power(rt[:, 0:3])
                power(rt[:, 0:6])
                power(rt[:, 6:54])
                for t in tiles(l):
                    power(rt[0:TILES[t][1], 54:55])
                power(rt[:, 0:3])
                power(rt[:, 0:3])

        @block.scalar
        def _(act):
            chain = Chain(act, a_link)

            def settle():
                chain.link(act.activation(scr[:, :], scr[:, :], ACT.Copy))

            act.wait_ge(ready0, 1)

            act.dma_start(xin[0:NMETA, 0, :], meta).then_inc(x_in, 16)
            act.dma_start(xin[:, 1:3, :], x[0].rearrange("(t p) d -> p t d", p=P)).then_inc(x_in, 16)
            act.dma_start(con[:, :], ins["constants"]).then_inc(con_in, 16)
            act.wait_ge(zeroed, 1)
            rows = 0
            for name, (first, per) in ROWS.items():
                w = P if per > 1 else QKH
                src = ins[name]
                if name == "conv_w":
                    src = src.rearrange("l j (c p) -> (l j c) p", p=P)
                elif per > 1:
                    src = src.rearrange("l (c p) -> (l c) p", p=P)
                act.dma_start(vrow[first:first + DEPTH * per, 0:w], src).then_inc(vec_in, 16)
                rows += 1
            act.dma_start(posi[NOPE:QKH, :], positions.to_broadcast([ROPE, SEQ])).then_inc(pos_in, 16)

            def split(s, width, land, i=0, per=0):
                act.wait_ge(landed[land % RAW], 16 * (land // RAW + 1) + 16 * (per // RAW) * i)
                if per == PER_EXPERT:
                    act.wait_ge(w_used, s - MOES0 + 1 + per * i)
                elif s >= SPL:
                    act.wait_ge(filled, chunk_used(s - SPL) + 2 * per * i)
                act.activation(whi[:, s % SPL, 0:width], raw[:, land % RAW, 0:width], ACT.Copy).then_inc(hi_done, 1)

            def mix_chunk(l, j):
                if j < 6:
                    split(SPLIT0[l] + j, KD * W_IN_COLS[j][1], MIX0[l] + j)
                else:
                    split(SPLIT0[l] + j - 2, KD * GC, MIX0[l] + j)

            def take(b, dst, func=ACT.Copy, rows=slice(0, P), cols=slice(0, T), done=None, i=0, **kw):
                act.wait_ge(filled, b.ready(i))
                act.activation(dst, bank(b, rows, cols), func, **kw).then_inc(emptied[b.bank], 1)

            def square(l, c0, base):
                for c in range(0, KD, 2):
                    act.activation(u32[:, c:c + 2, c0:T], hT[:, c:c + 2, c0:T], ACT.Square).then_inc(squares, 1)

            def round_u(n0, c0):
                for c in range(KD):
                    act.wait_ge(u_done, n0 + c + 1)
                    act.activation(uhi[:, c, c0:T], u32[:, c, c0:T], ACT.Copy).then_inc(uhi_done, 1)

            for c in range(1, KD, 2):
                take(B["x", c], hT[:, c, :])
            act.wait_ge(angle, 1)
            act.activation(sinT[NOPE:QKH, :], rope[NOPE:QKH, 2, :], ACT.Sin).then_inc(sine, 1)
            act.wait_ge(angle, 2)
            act.activation(cosT[NOPE:QKH, :], rope[NOPE:QKH, 3, :], ACT.Sin).then_inc(sine, 1)
            act.wait_ge(splus, 1)
            act.activation(spt[:, 1, :], spt[:, 0, :], ACT.Exp, scale=-1.0).then_inc(splus_e, 1)

            for l in range(DEPTH):
                c0 = first_token(l)
                mix_chunk(l, 0)
                mix_chunk(l, 1)
                act.wait_ge(h_done, 1 + 3 * l)
                if l == 0:
                    settle()
                square(l, 0, 0)
                round_u(2 * KD * l, 0)
                for c in range(4):
                    take(B[l, "xr", c], xr[:, c, CONV - 1:])
                    if c % 2:
                        mix_chunk(l, 2 + c // 2)
                for c in range(4):
                    take(B[l, "gt", c], gt[:, c, :])
                    if c % 2:
                        mix_chunk(l, 4 + c // 2)
                for c in range(QC):
                    take(B[l, "q", c], cq[:, c, :])
                for c in range(KVC):
                    take(B[l, "kv", c], ckv[:, c, :])
                r = slice(NOPE, QKH)
                take(B[l, "kr", 0], kr[r, 0, :], rows=r)
                settle()
                act.wait_ge(ulo_done, 2 * KD * l + KD)
                act.activation(u32[:, 0:QC, :], cq[:, :, :], ACT.Square).then_inc(squares, 1)
                act.activation(u32[:, QC:QC + KVC, :], ckv[:, :, :], ACT.Square).then_inc(squares, 1)
                act.wait_ge(hba_done, 1)
                for c in range(CH):
                    b = B[l, "wa", c]
                    n = l * CH + c
                    act.wait_ge(filled, b.ready())
                    act.activation(ta[:, c, :], bank(b), ACT.Tanh, bias=hba[:, n:n + 1], scale=0.5)\
                       .then_inc(emptied[b.bank], 1)
                settle()
                act.wait_ge(vec_done, 2)
                for c in range(CH):
                    n = l * CH + c
                    act.activation(ta[:, c, :], ta[:, c, :], ACT.Tanh, bias=sp2[:, n:n + 1], scale=sp2[:, n:n + 1])\
                       .then_inc(th_done, 1)
                for c in range(CH):
                    b = B[l, "wi", c]
                    n = l * CH + c
                    act.wait_ge(filled, b.ready())
                    act.activation(tb[:, c, :], bank(b), ACT.Tanh, bias=hbi[:, n:n + 1], scale=0.5)\
                       .then_inc(emptied[b.bank], 1)
                r = slice(0, QKH)
                for h in range(NH):
                    b = B[l, "uq", h]
                    act.wait_ge(filled, b.ready())
                    act.activation(qT[r, h, :], bank(b, r), ACT.Copy, scale=col("q_head_g", l, 0, r))
                    act.activation(u32[r, h, :], bank(b, r), ACT.Square).then_inc(emptied[b.bank], 1)
                act.activation(scr[:, :], scr[:, :], ACT.Copy).then_inc(qsq_done, 1)
                for h in range(NH):
                    b = B[l, "kn", h]
                    r = slice(0, NOPE)
                    act.wait_ge(filled, b.ready())
                    act.activation(kT[r, h, :], bank(b, r), ACT.Copy).then_inc(emptied[b.bank], 1)
                for t in range(3):
                    n = TILES[t][1]
                    take(B[l, "v", t], vt[0:n, t, :], rows=slice(0, n), cols=slice(0, DH2))
                act.wait_ge(kfull, l + 1)
                act.wait_ge(filled, B[l, "qss"].ready())
                act.activation(u32[0:QKH, :, :], kT[0:QKH, :, :], ACT.Square).then_inc(qksq, 1)
                act.wait_ge(w2_done, l + 1)
                act.activation(ta[:, :, :], ta[:, :, :], ACT.Sqrt, scale=-1.0).then_inc(root_done, 1)
                act.wait_ge(b_done, l + 1)
                act.activation(ta[:, :, :], gt[:, :, :], ACT.Square).then_inc(gsq_done, 1)
                act.wait_ge(ginner, l + 1)
                act.activation(ta[:, :, :], ta[:, :, :], ACT.Tanh, scale=0.7978845608028654).then_inc(gtanh, 1)
                act.wait_ge(rnn_done, l + 1)
                act.activation(ta[:, :, :], xc[:, :, :], ACT.Square).then_inc(squares, 1)
                mix_chunk(l, 8)
                mix_chunk(l, 9)
                for t in tiles(l):
                    k0 = tiles(l).index(t)
                    lead, n = TILES[t]
                    keys = lead + n
                    act.wait_ge(sc_done, len(tiles(0)) * l + k0 + 1)
                    for h in range(NH):
                        act.activation(u32[0:n, h, 0:keys], u32[0:n, h, 0:keys], ACT.Exp, bias=small[0:n, 1, h:h + 1],
                                       accum_out=small[0:n, 2, h:h + 1]).then_inc(exp_done, 1)
                    b = B[l, "ot", t]
                    act.wait_ge(filled, b.ready())
                    for c in range(CH):
                        act.activation(uhi[:, c, lead:lead + n], ps[:, b.bank, c * P:c * P + n], ACT.Copy,
                                       scale=col("attn_out_g", l, c)).then_inc(mixhi, 1)
                for c in range(CH):
                    act.wait_ge(rg_done, CH * l + c + 1)
                    act.activation(uhi[:, CH + c, c0:T], tb[:, c, c0:T], ACT.Copy).then_inc(mixhi, 1)
                mix_chunk(l, 10)
                mix_chunk(l, 11)
                act.wait_ge(h_done, 2 + 3 * l)
                square(l, c0, 0)
                if l == 0:
                    split(FFS0, KD * GC, FF0)
                    split(FFS0 + 1, KD * GC, FF0 + 1)
                    round_u(KD, c0)

                    with act.Fori(0, 5) as i:
                        for g in range(2):
                            j = 2 + 2 * g
                            split(FFS0 + j, KD * GC, FF0 + j, i, 4)
                            gb = [4, 5] if g else [0, 1]
                            act.wait_ge(filled, FFB + 2 + 4 * g + 8 * i)
                            for q in range(2):
                                act.activation(tff[:, q, :], ps[:, gb[q], 0:T], ACT.Tanh, scale=0.5).then_inc(sgff, 1)
                            split(FFS0 + j + 1, KD * GC, FF0 + j + 1, i, 4)
                            act.wait_ge(aff_done, 2 * i + g + 1)
                            act.activation(ahi[:, bass.ds(4 * i + 2 * g, 2), :], aff[:, :, :], ACT.Copy).then_inc(ahi_done, 1)
                    split(FFS0 + 22, FC * P, FF0 + 22)
                    act.wait_ge(filled, FFB + 42)
                    for q in range(2):
                        act.activation(tff[:, q, :], ps[:, q, 0:T], ACT.Tanh, scale=0.5).then_inc(sgff, 1)
                    act.wait_ge(aff_done, 11)
                    act.activation(ahi[:, 20:22, :], aff[:, :, :], ACT.Copy).then_inc(ahi_done, 1)
                    for j in range(1, KD):
                        split(FFS0 + 22 + j, FC * P, FF0 + 22 + j)

            act.wait_ge(top_done, 1)
            act.activation(rtmp[:, 1, 0:2], rtmp[:, 0, 0:2], ACT.Exp).then_inc(topx, 1)
            for t in range(2):
                for hf in range(2):
                    b = B["ut", t, hf]
                    act.wait_ge(filled, b.ready())
                    act.activation(uhi[:, :, :].rearrange("p k t -> p (k t)")[:, t * D + hf * 512:t * D + hf * 512 + 512],
                                   ps[:, b.bank, :], ACT.Copy).then_inc(tok_hi, 1)
            for t in range(2):
                for hf in range(2):
                    take(B["ht", t, hf], acc[:, t, hf * 512:hf * 512 + 512], cols=slice(0, 512))

            def experts(p):
                e0 = NE * p
                base = [(XB[b] * NE + 3) * p for b in range(2)]
                for q in range(2):
                    act.wait_ge(xr_full[1 - q], base[1 - q] + 1)
                    act.activation(xeh[:, 4 * q:4 * q + 4, :], ps[:, 7 - q, :].rearrange("p (k n) -> p k n", k=4), ACT.Copy).then_inc(xr_hi[1 - q], 1)
                base = [b + 1 for b in base]
                with act.Fori(0, NE) as e:
                    def w(j):
                        split(MOES0 + j + PER_EXPERT * e0, EXPERT_WIDTH[j], MOE0 + j + PER_EXPERT * e0, e, PER_EXPERT)

                    def full(bk, k):
                        act.wait_ge(xr_full[bk], base[bk] + k + XB[bk] * e)

                    w(0)
                    w(1)
                    act.wait_ge(w_used, W0 + PER_EXPERT * (e + e0))
                    act.activation(yhi[:, :], ps[:, 4:6, :].rearrange("p b n -> p (b n)"), ACT.Copy).then_inc(yhi_done, 1)
                    w(2)
                    w(3)

                    def sigmoid(hf, width):
                        act.wait_ge(w_used, W0 + PER_EXPERT * (e + e0) + 4 * hf + 2)
                        act.activation(sg[:, 0:2 * width].rearrange("p (b n) -> p b n", b=2), ps[:, 0:2, 0:width],
                                       ACT.Tanh, scale=0.5).then_inc(sg_done, 1)

                    sigmoid(0, HALF_A // 2)
                    w(4)
                    w(5)
                    w(6)
                    sigmoid(1, HALF_B // 2)
                    w(7)
                    w(8)
                    full(1, 3)
                    act.activation(xeh[:, 0:4, :], ps[:, 7, :].rearrange("p (k n) -> p k n", k=4), ACT.Copy).then_inc(xr_hi[1], 1)
                    full(0, 4)
                    act.activation(xeh[:, 4:8, :], ps[:, 6, :].rearrange("p (k n) -> p k n", k=4), ACT.Copy).then_inc(xr_hi[0], 1)
                    full(1, 4)
                    act.activation(heh[:, 0:4, :], ps[:, 7, :].rearrange("p (k n) -> p k n", k=4), ACT.Copy).then_inc(xr_hi[1], 1)
                    full(0, 5)
                    act.activation(heh[:, 4:6, :], ps[:, 6, 0:2 * P].rearrange("p (k n) -> p k n", k=2), ACT.Copy).then_inc(xr_hi[0], 1)
                    w(9)
                    full(1, 5)
                    act.activation(heh[:, 6:10, :], ps[:, 7, :].rearrange("p (k n) -> p k n", k=4), ACT.Copy).then_inc(xr_hi[1], 1)
                    full(0, 6)
                    act.activation(heh[:, 10:11, :], ps[:, 6, 0:P].rearrange("p (k n) -> p k n", k=1), ACT.Copy).then_inc(xr_hi[0], 1)
                    w(10)
                    w(11)
                act.wait_ge(w_used, W0 + PER_EXPERT * (NE + e0))
                act.activation(yhi[:, :], ps[:, 4:6, :].rearrange("p b n -> p (b n)"), ACT.Copy).then_inc(yhi_done, 1)

            experts(0)
            act.wait_ge(flag_done, 1)
            more = act.value_load(flag[0:1, 0:1], min_val=0, max_val=1)
            with act.If(more > 0):
                experts(1)
            with act.Else():
                act.nop()
            act.nop()

        @block.vector
        def _(dve):
            ch = Chain(dve, d_link)
            link = ch.link

            dve.memset(vrow[:, :], 0.0)
            dve.memset(gdiag[:, :, :, :], 0.0).then_inc(zeroed, 1)
            dve.memset(rt[:, :], 1.0)
            dve.memset(one[:, :], 1.0)
            dve.memset(spt[:, :, :], 0.0)
            dve.memset(scr[:, :], 0.0)
            dve.memset(small[:, :, :], 0.0)
            dve.memset(mhalf[:, :], -0.5).then_inc(ready0, 1)
            dve.wait_ge(ready0, 1)

            def lo(s, width, land, i=0, per=0):
                dve.wait_ge(hi_done, s + 1 + per * i)
                dve.tensor_tensor(wlo[:, s % SPL, 0:width], raw[:, land % RAW, 0:width],
                                  whi[:, s % SPL, 0:width].bitcast(F32), ALU.subtract).then_inc(lo_done, 1)

            def mix_chunk(l, j):
                if j < 6:
                    lo(SPLIT0[l] + j, KD * W_IN_COLS[j][1], MIX0[l] + j)
                else:
                    lo(SPLIT0[l] + j - 2, KD * GC, MIX0[l] + j)

            def sumsq(b, at, tl, width, k0=0, close=True, bank_cols=0):
                dve.wait_ge(filled, b.ready())
                for t in tl:
                    n = TILES[t][1]
                    q = dve.tensor_scalar(rt[0:n, at + t:at + t + 1], ps[0:n, b.bank, at + t:at + t + 1],
                                          1.0 / width, EPS, ALU.mult, ALU.add)
                return q

            def normed(l, name, c0, n0, g):
                tl = (0, 1, 2) if c0 == 0 else (1, 2)
                b = B[l, name + "ss"]
                sumsq(b, 0, tl, D).then_inc(var_done, 1)
                dve.engine_nop().then_inc(emptied[b.bank], 1)
                b = B[l, name + "bc"]
                dve.wait_ge(filled, b.ready())
                for c in range(KD):
                    q = dve.scalar_tensor_tensor(u32[:, c, c0:T], hT[:, c, c0:T], col(g, l, c), bank(b, cols=slice(c0, T)),
                                                 ALU.mult, ALU.mult)
                    q.then_inc(u_done, 1)
                dve.engine_nop().then_inc(emptied[b.bank], 1)

            def lows(n0, c0):
                for c in range(KD):
                    dve.wait_ge(uhi_done, n0 + c + 1)
                    dve.tensor_tensor(ulo[:, c, c0:T], u32[:, c, c0:T], uhi[:, c, c0:T].bitcast(F32), ALU.subtract)\
                       .then_inc(ulo_done, 1)

            for c in range(0, KD, 2):
                b = B["x", c]
                dve.wait_ge(filled, b.ready())
                q = dve.tensor_copy(hT[:, c, :], bank(b))
                q.then_inc(emptied[b.bank], 1)
            b = B["vec"]
            dve.wait_ge(filled, b.ready())
            dve.tensor_copy(vec[:, :], ps[:, b.bank, 0:P]).then_inc(emptied[b.bank], 1)
            dve.wait_ge(emptied[0], 3)
            dve.wait_ge(emptied[1], 2)
            dve.wait_ge(emptied[3], 2)
            dve.engine_nop().then_inc(h_done, 1)
            dve.engine_nop().then_inc(vec_done, 1)
            n = DEPTH * CH
            fa, fi, fl_ = ROWS["b_a"][0], ROWS["b_i"][0], ROWS["lru_lambda"][0]
            dve.tensor_scalar(hba[:, :], vec[:, fa:fa + n], 0.5, None, ALU.mult)
            dve.tensor_scalar(hbi[:, :], vec[:, fi:fi + n], 0.5, None, ALU.mult).then_inc(hba_done, 1)
            link(dve.tensor_scalar(spt[:, 0, :], vec[:, fl_:fl_ + n], -1.0, None, ALU.mult))
            dve.tensor_tensor(spt[:, 0, :], spt[:, 0, :], vec[:, fl_:fl_ + n], ALU.max).then_inc(splus, 1)
            r = slice(NOPE, QKH)
            dve.wait_ge(con_in, 16)
            dve.wait_ge(pos_in, 16)
            dve.tensor_copy(rope[r, 0, 0:NMETA], con[r, C_IOTA:C_IOTA + NMETA])
            link(dve.tensor_copy(rope[r, 0, NMETA:T], posi[r, :]))
            link(dve.tensor_scalar(rope[r, 0, NMETA:T], rope[r, 0, NMETA:T], float(NMETA), None, ALU.add))
            link(dve.tensor_scalar(rope[r, 0, :], rope[r, 0, :], con[r, C_FREQ:C_FREQ + 1], None, ALU.mult))
            magic = 12582912.0
            link(dve.tensor_scalar(rope[r, 1, :], rope[r, 0, :], 0.15915494309189535, magic, ALU.mult, ALU.add))
            link(dve.tensor_scalar(rope[r, 1, :], rope[r, 1, :], magic, None, ALU.subtract))
            for part in (6.28125, 0.0019350051879882812, 3.019916050561733e-07):
                link(dve.scalar_tensor_tensor(rope[r, 0, :], rope[r, 1, :], -part, rope[r, 0, :], ALU.mult, ALU.add))
            pi = 3.1415925
            dve.tensor_scalar(rope[r, 2, :], rope[r, 0, :], pi, -pi, ALU.min, ALU.max).then_inc(angle, 1)
            dve.wait_ge(angle, 1)
            link(dve.tensor_scalar(rope[r, 3, :], rope[r, 2, :], -1.0, None, ALU.mult))
            link(dve.tensor_tensor(rope[r, 3, :], rope[r, 3, :], rope[r, 2, :], ALU.max))
            dve.tensor_scalar(rope[r, 3, :], rope[r, 3, :], -1.0, 1.5707963267948966, ALU.mult, ALU.add).then_inc(angle, 1)
            e, z, z2, w = spt[:, 1, :], spt[:, 2, :], spt[:, 3, :], spt[:, 0, :]
            dve.wait_ge(splus_e, 1)
            link(dve.tensor_scalar(z, e, 2.0, None, ALU.add))
            link(dve.reciprocal(z, z))
            link(dve.tensor_tensor(z, z, e, ALU.mult))
            link(dve.tensor_tensor(z2, z, z, ALU.mult))
            link(dve.tensor_scalar(w, z2, 1.0 / 17, 1.0 / 15, ALU.mult, ALU.add))
            for k in (13, 11, 9, 7, 5, 3, 1):
                link(dve.tensor_tensor(w, w, z2, ALU.mult))
                link(dve.tensor_scalar(w, w, 1.0 / k, None, ALU.add))
            link(dve.tensor_tensor(w, w, z, ALU.mult))
            link(dve.tensor_scalar(e, vec[:, fl_:fl_ + n], -1.0, 0.0, ALU.mult, ALU.max))
            link(dve.scalar_tensor_tensor(e, w, 2.0, e, ALU.mult, ALU.add))
            dve.tensor_scalar(sp2[:, :], e, 2.0, None, ALU.mult).then_inc(vec_done, 1)
            dve.wait_ge(sine, 2)

            for l in range(DEPTH):
                c0 = first_token(l)
                mix_chunk(l, 0)
                mix_chunk(l, 1)
                dve.wait_ge(h_done, 1 + 3 * l)
                normed(l, "n1", 0, 2 * KD * l, "norm_mix_g")
                lows(2 * KD * l, 0)
                dve.memset(xr[:, :, 0:CONV - 1], 0.0)
                for j in range(2, 6):
                    mix_chunk(l, j)
                for c in range(CH):
                    b = B[l, "xr", c]
                    dve.wait_ge(emptied[b.bank], b.before + 1)
                    cw = [vec[:, ROWS["conv_w"][0] + (l * CONV + j) * CH + c:][:, 0:1] for j in range(CONV)]
                    link(dve.tensor_scalar(xc[:, c, :], xr[:, c, 0:T], cw[0], col("conv_b", l, c), ALU.mult, ALU.add))
                    for j in range(1, CONV):
                        q = dve.scalar_tensor_tensor(xc[:, c, :], xr[:, c, j:j + T], cw[j], xc[:, c, :], ALU.mult, ALU.add)
                        if j < CONV - 1:
                            link(q)
                    q.then_inc(xc_done, 1)
                b = B[l, "cqss"]
                dve.wait_ge(filled, b.ready())
                for t in range(3):
                    k = TILES[t][1]
                    dve.tensor_scalar(rt[0:k, t:t + 1], ps[0:k, b.bank, t:t + 1], 1.0 / QL, EPS, ALU.mult, ALU.add)
                    q = dve.tensor_scalar(rt[0:k, 3 + t:4 + t], ps[0:k, b.bank, 3 + t:4 + t], 1.0 / KVL, EPS, ALU.mult, ALU.add)
                q.then_inc(var_done, 1)
                dve.engine_nop().then_inc(emptied[b.bank], 1)
                b = B[l, "cqbc"]
                dve.wait_ge(filled, b.ready())
                for c in range(QC):
                    q = dve.scalar_tensor_tensor(cq[:, c, :], cq[:, c, :], col("q_norm_g", l, c), bank(b), ALU.mult, ALU.mult)
                    q.then_inc(lat_done, 1)
                dve.engine_nop().then_inc(emptied[b.bank], 1)
                b = B[l, "kvbc"]
                dve.wait_ge(filled, b.ready())
                for c in range(KVC):
                    q = dve.scalar_tensor_tensor(ckv[:, c, :], ckv[:, c, :], col("kv_norm_g", l, c), bank(b), ALU.mult, ALU.mult)
                    q.then_inc(lat_done, 1)
                dve.engine_nop().then_inc(emptied[b.bank], 1)
                r = slice(NOPE, QKH)
                bb = B[l, "kr", 0]
                dve.wait_ge(emptied[bb.bank], bb.before + 1)
                for h in range(NH):
                    q = dve.tensor_copy(kT[r, h, :], kr[r, 0, :])
                link(q)
                dve.tensor_scalar(kr[r, 0, :], kr[r, 0, :], col("k_head_g", l, 0, r), None, ALU.mult).then_inc(krg_done, 1)
                for h in range(NH):
                    b = B[l, "kn", h]
                    dve.wait_ge(emptied[b.bank], b.before + 1)
                dve.engine_nop().then_inc(kfull, 1)
                dve.wait_ge(krg_done, l + 1)
                link(dve.tensor_tensor(kr[r, 1, :], kr[r, 0, :], cosT[r, :], ALU.mult))
                b = B[l, "krr"]
                dve.wait_ge(filled, b.ready())
                q = dve.tensor_tensor(kr[r, 0, :], bank(b, r), sinT[r, :], ALU.mult)
                q.then_inc(emptied[b.bank], 1)
                dve.wait_ge(emptied[b.bank], b.before + 1)
                link(dve.tensor_tensor(kr[r, 1, :], kr[r, 0, :], kr[r, 1, :], ALU.add))
                tmp = xr[:, :, 0:T]
                dve.wait_ge(th_done, CH * (l + 1))
                link(dve.tensor_scalar(tmp, ta[:, :, :], 1.0, None, ALU.add))
                link(dve.reciprocal(tmp, tmp))
                link(dve.tensor_tensor(ta[:, :, :], ta[:, :, :], tmp, ALU.mult))
                link(dve.tensor_scalar(tmp, ta[:, :, :], -2.0, 1.0, ALU.mult, ALU.add))
                dve.scalar_tensor_tensor(ta[:, :, :], ta[:, :, :], 1.0, ta[:, :, :], ALU.subtract, ALU.mult).then_inc(w2_done, 1)
                for c in range(CH):
                    b = B[l, "wi", c]
                    dve.wait_ge(emptied[b.bank], b.before + 1)
                link(dve.scalar_tensor_tensor(tb[:, :, :], tb[:, :, :], 1.0, xc[:, :, :], ALU.add, ALU.mult))
                for h in range(NH):
                    b = B[l, "uq", h]
                    dve.wait_ge(emptied[b.bank], b.before + 1)
                r = slice(NOPE, QKH)
                dve.wait_ge(qksq, l + 1)
                for h in range(NH):
                    dve.tensor_copy(kT[r, h, :], kr[r, 1, :])
                link(dve.tensor_scalar(kT[0:NOPE, :, :], kT[0:NOPE, :, :], col("k_head_g", l, 0, slice(0, NOPE)), None, ALU.mult))
                for name, off, mul, add in (("qss", 0, 1.0, EPS * QKH), ("kss", NH, 1.0 / QKH, EPS)):
                    b = B[l, name]
                    dve.wait_ge(filled, b.ready())
                    for t in range(3):
                        k = TILES[t][1]
                        at = 6 + 16 * t + off
                        q = dve.tensor_scalar(rt[0:k, at:at + NH], ps[0:k, b.bank, 16 * t:16 * t + NH], mul, add,
                                              ALU.mult, ALU.add)
                    if off:
                        q.then_inc(var_done, 1)
                        dve.engine_nop().then_inc(emptied[b.bank], 1)
                    else:
                        q.then_inc(emptied[b.bank], 1)
                for h in range(NH):
                    b = B[l, "qr", h]
                    dve.wait_ge(filled, b.ready())
                    dve.tensor_tensor(u32[r, h, :], bank(b, r), sinT[r, :], ALU.mult).then_inc(emptied[b.bank], 1)
                    q = dve.tensor_tensor(qT[r, h, :], qT[r, h, :], cosT[r, :], ALU.mult)
                link(q)
                dve.tensor_tensor(qT[r, :, :], qT[r, :, :], u32[r, :, :], ALU.add).then_inc(qrot_done, 1)
                r = slice(0, QKH)
                for h in range(NH):
                    b = B[l, "kbc", h]
                    dve.wait_ge(filled, b.ready())
                    dve.tensor_tensor(kT[r, h, :], kT[r, h, :], bank(b, r), ALU.mult).then_inc(emptied[b.bank], 1)
                dve.wait_ge(root_done, l + 1)
                dve.tensor_tensor(tb[:, :, :], tb[:, :, :], ta[:, :, :], ALU.mult).then_inc(b_done, 1)
                dve.wait_ge(b_done, l + 1)
                for c in range(CH):
                    q = dve.tensor_tensor_scan(xc[:, c, :], tmp[:, c, :], tb[:, c, :], 0.0, ALU.mult, ALU.add)
                dve.wait_ge(gsq_done, l + 1)
                link(dve.tensor_scalar(ta[:, :, :], ta[:, :, :], 0.044715, 1.0, ALU.mult, ALU.add))
                dve.tensor_tensor(ta[:, :, :], ta[:, :, :], gt[:, :, :], ALU.mult).then_inc(ginner, 1)
                dve.wait_ge(gtanh, l + 1)
                link(dve.scalar_tensor_tensor(ta[:, :, :], ta[:, :, :], 1.0, gt[:, :, :], ALU.add, ALU.mult))
                dve.scalar_tensor_tensor(xc[:, :, :], ta[:, :, :], 0.5, xc[:, :, :], ALU.mult, ALU.mult).then_inc(rnn_done, 1)
                mix_chunk(l, 8)
                mix_chunk(l, 9)
                dve.wait_ge(rstd_done, POWERS[l, "qk"])
                for t in tiles(l):
                    k0 = tiles(l).index(t)
                    lead, n = TILES[t]
                    keys = lead + n
                    m0 = C_MASK + T - P - lead
                    at = 6 + 16 * t
                    for h in range(NH):
                        b = B[l, "s", t, h]
                        dve.wait_ge(filled, b.ready())
                        q = dve.tensor_tensor_reduce(out=u32[0:n, h, 0:keys], in0=ps[0:n, b.bank, 0:keys],
                                                     in1=con[0:n, m0:m0 + keys], scale=rt[0:n, at + h:at + h + 1],
                                                     scalar=-3e38, op0=ALU.add, op1=ALU.max,
                                                     accum_out=small[0:n, 0, h:h + 1])
                        q.then_inc(emptied[b.bank], 1)
                    dve.wait_ge(emptied[b.bank], b.before + 1)
                    dve.tensor_scalar(small[0:n, 1, :], small[0:n, 0, :], -1.0, None, ALU.mult).then_inc(sc_done, 1)
                    for h in range(NH):
                        b = B[l, "p", t, h]
                        dve.wait_ge(filled, b.ready())
                        if h >= 2:
                            dve.wait_ge(pv_done, (NH - 1) * (len(tiles(0)) * l + k0) + h - 1)
                        q = dve.tensor_copy(pT[0:NMETA, h % 2, 0:n], ps[0:NMETA, b.bank, 0:n])
                        if t:
                            q = dve.tensor_copy(pT[:, h % 2, P:(t + 1) * P], ps[:, b.bank, P:(t + 1) * P])
                        q.then_inc(emptied[b.bank], 1)
                    link(dve.reciprocal(small[0:n, 3, :], small[0:n, 2, :]))
                    b = B[l, "o", t]
                    dve.wait_ge(filled, b.ready())
                    q = dve.tensor_tensor(osb[0:n, :].rearrange("p (h d) -> p h d", h=NH),
                                          ps[0:n, b.bank, :].rearrange("p (h d) -> p h d", h=NH),
                                          small[0:n, 3, :].rearrange("p (h o) -> p h o", o=1).to_broadcast([n, NH, VH]), ALU.mult)
                    q.then_inc(emptied[b.bank], 1)
                    dve.wait_ge(emptied[b.bank], b.before + 1)
                    link(dve.tensor_tensor_reduce(out=u32[0:n, 0:2, 0:256], in0=osb[0:n, :].rearrange("p (a b) -> p a b", a=2),
                                                  in1=osb[0:n, :].rearrange("p (a b) -> p a b", a=2), scale=1.0, scalar=0.0,
                                                  op0=ALU.mult, op1=ALU.add, accum_out=small[0:n, 4, 1:2]))
                    dve.tensor_scalar(rt[0:n, 54:55], small[0:n, 4, 1:2], 1.0 / DH2, EPS, ALU.mult, ALU.add).then_inc(var_done, 1)
                    dve.wait_ge(rstd_done, POWERS[l, ("att", t)])
                    dve.tensor_scalar(osb[0:n, :], osb[0:n, :], rt[0:n, 54:55], None, ALU.mult).then_inc(on_done, 1)
                    b = B[l, "ot", t]
                    dve.wait_ge(filled, b.ready())
                    mh = MIXHI[l] + CH * k0
                    dve.wait_ge(mixhi, mh + CH)
                    for c in range(CH):
                        q = dve.scalar_tensor_tensor(ulo[:, c, lead:lead + n], ps[:, b.bank, c * P:c * P + n],
                                                     col("attn_out_g", l, c), uhi[:, c, lead:lead + n].bitcast(F32),
                                                     ALU.mult, ALU.subtract)
                    q.then_inc(emptied[b.bank], 1)
                b = B[l, "rnss"]
                sumsq(b, 0, tiles(l), DH2).then_inc(var_done, 1)
                dve.engine_nop().then_inc(emptied[b.bank], 1)
                b = B[l, "rnbc"]
                dve.wait_ge(filled, b.ready())
                for c in range(CH):
                    dve.scalar_tensor_tensor(tb[:, c, c0:T], xc[:, c, c0:T], col("rnn_out_g", l, c),
                                             bank(b, cols=slice(c0, T)), ALU.mult, ALU.mult).then_inc(rg_done, 1)
                dve.engine_nop().then_inc(emptied[b.bank], 1)
                mh = MIXHI[l] + CH * len(tiles(l))
                for c in range(CH):
                    dve.wait_ge(mixhi, mh + c + 1)
                    q = dve.tensor_tensor(ulo[:, CH + c, c0:T], tb[:, c, c0:T], uhi[:, CH + c, c0:T].bitcast(F32), ALU.subtract)
                q.then_inc(mixlo, 1)
                for j in range(2):
                    mix_chunk(l, 10 + j)
                    for m in range(2 * j, 2 * j + 2):
                        b = B[l, "wo", m]
                        dve.wait_ge(filled, b.ready())
                        dve.tensor_tensor(hT[:, m, c0:T], hT[:, m, c0:T], bank(b, cols=slice(c0, T)), ALU.add)\
                           .then_inc(emptied[b.bank], 1)
                for m in range(4, KD):
                    b = B[l, "wo", m]
                    dve.wait_ge(filled, b.ready())
                    dve.tensor_tensor(hT[:, m, c0:T], hT[:, m, c0:T], bank(b, cols=slice(c0, T)), ALU.add)\
                       .then_inc(emptied[b.bank], 1)
                for m in range(4, KD):
                    b = B[l, "wo", m]
                    dve.wait_ge(emptied[b.bank], b.before + 1)
                dve.engine_nop().then_inc(h_done, 1)
                if l == 0:
                    lo(FFS0, KD * GC, FF0)
                    lo(FFS0 + 1, KD * GC, FF0 + 1)
                dve.wait_ge(h_done, 2 + 3 * l)
                normed(l, "n2", c0, KD + 2 * KD * l, "norm_ffn_g")
                if l == 0:
                    lows(KD, c0)

                    def group(banks, k, rd, mid, m):
                        for q in range(2):
                            dve.wait_ge(sgff, 2 * k + q + 1)
                            if q == 0:
                                dve.wait_ge(alo_done, k + 1)
                            dve.scalar_tensor_tensor(aff[:, q, :], tff[:, q, :], 1.0, ps[:, banks[q], 0:T], ALU.add, ALU.mult)\
                               .then_inc(emptied[banks[q]], 1)
                        dve.wait_ge(filled, rd)
                        dve.wait_ge(emptied[banks[1]], mid)
                        for q in range(2):
                            x2 = dve.scalar_tensor_tensor(aff[:, q, :], aff[:, q, :], 0.5, ps[:, banks[2 + q], 0:T], ALU.mult, ALU.mult)
                            x2.then_inc(emptied[banks[2 + q]], 1)
                        dve.engine_nop().then_inc(aff_done, 1)
                        dve.wait_ge(ahi_done, k + 1)
                        dve.tensor_tensor(alo[:, bass.ds(m, 2), :], aff[:, :, :], ahi[:, bass.ds(m, 2), :].bitcast(F32),
                                          ALU.subtract).then_inc(alo_done, 1)

                    dve.engine_nop().then_inc(alo_done, 1)
                    with dve.Fori(0, 5) as i:
                        lo(FFS0 + 2, KD * GC, FF0 + 2, i, 4)
                        lo(FFS0 + 3, KD * GC, FF0 + 3, i, 4)
                        group([0, 1, 2, 3], 2 * i, FFB + 4 + 8 * i, B["ff0", 1].before + 1 + i, 4 * i)
                        lo(FFS0 + 4, KD * GC, FF0 + 4, i, 4)
                        lo(FFS0 + 5, KD * GC, FF0 + 5, i, 4)
                        group([4, 5, 6, 7], 2 * i + 1, FFB + 8 + 8 * i, B["ff", 1].before + 1 + i, 4 * i + 2)
                    lo(FFS0 + 22, FC * P, FF0 + 22)
                    group([0, 1, 2, 3], 10, FFB + 44, B["ff0", 1].before + 6, 20)
                    for m in range(KD):
                        if m < KD - 1:
                            lo(FFS0 + 23 + m, FC * P, FF0 + 23 + m)
                        i, q = divmod(m, 4)
                        b = B["dn", q]
                        dve.wait_ge(filled, b.ready(i))
                        dve.tensor_tensor(hT[:, m, :], hT[:, m, :], bank(b), ALU.add).then_inc(emptied[b.bank], 1)
                    dve.engine_nop().then_inc(h_done, 2)

            b = B["lg"]
            dve.wait_ge(filled, b.ready())
            dve.memset(sel[:, :, :], 0.0)
            dve.memset(gate[:, :, :], 0.0)
            dve.memset(pos[:, :, :], 0.0)
            dve.tensor_copy(identr[:, :], ident)
            link(dve.tensor_copy(lgt[:, :, :], ps[:, b.bank, 0:2 * NE].rearrange("p (t e) -> p t e", t=2)))
            dve.engine_nop().then_inc(emptied[b.bank], 1)
            for t in range(2):
                q = dve.max(top[:, t, :], lgt[:, t, :])
            link(q)
            for t in range(2):
                q = dve.max_index(topi[:, t, :], top[:, t, :], lgt[:, t, :])
            link(q)
            link(dve.tensor_copy(topf[:, :, :], topi[:, :, :]))
            for t in range(2):
                q = dve.tensor_tensor(rtmp[:, 0, t:t + 1], top[:, t, 1:2], top[:, t, 0:1], ALU.subtract)
            q.then_inc(top_done, 1)
            dve.wait_ge(topx, 1)
            link(dve.tensor_scalar(rtmp[:, 2, 0:2], rtmp[:, 1, 0:2], 1.0, None, ALU.add))
            link(dve.reciprocal(rtmp[:, 2, 0:2], rtmp[:, 2, 0:2]))
            link(dve.tensor_tensor(rtmp[:, 3, 0:2], rtmp[:, 2, 0:2], rtmp[:, 1, 0:2], ALU.mult))
            e8 = con[:, C_E8:C_E8 + NE]
            for t in range(2):
                dve.tensor_scalar(rtmp[:, 4, :], e8, topf[:, t, 0:1], None, ALU.is_equal)
                link(dve.tensor_scalar(rtmp[:, 5, :], e8, topf[:, t, 1:2], None, ALU.is_equal))
                dve.tensor_tensor(sel[:, t, 0:NE], rtmp[:, 4, :], rtmp[:, 5, :], ALU.add)
                link(dve.tensor_scalar(rtmp[:, 4, :], rtmp[:, 4, :], rtmp[:, 2, t:t + 1], None, ALU.mult))
                link(dve.scalar_tensor_tensor(gate[:, t, 1:NE + 1], rtmp[:, 5, :], rtmp[:, 3, t:t + 1], rtmp[:, 4, :],
                                              ALU.mult, ALU.add))
            dve.engine_nop().then_inc(sel_done, 1)
            b = B["cum"]
            dve.wait_ge(filled, b.ready())
            for t in range(2):
                dve.tensor_copy(pos[:, t, 0:NE], ps[:, b.bank, t * NE:t * NE + NE])
            link(dve.tensor_reduce(rtmp[:, 0, 0:1], ps[:, b.bank, 2 * NE:3 * NE], AX.X, ALU.max))
            dve.engine_nop().then_inc(emptied[b.bank], 1)
            dve.tensor_scalar(flag[:, :], rtmp[:, 0, 0:1], float(P), None, ALU.is_gt).then_inc(flag_done, 1)
            for t in range(2):
                for hf in range(2):
                    b = B["ut", t, hf]
                    n = 2 * t + hf
                    dve.wait_ge(tok_hi, n + 1)
                    v = slice(t * D + hf * 512, t * D + hf * 512 + 512)
                    dve.tensor_tensor(ulo[:, :, :].rearrange("p k t -> p (k t)")[:, v], ps[:, b.bank, :],
                                      uhi[:, :, :].rearrange("p k t -> p (k t)")[:, v].bitcast(F32), ALU.subtract)\
                       .then_inc(emptied[b.bank], 1)
            dve.engine_nop().then_inc(tok_lo, 1)
            dve.memset(onehT[:, :, :].bitcast(F32), 0.0)
            dve.memset(ylo[:, :].bitcast(F32), 0.0)
            for t in range(2):
                for hf in range(2):
                    b = B["ht", t, hf]
                    dve.wait_ge(emptied[b.bank], b.before + 1)
            dve.memset(yhi[:, :].bitcast(F32), 0.0)
            dve.engine_nop().then_inc(hact_done, 1)

            def hot(e, p):
                for t in range(2):
                    q = dve.tensor_scalar(onehot[:, t, :], con[:, C_IOTA + P * p:C_IOTA + P * p + P],
                                          pos[:, t, bass.ds(e, 1)], sel[:, t, bass.ds(e, 1)], ALU.is_equal, ALU.mult)
                q.then_inc(hot_done, 1)

            def experts(p):
                e0 = NE * p
                hot(0, p)
                base = [(XB[b] * NE + 3) * p for b in range(2)]
                hbase = [(XH[b] * NE + 1) * p for b in range(2)]
                for q in range(2):
                    bk = 1 - q
                    dve.wait_ge(xr_hi[bk], hbase[bk] + 1)
                    dve.tensor_tensor(xel[:, 4 * q:4 * q + 4, :], ps[:, 7 - q, :].rearrange("p (k n) -> p k n", k=4),
                                      xeh[:, 4 * q:4 * q + 4, :].bitcast(F32), ALU.subtract).then_inc(xr_free[bk], 1)
                base = [b + 1 for b in base]
                hbase = [b + 1 for b in hbase]

                def add_expert(e, n_full, gcol):
                    for t in range(2):
                        for hf in range(2):
                            bk = hf
                            dve.wait_ge(xr_full[bk], n_full[bk] + t + 1)
                            v = slice(hf * 512, hf * 512 + 512)
                            dve.scalar_tensor_tensor(acc[:, t, v], ps[:, 6 + bk, :], gate[:, t, bass.ds(gcol, 1)],
                                                     acc[:, t, v], ALU.mult, ALU.add).then_inc(xr_free[bk], 1)

                with ch.loop(NE, 2) as e:
                    def w(j):
                        lo(MOES0 + j + PER_EXPERT * e0, EXPERT_WIDTH[j], MOE0 + j + PER_EXPERT * e0, e, PER_EXPERT)

                    def low(bk, k, dst, hi, src):
                        dve.wait_ge(xr_hi[bk], hbase[bk] + k + XH[bk] * e)
                        dve.tensor_tensor(dst, src, hi.bitcast(F32), ALU.subtract).then_inc(xr_free[bk], 1)

                    def silu(hf, width):
                        half = slice(HALF_A * hf, HALF_A * hf + 2 * width)
                        dve.wait_ge(sg_done, 2 * (e + e0) + hf + 1)
                        two = "p (b n) -> p b n"
                        link(dve.scalar_tensor_tensor(act1[:, 0:2 * width].rearrange(two, b=2),
                                                      sg[:, 0:2 * width].rearrange(two, b=2), 1.0, ps[:, 0:2, 0:width],
                                                      ALU.add, ALU.mult))
                        return half

                    def times_up(hf, width, half):
                        dve.wait_ge(w_used, W0 + PER_EXPERT * (e + e0) + 4 * hf + 4)
                        q = (dve.scalar_tensor_tensor(hact[:, half].rearrange("p (b n) -> p b n", b=2),
                                                      act1[:, 0:2 * width].rearrange("p (b n) -> p b n", b=2), 0.5,
                                                      ps[:, 2:4, 0:width], ALU.mult, ALU.mult))
                        q.then_inc(hact_done, 1)

                    w(0)
                    w(1)
                    dve.wait_ge(yhi_done, (NE + 1) * p + e + 1)
                    dve.tensor_tensor(ylo[:, :], ps[:, 4:6, :].rearrange("p b n -> p (b n)"), yhi[:, :].bitcast(F32),
                                      ALU.subtract).then_inc(ylo_done, 1)
                    w(2)
                    w(3)
                    half = silu(0, HALF_A // 2)
                    w(4)
                    times_up(0, HALF_A // 2, half)
                    add_expert(e, [base[0] + XB[0] * e, base[1] + XB[1] * e], e)
                    dve.wait_ge(xr_full[0], base[0] + 3 + XB[0] * e)
                    dve.tensor_copy(onehT[:, :, :], ps[:, 6, 0:2 * P].rearrange("p (t n) -> p t n", t=2)).then_inc(xr_free[0], 1)
                    w(5)
                    hot(e + 1, p)
                    w(6)
                    w(7)
                    half = silu(1, HALF_B // 2)
                    w(8)
                    times_up(1, HALF_B // 2, half)
                    low(1, 1, xel[:, 0:4, :], xeh[:, 0:4, :], ps[:, 7, :].rearrange("p (k n) -> p k n", k=4))
                    low(0, 1, xel[:, 4:8, :], xeh[:, 4:8, :], ps[:, 6, :].rearrange("p (k n) -> p k n", k=4))
                    low(1, 2, hel[:, 0:4, :], heh[:, 0:4, :], ps[:, 7, :].rearrange("p (k n) -> p k n", k=4))
                    low(0, 2, hel[:, 4:6, :], heh[:, 4:6, :], ps[:, 6, 0:2 * P].rearrange("p (k n) -> p k n", k=2))
                    w(9)
                    low(1, 3, hel[:, 6:10, :], heh[:, 6:10, :], ps[:, 7, :].rearrange("p (k n) -> p k n", k=4))
                    low(0, 3, hel[:, 10:11, :], heh[:, 10:11, :], ps[:, 6, 0:P].rearrange("p (k n) -> p k n", k=1))
                    w(10)
                    w(11)
                dve.wait_ge(yhi_done, (NE + 1) * (p + 1))
                dve.tensor_tensor(ylo[:, :], ps[:, 4:6, :].rearrange("p b n -> p (b n)"), yhi[:, :].bitcast(F32),
                                  ALU.subtract).then_inc(ylo_done, 1)
                add_expert(NE, [base[0] + XB[0] * NE, base[1] + XB[1] * NE], NE)

            experts(0)
            more = dve.value_load(flag[0:1, 0:1], min_val=0, max_val=1)
            with dve.If(more > 0):
                experts(1)
            with dve.Else():
                dve.nop()
            dve.nop()
            dve.engine_nop().then_inc(acc_done, 1)

        @block.tensor
        def _(pe):
            pe.wait_ge(ready0, 1)
            pe.wait_ge(con_in, 16)
            pe.wait_ge(x_in, 32)
            for c in range(KD):
                b = B["x", c]
                fill(pe, b)
                for t, (lead, n) in enumerate(TILES):
                    q = pe.transpose(ps[:, b.bank, lead:lead + n], xin[0:n, t, c * P:(c + 1) * P], ident[0:n, 0:n])
                q.then_inc(filled, 1)
            pe.wait_ge(vec_in, 16 * len(ROWS))
            b = B["vec"]
            fill(pe, b)
            pe.transpose(ps[:, b.bank, 0:P], vrow[:, :], ident).then_inc(filled, 1)

            def ones(rows, n):
                return one[rows, :].to_broadcast([rows.stop - rows.start, n])

            def sums(b, at, chunks, src, tl, first=True):
                tl = [t for t in tl if t] + [t for t in tl if not t]
                for t in tl:
                    lead, n = TILES[t]
                    for k, c in enumerate(chunks):
                        q = pe.matmul(ps[0:n, b.bank, at + t:at + t + 1], src[:, c, lead:lead + n], one[:, :],
                                      start=(k == 0), stop=(k == len(chunks) - 1))
                return q

            def spread(b, at, tl, width=P):
                for t in tl:
                    lead, n = TILES[t]
                    q = pe.matmul(ps[0:width, b.bank, lead:lead + n], rt[0:n, at(t):at(t) + 1].to_broadcast([n, width]),
                                  ident[0:n, 0:n], start=True, stop=True)
                return q

            def norm(l, name, tl, nsq):
                b = B[l, name + "ss"]
                fill(pe, b)
                pe.wait_ge(squares, nsq)
                sums(b, 0, range(KD), u32, tl).then_inc(filled, 1)
                b = B[l, name + "bc"]
                fill(pe, b)
                pe.wait_ge(rstd_done, POWERS[l, name])
                spread(b, lambda t: t, tl).then_inc(filled, 1)

            def chunk_ready(s, i=0, per=0):
                pe.wait_ge(lo_done, s + 1 + per * i)

            def dense_block(b, s, k, cols, m, n, c0=0, last=None, i=0, out_rows=slice(0, P), xs=None, k0=0, start=True, stop=True,
                            wait_x=None):
                xh, xl = xs
                for kk in range(k):
                    if wait_x is not None:
                        pe.wait_ge(wait_x[0], wait_x[1] + kk + 1)
                    at = kk * cols + m
                    w = (whi[:, s % SPL, at:at + n], wlo[:, s % SPL, at:at + n])
                    q = matmul3(pe, ps[out_rows, b.bank, 0:T - c0] if c0 is None else ps[out_rows, b.bank, c0:T], w,
                                (xh[:, k0 + kk, c0:T], xl[:, k0 + kk, c0:T]), start and kk == 0, stop and kk == k - 1)
                return q

            for l in range(DEPTH):
                c0 = first_token(l)
                norm(l, "n1", (0, 1, 2), SQUARES[l, "n1"])
                names = [("xr", 0), ("xr", 2), ("gt", 0), ("gt", 2), ("q", 0), ("kv", 0)]
                for j, (name, m0) in enumerate(names):
                    s = SPLIT0[l] + j
                    cols = W_IN_COLS[j][1]
                    chunk_ready(s)
                    for m in range(cols // P):
                        b = B[l, name, m0 + m]
                        fill(pe, b)
                        q = dense_block(b, s, KD, cols, m * P, P, xs=(uhi, ulo),
                                        wait_x=(ulo_done, 2 * KD * l) if j == 0 and m == 0 else None)
                        q.then_inc(filled, 1)
                    if j == 5:
                        b = B[l, "kr", 0]
                        fill(pe, b)
                        for kk in range(KD):
                            at = kk * cols + KVL + ROPE - QKH
                            w = (whi[:, s % SPL, at:at + QKH], wlo[:, s % SPL, at:at + QKH])
                            q = matmul3(pe, bank(b, slice(0, QKH)), w, (uhi[:, kk, :], ulo[:, kk, :]), kk == 0, kk == KD - 1)
                        q.then_inc(filled, 1)
                b = B[l, "cqss"]
                fill(pe, b)
                pe.wait_ge(squares, SQUARES[l, "lat"])
                sums(b, 0, range(QC), u32, (0, 1, 2))
                sums(b, 3, range(QC, QC + KVC), u32, (0, 1, 2)).then_inc(filled, 1)
                pe.wait_ge(rstd_done, POWERS[l, "lat"])
                for name, at in (("cqbc", 0), ("kvbc", 3)):
                    b = B[l, name]
                    fill(pe, b)
                    spread(b, lambda t: at + t, (0, 1, 2)).then_inc(filled, 1)
                pe.wait_ge(gdiag_in, 64 * (l + 1))
                for kind, name in enumerate(("wa", "wi")):
                    for c in range(CH):
                        b = B[l, name, c]
                        fill(pe, b)
                        pe.wait_ge(xc_done, CH * l + c + 1)
                        pe.matmul(bank(b), gdiag[:, kind, c, :], xc[:, c, :], start=True, stop=True).then_inc(filled, 1)
                n = MIX0[l] + 6
                wq = raw[:, n % RAW, 0:QC * NH * QKH].rearrange("p (k c) -> p k c", k=QC)
                pe.wait_ge(landed[n % RAW], 16 * (n // RAW + 1))
                pe.wait_ge(lat_done, 5 * l + 3)
                for h in range(NH):
                    b = B[l, "uq", h]
                    fill(pe, b)
                    for k in range(QC):
                        q = pe.matmul(bank(b, slice(0, QKH)), wq[:, k, h * QKH:(h + 1) * QKH], cq[:, k, :],
                                      start=(k == 0), stop=(k == QC - 1))
                    q.then_inc(filled, 1)
                n += 1
                wkv = raw[:, n % RAW, 0:KVC * NH * (NOPE + VH)].rearrange("p (k c) -> p k c", k=KVC)
                pe.wait_ge(landed[n % RAW], 16 * (n // RAW + 1))
                pe.wait_ge(lat_done, 5 * l + 5)
                for h in range(NH):
                    b = B[l, "kn", h]
                    fill(pe, b)
                    for k in range(KVC):
                        at = h * (NOPE + VH)
                        q = pe.matmul(bank(b, slice(0, NOPE)), wkv[:, k, at:at + NOPE], ckv[:, k, :],
                                      start=(k == 0), stop=(k == KVC - 1))
                    q.then_inc(filled, 1)
                for t, (lead, m) in enumerate(TILES):
                    b = B[l, "v", t]
                    fill(pe, b)
                    for k in range(KVC):
                        wv = wkv[:, k, :].rearrange("p (h d) -> p h d", h=NH)[:, :, NOPE:]
                        q = pe.matmul(ps[0:m, b.bank, :].rearrange("p (h d) -> p h d", h=NH), ckv[:, k, lead:lead + m], wv,
                                      start=(k == 0), stop=(k == KVC - 1))
                    q.then_inc(filled, 1)
                r = slice(NOPE, QKH)
                rot = con[r, C_ROT:C_ROT + ROPE]
                b = B[l, "krr"]
                fill(pe, b)
                pe.wait_ge(krg_done, l + 1)
                pe.matmul(bank(b, r), rot, kr[r, 0, :], start=True, stop=True).then_inc(filled, 1)
                for name, done in (("qss", qsq_done), ("kss", qksq)):
                    b = B[l, name]
                    fill(pe, b)
                    pe.wait_ge(done, l + 1)
                    for t in (1, 2, 0):
                        lead, n = TILES[t]
                        for h in range(NH):
                            q = pe.matmul(ps[0:n, b.bank, 16 * t + h:16 * t + h + 1], u32[0:QKH, h, lead:lead + n],
                                          one[0:QKH, :], start=True, stop=True)
                    q.then_inc(filled, 1)
                for h in range(NH):
                    u = B[l, "uq", h]
                    pe.wait_ge(emptied[u.bank], u.before + 1)
                    b = B[l, "qr", h]
                    fill(pe, b)
                    pe.matmul(bank(b, r), rot, qT[r, h, :], start=True, stop=True).then_inc(filled, 1)
                pe.wait_ge(rstd_done, POWERS[l, "qk"])
                for h in range(NH):
                    b = B[l, "kbc", h]
                    fill(pe, b)
                    spread(b, lambda t: 6 + 16 * t + NH + h, (0, 1, 2), QKH).then_inc(filled, 1)
                pe.wait_ge(qrot_done, l + 1)
                for k0, t in enumerate(tiles(l)):
                    lead, n = TILES[t]
                    keys = lead + n
                    turn = len(tiles(0)) * l + k0
                    for h in range(NH):
                        b = B[l, "s", t, h]
                        fill(pe, b)
                        kb = B[l, "kbc", h]
                        pe.wait_ge(emptied[kb.bank], kb.before + 1)
                        pe.matmul(ps[0:n, b.bank, 0:keys], qT[0:QKH, h, lead:lead + n], kT[0:QKH, h, 0:keys],
                                  start=True, stop=True).then_inc(filled, 1)
                    fill(pe, B[l, "o", t])
                    for h in range(NH + 1):
                        if h < NH:
                            b = B[l, "p", t, h]
                            fill(pe, b)
                            pe.wait_ge(exp_done, NH * turn + h + 1)
                            for j in range(t + 1):
                                kl, kn = TILES[j]
                                q = pe.transpose(ps[0:kn, b.bank, j * P:j * P + n], u32[0:n, h, kl:kl + kn], ident[0:n, 0:n])
                            q.then_inc(filled, 1)
                        if h:
                            g = h - 1
                            b = B[l, "p", t, g]
                            pe.wait_ge(emptied[b.bank], b.before + 1)
                            for j in range(t + 1):
                                kn = TILES[j][1]
                                q = pe.matmul(ps[0:n, B[l, "o", t].bank, g * VH:(g + 1) * VH], pT[0:kn, g % 2, j * P:j * P + n],
                                              vt[0:kn, j, g * VH:(g + 1) * VH], start=(j == 0), stop=(j == t))
                            q.then_inc(pv_done if g < NH - 1 else filled, 1)
                    b = B[l, "ot", t]
                    fill(pe, b)
                    pe.wait_ge(on_done, turn + 1)
                    for c in range(CH):
                        q = pe.transpose(ps[:, b.bank, c * P:c * P + n], osb[0:n, c * P:(c + 1) * P], ident[0:n, 0:n])
                    q.then_inc(filled, 1)
                b = B[l, "rnss"]
                fill(pe, b)
                pe.wait_ge(squares, SQUARES[l, "rnn"])
                sums(b, 0, range(CH), ta, tiles(l)).then_inc(filled, 1)
                b = B[l, "rnbc"]
                fill(pe, b)
                pe.wait_ge(rstd_done, POWERS[l, "rnn"])
                spread(b, lambda t: t, tiles(l)).then_inc(filled, 1)
                pe.wait_ge(mixlo, l + 1)
                for j in range(4):
                    s = SPLIT0[l] + 6 + j
                    chunk_ready(s)
                    for m in range(2):
                        b = B[l, "wo", 2 * j + m]
                        fill(pe, b)
                        dense_block(b, s, KD, GC, m * P, P, c0=c0, xs=(uhi, ulo)).then_inc(filled, 1)
                if l == 1:
                    pe.matmul(ps[0:1, B[l, "n2ss"].bank, 511:512], one[:, :], one[:, :], start=True, stop=True)\
                      .then_inc(w_used, W0)
                norm(l, "n2", tiles(l), SQUARES[l, "n2"])
                if l == 0:
                    def group(banks, s, per, i, emp):
                        for part in range(2):
                            chunk_ready(s + part, i, per)
                            for m in range(2):
                                bk = banks[2 * part + m]
                                pe.wait_ge(emptied[bk], emp[2 * part + m])
                                for kk in range(KD):
                                    if part == 0 and m == 0 and not per:
                                        pe.wait_ge(ulo_done, KD + kk + 1)
                                    sl = (s + part) % SPL
                                    at = kk * GC + m * P
                                    q = matmul3(pe, ps[:, bk, 0:T], (whi[:, sl, at:at + P], wlo[:, sl, at:at + P]),
                                                (uhi[:, kk, :], ulo[:, kk, :]), kk == 0, kk == KD - 1)
                                q.then_inc(filled, 1)

                    group([0, 1, 2, 3], FFS0, 0, 0, [B["ff0", q].before for q in range(4)])
                    with pe.Fori(0, 5) as i:
                        group([4, 5, 6, 7], FFS0 + 2, 4, i, [B["ff", q].emptied(i) for q in range(4)])
                        group([0, 1, 2, 3], FFS0 + 4, 4, i, [B["ff", q].emptied(i) for q in range(4, 8)])
                    pe.wait_ge(alo_done, 12)
                    for m in range(KD):
                        i, q = divmod(m, 4)
                        b = B["dn", q]
                        s = FFS0 + 22 + m
                        chunk_ready(s)
                        pe.wait_ge(emptied[b.bank], b.emptied(i))
                        dense_block(b, s, FC, P, 0, P, xs=(ahi, alo)).then_inc(filled, 1)

            b = B["lg"]
            fill(pe, b)
            pe.wait_ge(rw_in, 16)
            pe.wait_ge(u_done, 4 * KD)
            for t in range(2):
                lead, n = TILES[t + 1]
                for k in range(KD):
                    q = pe.matmul(ps[:, b.bank, t * NE:(t + 1) * NE], u32[:, k, lead:lead + n], rw[:, k, :],
                                  start=(k == 0), stop=(k == KD - 1))
            q.then_inc(filled, 1)
            b = B["cum"]
            fill(pe, b)
            pe.wait_ge(sel_done, 1)
            before = con[:, C_LT:C_LT + P]
            every = one[:, :].to_broadcast([P, P])
            pe.matmul(ps[:, b.bank, 0:NE], before, sel[:, 0, 0:NE], start=True, stop=True)
            pe.matmul(ps[:, b.bank, NE:2 * NE], every, sel[:, 0, 0:NE], start=True, stop=False)
            pe.matmul(ps[:, b.bank, NE:2 * NE], before, sel[:, 1, 0:NE], start=False, stop=True)
            pe.matmul(ps[:, b.bank, 2 * NE:3 * NE], every, sel[:, 0, 0:NE], start=True, stop=False)
            pe.matmul(ps[:, b.bank, 2 * NE:3 * NE], every, sel[:, 1, 0:NE], start=False, stop=True).then_inc(filled, 1)
            for name, src in (("ut", u32), ("ht", hT)):
                for t in range(2):
                    lead, n = TILES[t + 1]
                    for hf in range(2):
                        b = B[name, t, hf]
                        fill(pe, b)
                        for c in range(4):
                            q = pe.transpose(ps[:, b.bank, c * P:(c + 1) * P], src[:, 4 * hf + c, lead:lead + n], ident)
                        q.then_inc(filled, 1)

            tokh = uhi[:, :, :].rearrange("p k t -> p (k t)")
            tokl = ulo[:, :, :].rearrange("p k t -> p (k t)")
            pe.wait_ge(tok_lo, 1)
            for hf in range(2):
                b = B["ht", 1, hf]
                pe.wait_ge(emptied[b.bank], b.before + 1)
            for b in (4, 5, 6, 7):
                pe.wait_ge(emptied[b], pl.before[b])

            def experts(p):
                e0 = NE * p
                base = [(XB[b] * NE + 3) * p for b in range(2)]

                def room(bk, k):
                    if isinstance(k, int) and k == 0:
                        return
                    pe.wait_ge(xr_free[bk], k)

                def gather(n_hot, before7, before6):
                    pe.wait_ge(hot_done, n_hot)
                    for q, (bk, k) in enumerate(((1, before7), (0, before6))):
                        room(bk, k)
                        for c in range(4):
                            at = (4 * q + c) * P
                            for t in range(2):
                                pe.matmul(ps[:, 6 + bk, c * P:(c + 1) * P], tokh[:, t * D + at:t * D + at + P],
                                          onehot[:, t, :], start=(t == 0), stop=False)
                                m = pe.matmul(ps[:, 6 + bk, c * P:(c + 1) * P], tokl[:, t * D + at:t * D + at + P],
                                              onehot[:, t, :], start=False, stop=(t == 1))
                        m.then_inc(xr_full[bk], 1)

                def combine(n_y, before6, before7):
                    pe.wait_ge(ylo_done, n_y)
                    for t in range(2):
                        for hf in range(2):
                            room(hf, (before6, before7)[hf] + t)
                            v = slice(hf * 512, hf * 512 + 512)
                            pe.matmul(ps[:, 6 + hf, :], onehT[:, t, :], yhi[:, v], start=True, stop=False)
                            pe.matmul(ps[:, 6 + hf, :], onehT[:, t, :], ylo[:, v], start=False, stop=True)\
                              .then_inc(xr_full[hf], 1)

                gather((NE + 1) * p + 1, base[1], base[0])
                base = [b + 1 for b in base]
                with pe.Fori(0, NE) as e:
                    n0 = [base[b] + XB[b] * e for b in range(2)]

                    def weights(j):
                        pe.wait_ge(lo_done, MOES0 + j + 1 + PER_EXPERT * (e + e0))
                        return (MOES0 + j) % SPL

                    def hidden(hf, part, width):
                        for c in range(2):
                            sl = weights(4 * hf + 2 * part + c)
                            if part == 0 and c == 0:
                                pe.wait_ge(hact_done, 2 * (e + e0) + hf + 1)
                                if hf == 0:
                                    for bk in range(2):
                                        pe.wait_ge(xr_free[bk], n0[bk])
                            for k in range(4):
                                kk = 4 * c + k
                                for xs, ws in ((xeh, (whi, wlo)), (xel, (whi,))):
                                    for w in ws:
                                        for n in range(2):
                                            at = k * 2 * width + n * width
                                            q = pe.matmul(ps[:, 2 * part + n, 0:width], xs[:, kk, :], w[:, sl, at:at + width],
                                                          start=(kk == 0 and xs is xeh and w is whi),
                                                          stop=(kk == KD - 1 and xs is xel), skip_group_check=True)
                            q.then_inc(w_used, 1)

                    def turn(hf, k0, kn, bks):
                        k = 0
                        for bk, cnt, blk in bks:
                            room(bk, n0[bk] + blk - 1)
                            for j in range(cnt):
                                at = (k0 + k) * P
                                q = pe.transpose(ps[:, 6 + bk, j * P:(j + 1) * P], hact[:, at:at + P], ident)
                                k += 1
                            q.then_inc(xr_full[bk], 1)

                    def down(j, k0, kn):
                        sl = weights(j)
                        for k in range(kn):
                            kk = k0 + k
                            for xs, ws in ((heh, (whi, wlo)), (hel, (whi,))):
                                for w in ws:
                                    for n in range(2):
                                        at = k * D + n * 512
                                        q = pe.matmul(ps[:, 4 + n, :], xs[:, kk, :], w[:, sl, at:at + 512],
                                                      start=(kk == 0 and xs is heh and w is whi),
                                                      stop=(kk == FEC - 1 and xs is hel), skip_group_check=True)
                        q.then_inc(w_used, 1)

                    hidden(0, 0, HALF_A // 2)
                    hidden(0, 1, HALF_A // 2)
                    combine((NE + 1) * p + e + 1, n0[0], n0[1])
                    room(0, n0[0] + 2)
                    for t in range(2):
                        q = pe.matmul(ps[:, 6, t * P:(t + 1) * P], onehot[:, t, :], identr[:, :], start=True, stop=True)
                    q.then_inc(xr_full[0], 1)
                    hidden(1, 0, HALF_B // 2)
                    hidden(1, 1, HALF_B // 2)
                    gather((NE + 1) * p + e + 2, n0[1] + 2, n0[0] + 3)
                    pe.wait_ge(hact_done, 2 * (e + e0) + 2)
                    turn(0, 0, 6, ((1, 4, 4), (0, 2, 5)))
                    pe.wait_ge(xr_free[1], n0[1] + 4)
                    pe.wait_ge(xr_free[0], n0[0] + 5)
                    down(8, 0, 3)
                    down(9, 3, 3)
                    pe.wait_ge(hact_done, 2 * (e + e0) + 3)
                    turn(1, 6, 5, ((1, 4, 5), (0, 1, 6)))
                    pe.wait_ge(xr_free[1], n0[1] + 5)
                    pe.wait_ge(xr_free[0], n0[0] + 6)
                    down(10, 6, 3)
                    down(11, 9, 2)
                combine((NE + 1) * (p + 1), base[0] + XB[0] * NE, base[1] + XB[1] * NE)

            experts(0)
            pe.wait_ge(flag_done, 1)
            more = pe.value_load(flag[0:1, 0:1], min_val=0, max_val=1)
            with pe.If(more > 0):
                experts(1)
            with pe.Else():
                pe.nop()
            pe.nop()


_INS = ["x", "positions", "meta_tokens", "norm_mix_g", "w_in", "q_norm_g", "w_uq", "kv_norm_g", "w_ukv", "q_head_g",
        "k_head_g", "conv_w", "conv_b", "w_a", "b_a", "w_i", "b_i", "lru_lambda", "attn_out_g", "rnn_out_g", "w_out",
        "norm_ffn_g", "ffn_w_gate", "ffn_w_up", "ffn_w_down", "router_w", "moe_w_gate", "moe_w_up", "moe_w_down"]


def kernel(**inputs):
    import concourse.bacc as _bacc
    from concourse.bass_utils import run_bass_kernel_spmd as _run

    nc = _bacc.Bacc("TRN2", target_bir_lowering=False, num_devices=1)
    arrays, aps = {}, {}
    given = {name: np.ascontiguousarray(inputs[name]) for name in _INS}
    given["constants"] = constants()
    for name, a in given.items():
        arrays[f"in_{name}_dram"] = a
        aps[name] = nc.dram_tensor(f"in_{name}_dram", a.shape, mybir.dt.from_np(a.dtype), kind="ExternalInput").ap()
    out = nc.dram_tensor("out_0_dram", (1, SEQ, D), F32, kind="ExternalOutput").ap()
    build(nc, aps, out)
    r = _run(nc, [arrays], core_ids=[0])
    return r.results[0]["out_0_dram"]
```

```python
import concourse.bass as bass
from concourse import mybir
from concourse.alu_op_type import AluOpType as ALU
from contextlib import ExitStack, contextmanager
import numpy as np

F32 = mybir.dt.float32
F32R = mybir.dt.float32r
I32 = mybir.dt.int32
U32 = mybir.dt.uint32
ACT = mybir.ActivationFunctionType
AX = mybir.AxisListType

P = 128
D = 1024
KD = D // P
SEQ, NMETA = 256, 16
T = SEQ + NMETA
DEPTH = 2
DH2 = D // 2
CH = DH2 // P
NH, NOPE, ROPE = 8, 64, 32
QKH = NOPE + ROPE
VH = DH2 // NH
QL, KVL = 384, 256
QC, KVC = QL // P, KVL // P
D_IN = QL + KVL + ROPE + 2 * DH2
CONV = 4
FF = 2816
FC = FF // P
NE, FE = 8, 1408
FEC = FE // P
EPS = 1e-6
TILES = [(0, NMETA), (NMETA, P), (NMETA + P, P)]

RAW = 4
SLOT = 3072
SPL = 4
PIECE = 1536
GC = 256
HALF_A = 6 * P
HALF_B = FE - HALF_A

C_ID, C_LT = 0, P
C_MASK = 2 * P
C_IOTA = C_MASK + T
C_E8 = C_IOTA + 2 * P
C_ROT = C_E8 + NE
C_FREQ = C_ROT + ROPE
C_ALL = C_FREQ + 1


def constants():
    c = np.zeros((P, C_ALL), np.float32)
    c[:, C_ID:C_ID + P] = np.eye(P)
    c[:, C_LT:C_LT + P] = np.triu(np.ones((P, P)), 1)
    c[:, C_MASK + T - P:C_MASK + T] = np.triu(np.full((P, P), -1e30), 1)
    c[:, C_IOTA:C_IOTA + 2 * P] = np.arange(2 * P)
    c[:, C_E8:C_E8 + NE] = np.arange(NE)
    for m in range(ROPE // 2):
        c[NOPE + m + ROPE // 2, C_ROT + m] = -1.0
        c[NOPE + m, C_ROT + m + ROPE // 2] = 1.0
    freq = np.float32(10000.0) ** (-np.arange(0, ROPE, 2, dtype=np.float32) / np.float32(ROPE))
    c[NOPE:QKH, C_FREQ] = np.concatenate([freq, freq])
    return c


ROWS = {}
_n = 0
for _name, _k in (("norm_mix_g", KD), ("norm_ffn_g", KD), ("q_norm_g", QC), ("kv_norm_g", KVC), ("attn_out_g", CH),
                  ("rnn_out_g", CH), ("conv_w", CONV * CH), ("conv_b", CH), ("b_a", CH), ("b_i", CH),
                  ("lru_lambda", CH), ("q_head_g", 1), ("k_head_g", 1)):
    ROWS[_name] = (_n, _k)
    _n += DEPTH * _k
NROWS = _n


def tiles(l):
    return (0, 1, 2) if l < DEPTH - 1 else (1, 2)


def first_token(l):
    return TILES[tiles(l)[0]][0]


class Block:

    def __init__(self, bank, order, before, per_order=0, per_before=0):
        self.bank, self.order, self.before = bank, order, before
        self.per_order, self.per_before = per_order, per_before

    def ready(self, i=0):
        return self.order + 1 + self.per_order * i

    def emptied(self, i=0):
        return self.before + self.per_before * i


class Plan:

    def __init__(self):
        self.order, self.before, self.blocks, self.turn = 0, [0] * 8, {}, 0

    def add(self, name, bank=None):
        if bank is None:
            bank, self.turn = self.turn % 4, self.turn + 1
        self.blocks[name] = Block(bank, self.order, self.before[bank])
        self.order += 1
        self.before[bank] += 1

    def loop(self, name, banks, times):
        per = [banks.count(b) for b in range(8)]
        for j, b in enumerate(banks):
            self.blocks[name, j] = Block(b, self.order + j, self.before[b] + banks[:j].count(b), len(banks), per[b])
        self.order += len(banks) * times
        for b in range(8):
            self.before[b] += per[b] * times


class Chain:

    def __init__(self, eng, sem):
        self.eng, self.sem, self.base, self.n = eng, sem, 0, 0

    def link(self, ins):
        ins.then_inc(self.sem, 1)
        self.n += 1
        self.eng.wait_ge(self.sem, self.base + self.n)

    @contextmanager
    def loop(self, times, per):
        start = self.base + self.n
        with self.eng.Fori(0, times) as i:
            self.base, self.n = start + per * i, 0
            yield i
            assert self.n == per, self.n
        self.base, self.n = start + per * times, 0


def plan_blocks():
    pl = Plan()
    for c in range(KD):
        pl.add(("x", c))
    pl.add("vec")
    for l in range(DEPTH):
        def add(*name, bank=None):
            pl.add((l, *name), bank)
        add("n1ss", bank=4)
        add("n1bc", bank=4)
        for n, k in (("xr", CH), ("gt", CH), ("q", QC), ("kv", KVC), ("kr", 1)):
            for c in range(k):
                add(n, c)
        add("cqss", bank=4)
        add("cqbc", bank=4)
        add("kvbc", bank=5)
        for n in ("wa", "wi"):
            for c in range(CH):
                add(n, c)
        for h in range(NH):
            add("uq", h)
        for h in range(NH):
            add("kn", h)
        for t in range(3):
            add("v", t)
        add("krr")
        add("qss", bank=4)
        add("kss", bank=4)
        for h in range(NH):
            add("qr", h)
        for h in range(NH):
            add("kbc", h)
        for t in tiles(l):
            for h in range(NH):
                add("s", t, h)
            for h in range(NH):
                add("p", t, h, bank=6 + h % 2)
            add("o", t, bank=5)
            add("ot", t, bank=4)
        add("rnss", bank=4)
        add("rnbc", bank=4)
        for m in range(KD):
            add("wo", m)
        add("n2ss", bank=4)
        add("n2bc", bank=4)
        if l == 0:
            for j, b in enumerate((0, 1, 2, 3)):
                pl.add(("ff0", j), b)
            pl.loop("ff", [4, 5, 6, 7, 0, 1, 2, 3], 5)
            pl.loop("dn", [4, 5, 6, 7], 2)

        else:
            pl.add("lg", 0)
            pl.add("cum", 1)
            for t in range(2):
                for hf in range(2):
                    pl.add(("ut", t, hf))
            for t in range(2):
                for hf in range(2):
                    pl.add(("ht", t, hf))
    return pl


PER_MIX = 12
MIX_SPLIT = 22
W_IN_COLS = [(QL + KVL + ROPE, GC), (QL + KVL + ROPE + GC, GC), (QL + KVL + ROPE + DH2, GC),
             (QL + KVL + ROPE + DH2 + GC, GC), (0, QL), (QL, KVL + ROPE)]
W_IN_PIECES = [(j, m * P, P) for j in range(5) for m in range(W_IN_COLS[j][1] // P)]
W_IN_PIECES += [(5, 0, P), (5, P, P), (5, KVL + ROPE - QKH, QKH)]
N_IN = len(W_IN_PIECES)
N_FF = 2 * (FF // GC) + KD
MIX0 = [0, PER_MIX + N_FF]
SPLIT0 = [0, MIX_SPLIT + 2 * N_FF]
FF0, FFS0 = PER_MIX, MIX_SPLIT
MOE0, MOES0 = MIX0[1] + PER_MIX, SPLIT0[1] + MIX_SPLIT
PER_EXPERT = 12
EP = 2 * PER_EXPERT
W0 = SPL
XB, XH = (7, 6), (2, 2)
TURN_A, TURN_B = ((1, 4, 3), (0, 2, 4)), ((1, 4, 6), (0, 1, 7))

POWERS, SQUARES, _k, _q = {}, {}, 0, 0
for _l in range(DEPTH):
    for _name in ["n1", "lat", "qk"] + [("att", _t) for _t in tiles(_l)] + ["rnn", "n2"]:
        _k += 1
        POWERS[_l, _name] = _k
    for _name, _m in (("n1", KD // 2), ("lat", 2), ("rnn", 1), ("n2", KD // 2)):
        _q += _m
        SQUARES[_l, _name] = _q
MIXHI = [0, CH * (len(tiles(0)) + 1)]


def build(nc, ins, out):
    pl = plan_blocks()
    B = pl.blocks
    x, positions, meta = ins["x"], ins["positions"], ins["meta_tokens"]

    with ExitStack() as ctx:
        def sem(name):
            return ctx.enter_context(nc.semaphore(name))

        def sb(name, shape, dt=F32, to=ctx):
            return to.enter_context(nc.sbuf_tensor(name, shape, dt))

        ps = ctx.enter_context(nc.psum_tensor("ps", [P, 8, 512], F32))
        raw = sb("raw", [P, RAW, SLOT])
        whi = sb("whi", [P, SPL, PIECE], F32R)
        wlo = sb("wlo", [P, SPL, PIECE], F32R)
        con = sb("con", [P, C_ALL])
        vrow = sb("vrow", [P, P])
        vec = sb("vec", [P, P])
        hT = sb("hT", [P, KD, T])
        u32 = sb("u32", [P, KD, T])
        uhi = sb("uhi", [P, KD, T], F32R)
        ulo = sb("ulo", [P, KD, T], F32R)
        one = sb("one", [P, 1])
        mhalf = sb("mhalf", [P, 1])
        cosT = sb("cosT", [P, T])
        sinT = sb("sinT", [P, T])
        rt = sb("rt", [P, 56])
        gdiag = sb("gdiag", [P, 2, CH, P])
        hba = sb("hba", [P, DEPTH * CH])
        hbi = sb("hbi", [P, DEPTH * CH])
        sp2 = sb("sp2", [P, DEPTH * CH])
        spt = sb("spt", [P, 4, DEPTH * CH])
        small = sb("small", [P, 5, NH])
        scr = sb("scr", [P, 1])
        rw = sb("rw", [P, KD, NE])
        mixer = ExitStack()
        xr = sb("xr", [P, CH, T + CONV - 1], to=mixer)
        gt = sb("gt", [P, CH, T], to=mixer)
        xc = sb("xc", [P, CH, T], to=mixer)
        ta = sb("ta", [P, CH, T], to=mixer)
        tb = sb("tb", [P, CH, T], to=mixer)
        cq = sb("cq", [P, QC, T], to=mixer)
        ckv = sb("ckv", [P, KVC, T], to=mixer)
        kr = sb("kr", [P, 2, T], to=mixer)
        qT = sb("qT", [P, NH, T], to=mixer)
        kT = sb("kT", [P, NH, T], to=mixer)
        vt = sb("vt", [P, 3, DH2], to=mixer)
        pT = sb("pT", [P, 2, 3 * P], to=mixer)
        osb = sb("osb", [P, DH2], to=mixer)
        mixer.close()
        dense = ExitStack()
        ahi = sb("ahi", [P, FC, T], F32R, to=dense)
        alo = sb("alo", [P, FC, T], F32R, to=dense)
        aff = sb("aff", [P, 2, T], to=dense)
        tff = sb("tff", [P, 2, T], to=dense)
        dense.close()
        load = ExitStack()
        xin = sb("xin", [P, 3, D], to=load)
        posi = sb("posi", [P, SEQ], I32, to=load)
        rope = sb("rope", [P, 4, T], to=load)
        load.close()
        moe = ExitStack()
        acc = sb("acc", [P, 2, D], to=moe)
        sel = sb("sel", [P, 2, NE + 1], to=moe)
        gate = sb("gate", [P, 2, NE + 1], to=moe)
        pos = sb("pos", [P, 2, NE + 1], to=moe)
        lgt = sb("lgt", [P, 2, NE], to=moe)
        top = sb("top", [P, 2, 8], to=moe)
        topi = sb("topi", [P, 2, 8], U32, to=moe)
        topf = sb("topf", [P, 2, 8], to=moe)
        rtmp = sb("rtmp", [P, 6, NE], to=moe)
        flag = sb("flag", [P, 1], I32, to=moe)
        onehot = sb("onehot", [P, 2, P], F32R, to=moe)
        onehT = sb("onehT", [P, 2, P], F32R, to=moe)
        identr = sb("identr", [P, P], F32R, to=moe)
        xeh = sb("xeh", [P, KD, P], F32R, to=moe)
        xel = sb("xel", [P, KD, P], F32R, to=moe)
        sg = sb("sg", [P, HALF_A], to=moe)
        act1 = sb("act1", [P, HALF_A], to=moe)
        hact = sb("hact", [P, FE], to=moe)
        heh = sb("heh", [P, FEC, P], F32R, to=moe)
        hel = sb("hel", [P, FEC, P], F32R, to=moe)
        yhi = sb("yhi", [P, D], F32R, to=moe)
        ylo = sb("ylo", [P, D], F32R, to=moe)
        moe.close()

        landed = [sem(f"landed{n}") for n in range(RAW)]
        hi_done = sem("hi_done")
        lo_done = sem("lo_done")
        w_used = sem("w_used")
        filled = sem("filled")
        emptied = [sem(f"emptied{b}") for b in range(8)]
        x_in = sem("x_in")
        con_in = sem("con_in")
        vec_in = sem("vec_in")
        pos_in = sem("pos_in")
        rw_in = sem("rw_in")
        gdiag_in = sem("gdiag_in")
        out_done = sem("out_done")
        zeroed = sem("zeroed")
        vec_done = sem("vec_done")
        hba_done = sem("hba_done")
        h_done = sem("h_done")
        squares = sem("squares")
        var_done = sem("var_done")
        rstd_done = sem("rstd_done")
        u_done = sem("u_done")
        uhi_done = sem("uhi_done")
        ulo_done = sem("ulo_done")
        xc_done = sem("xc_done")
        th_done = sem("th_done")
        w2_done = sem("w2_done")
        root_done = sem("root_done")
        b_done = sem("b_done")
        gsq_done = sem("gsq_done")
        ginner = sem("ginner")
        gtanh = sem("gtanh")
        rnn_done = sem("rnn_done")
        lat_done = sem("lat_done")
        krg_done = sem("krg_done")
        qrot_done = sem("qrot_done")
        kfull = sem("kfull")
        qksq = sem("qksq")
        sc_done = sem("sc_done")
        exp_done = sem("exp_done")
        pt_done = sem("pt_done")
        pv_done = sem("pv_done")
        on_done = sem("on_done")
        mixhi = sem("mixhi")
        mixlo = sem("mixlo")
        rg_done = sem("rg_done")
        sgff = sem("sgff")
        aff_done = sem("aff_done")
        ahi_done = sem("ahi_done")
        alo_done = sem("alo_done")
        angle = sem("angle")
        sine = sem("sine")
        splus = sem("splus")
        splus_e = sem("splus_e")
        top_done = sem("top_done")
        topx = sem("topx")
        sel_done = sem("sel_done")
        flag_done = sem("flag_done")
        tok_hi = sem("tok_hi")
        tok_lo = sem("tok_lo")
        ready0 = sem("ready0")
        qsq_done = sem("qsq_done")
        hot_done = sem("hot_done")
        xr_full = [sem(f"x{b}_full") for b in range(2)]
        xr_hi = [sem(f"x{b}_hi") for b in range(2)]
        xr_free = [sem(f"x{b}_free") for b in range(2)]
        sg_done = sem("sg_done")
        gate_read = sem("gate_read")
        hact_done = sem("hact_done")
        yhi_done = sem("yhi_done")
        ylo_done = sem("ylo_done")
        acc_done = sem("acc_done")
        d_link = sem("d_link")
        a_link = sem("a_link")

        block = ctx.enter_context(nc.Block())
        ident = con[:, C_ID:C_ID + P]

        def col(name, l, k=0, rows=slice(0, P)):
            first, per = ROWS[name]
            n = first + l * per + k
            return vec[rows, n:n + 1]

        def fill(eng, b, i=0):
            if b.before or b.per_before:
                if isinstance(b.emptied(i), int) and b.emptied(i) == 0:
                    return
                eng.wait_ge(emptied[b.bank], b.emptied(i))

        def bank(b, rows=slice(0, P), cols=slice(0, T)):
            return ps[rows, b.bank, cols]

        FFB = B["ff0", 0].order
        IN_BLOCKS = [("xr", c) for c in range(CH)] + [("gt", c) for c in range(CH)] + [("q", c) for c in range(QC)]
        IN_BLOCKS += [("kv", 0), ("kv", 1), ("kr", 0)]

        def piece_used(s):
            for l in range(DEPTH):
                j = s - SPLIT0[l]
                if 0 <= j < N_IN:
                    return B[(l, *IN_BLOCKS[j])].ready()
                if N_IN <= j < MIX_SPLIT:
                    return B[l, "wo", j - N_IN].ready()
            c = s - FFS0
            if c < 44:
                return FFB + c + 1
            return B["dn", 0].order + (c - 44) // 2 + 1

        def piece_of(land, k, cols, at, n):
            return raw[:, land % RAW, 0:k * cols].rearrange("p (k c) -> p k c", k=k)[:, :, at:at + n]

        def mix_piece(l, j):
            if j < N_IN:
                n, at, w = W_IN_PIECES[j]
                return MIX0[l] + n, piece_of(MIX0[l] + n, KD, W_IN_COLS[n][1], at, w)
            n, m = divmod(j - N_IN, 2)
            return MIX0[l] + 8 + n, piece_of(MIX0[l] + 8 + n, KD, GC, m * P, P)

        def ff_piece(c):
            n, m = divmod(c, 2)
            if c < 44:
                return FF0 + n, piece_of(FF0 + n, KD, GC, m * P, P)
            return FF0 + n, piece_of(FF0 + n, FC, P, 0, P)[:, m * FC // 2:(m + 1) * FC // 2, :]

        def expert_piece(c):
            n, m = divmod(c, 2)
            if n < 8:
                w = HALF_A if n < 4 else HALF_B
                return MOE0 + n, piece_of(MOE0 + n, 4, w, 0, w)[:, 2 * m:2 * m + 2, :]
            return MOE0 + n, piece_of(MOE0 + n, 2 if n == 11 else 3, D, m * 512, 512)

        def placed(ring, s, src):
            k, n = src.shape[1], src.shape[2]
            return ring[:, s % SPL, 0:k * n].rearrange("p (k c) -> p k c", k=k)

        def matmul3(pe, dst, w, xs, start, stop, swap=False):
            (wh, wl), (xh, xl) = w, xs
            pe.matmul(dst, wh, xh, start=start, stop=False, skip_group_check=True)
            pe.matmul(dst, wh, xl, start=False, stop=False, skip_group_check=True)
            return pe.matmul(dst, wl, xh, start=False, stop=stop, skip_group_check=True)

        def w_in_src(l, n):
            c, k = W_IN_COLS[n]
            return ins["w_in"][l].rearrange("(k p) c -> p k c", p=P)[:, :, c:c + k], KD, k

        def slot_of(n, k, c):
            s = n % RAW
            return raw[:, s, 0:k * c].rearrange("p (k c) -> p k c", k=k)

        @block.sync
        def _(sp):
            def freed(n, need_lo=None, need_filled=None):
                if need_lo is not None:
                    sp.wait_ge(lo_done, need_lo)
                if need_filled is not None:
                    sp.wait_ge(filled, need_filled)

            def mix_split(l, j):
                return SPLIT0[l] + ((2, 4, 6, 8, 11, 14)[j] if j < 6 else N_IN + 2 * (j - 7))

            def mixer_loads(l):
                for j in range(PER_MIX):
                    n = MIX0[l] + j
                    old = j - RAW
                    if l and old < 0:
                        freed(n, need_lo=SPLIT0[l] + 2 * (old + 1))
                    elif old >= 0:
                        if old in (6, 7):
                            freed(n, need_filled=B[(l, "uq", NH - 1) if old == 6 else (l, "v", 2)].ready())
                        else:
                            freed(n, need_lo=mix_split(l, old))
                    if j < 6:
                        src, k, c = w_in_src(l, j)
                    elif j == 6:
                        src, k, c = ins["w_uq"][l].rearrange("(k p) c -> p k c", p=P), QC, NH * QKH
                    elif j == 7:
                        src, k, c = ins["w_ukv"][l].rearrange("(k p) c -> p k c", p=P), KVC, NH * (NOPE + VH)
                    else:
                        m = (j - 8) * GC
                        src, k, c = ins["w_out"][l].rearrange("(k p) c -> p k c", p=P)[:, :, m:m + GC], KD, GC
                    sp.dma_start(slot_of(n, k, c), src).then_inc(landed[n % RAW], 16)
                    if j == 5:
                        if l:
                            sp.wait_ge(filled, B[0, "wi", CH - 1].ready())
                        else:
                            sp.wait_ge(zeroed, 1)
                        for kind, name in enumerate(("w_a", "w_i")):
                            for s in range(2):
                                r = slice(64 * s, 64 * s + 64)
                                sp.dma_start(gdiag[r, kind, :, r],
                                             ins[name][l].rearrange("(c s) a b -> s a c b", s=2)[s]).then_inc(gdiag_in, 16)

            gsrc = [ins[n][0].rearrange("(k p) c -> p k c", p=P) for n in ("ffn_w_gate", "ffn_w_up")]
            dsrc = ins["ffn_w_down"][0].rearrange("(k p) c -> p k c", p=P)

            mixer_loads(0)
            sp.dma_start(rw[:, :, :], ins["router_w"][0].rearrange("(k p) e -> p k e", p=P)).then_inc(rw_in, 16)
            for j in range(2):
                n = FF0 + j
                freed(n, need_lo=FFS0 + 2 * (j - RAW + 1))
                sp.dma_start(slot_of(n, KD, GC), gsrc[j][:, :, 0:GC]).then_inc(landed[n % RAW], 16)
            with sp.Fori(0, 5) as i:
                for j in range(4):
                    n = FF0 + 2 + j
                    freed(n, need_lo=FFS0 + 2 * (2 + j - RAW + 1) + 8 * i)
                    sp.dma_start(slot_of(n, KD, GC), gsrc[j % 2][:, :, bass.ds((2 * i + j // 2 + 1) * GC, GC)])\
                      .then_inc(landed[n % RAW], 16)
            with sp.Fori(0, 2) as i:
                for j in range(4):
                    n = FF0 + 22 + j
                    freed(n, need_lo=FFS0 + 2 * (22 + j - RAW + 1) + 8 * i)
                    sp.dma_start(slot_of(n, FC, P), dsrc[:, :, bass.ds((4 * i + j) * P, P)])\
                      .then_inc(landed[n % RAW], 16)
            mixer_loads(1)

            eg = [ins[n][0].rearrange("e (k p) c -> e p k c", p=P) for n in ("moe_w_gate", "moe_w_up")]
            ed = ins["moe_w_down"][0].rearrange("e (k p) c -> e p k c", p=P)

            def expert_loads(done):
                with sp.Fori(0, NE) as e:
                    for j in range(PER_EXPERT):
                        n = MOE0 + j
                        freed(n, need_lo=MOES0 + 2 * (j - RAW + 1) + EP * (e + done))
                        if j < 8:
                            hf, kind, kk = j // 4, j // 2 % 2, j % 2
                            c0, c = (0, HALF_A) if hf == 0 else (HALF_A, HALF_B)
                            src = eg[kind][bass.ds(e, 1), :, 4 * kk:4 * kk + 4, c0:c0 + c]
                            k = 4
                        else:
                            k0, k = ((0, 3), (3, 3), (6, 3), (9, 2))[j - 8]
                            c = D
                            src = ed[bass.ds(e, 1), :, k0:k0 + k, :]
                        sp.dma_start(slot_of(n, k, c), src.rearrange("o p k c -> p (o k) c")).then_inc(landed[n % RAW], 16)

            expert_loads(0)
            sp.wait_ge(flag_done, 1)
            more = sp.value_load(flag[0:1, 0:1], min_val=0, max_val=1)
            with sp.If(more > 0):
                expert_loads(NE)
            with sp.Else():
                sp.nop()
            sp.nop()
            sp.wait_ge(acc_done, 1)
            sp.dma_start(out[0].rearrange("(t p) d -> p t d", p=P), acc[:, :, :]).then_inc(out_done, 16)
            sp.wait_ge(out_done, 16)

        @block.gpsimd
        def _(pool):
            n = [0]

            def power(ap):
                n[0] += 1
                pool.wait_ge(var_done, n[0])
                pool.tensor_tensor(ap, ap, mhalf[0:ap.shape[0], :].to_broadcast(list(ap.shape)), ALU.pow)\
                    .then_inc(rstd_done, 1)

            for l in range(DEPTH):
                power(rt[:, 0:3])
                power(rt[:, 0:6])
                power(rt[:, 6:54])
                for t in tiles(l):
                    power(rt[0:TILES[t][1], 54:55])
                power(rt[:, 0:3])
                power(rt[:, 0:3])

        @block.scalar
        def _(act):
            chain = Chain(act, a_link)

            def settle():
                chain.link(act.activation(scr[:, :], scr[:, :], ACT.Copy))

            act.wait_ge(ready0, 1)

            act.dma_start(xin[0:NMETA, 0, :], meta).then_inc(x_in, 16)
            act.dma_start(xin[:, 1:3, :], x[0].rearrange("(t p) d -> p t d", p=P)).then_inc(x_in, 16)
            act.dma_start(con[:, :], ins["constants"]).then_inc(con_in, 16)
            act.wait_ge(zeroed, 1)
            rows = 0
            for name, (first, per) in ROWS.items():
                w = P if per > 1 else QKH
                src = ins[name]
                if name == "conv_w":
                    src = src.rearrange("l j (c p) -> (l j c) p", p=P)
                elif per > 1:
                    src = src.rearrange("l (c p) -> (l c) p", p=P)
                act.dma_start(vrow[first:first + DEPTH * per, 0:w], src).then_inc(vec_in, 16)
                rows += 1
            act.dma_start(posi[NOPE:QKH, :], positions.to_broadcast([ROPE, SEQ])).then_inc(pos_in, 16)

            def split(s, land, src, i=0, chunks=0):
                act.wait_ge(landed[land % RAW], 16 * (land // RAW + 1) + 16 * (chunks // RAW) * i)
                if s >= MOES0:
                    act.wait_ge(w_used, s - MOES0 + 1 + 2 * chunks * i)
                elif s >= SPL:
                    act.wait_ge(filled, piece_used(s - SPL) + 2 * chunks * i)
                act.activation(placed(whi, s, src), src, ACT.Copy).then_inc(hi_done, 1)

            def mix(l, *js):
                for j in js:
                    split(SPLIT0[l] + j, *mix_piece(l, j))

            def ff(c, i=0, chunks=0):
                split(FFS0 + c, *ff_piece(c), i, chunks)

            def take(b, dst, func=ACT.Copy, rows=slice(0, P), cols=slice(0, T), done=None, i=0, **kw):
                act.wait_ge(filled, b.ready(i))
                act.activation(dst, bank(b, rows, cols), func, **kw).then_inc(emptied[b.bank], 1)

            def square(l, c0, base):
                for c in range(0, KD, 2):
                    act.activation(u32[:, c:c + 2, c0:T], hT[:, c:c + 2, c0:T], ACT.Square).then_inc(squares, 1)

            def round_u(n0, c0):
                for c in range(KD):
                    act.wait_ge(u_done, n0 + c + 1)
                    act.activation(uhi[:, c, c0:T], u32[:, c, c0:T], ACT.Copy).then_inc(uhi_done, 1)

            for c in range(1, KD, 2):
                take(B["x", c], hT[:, c, :])
            act.wait_ge(angle, 1)
            act.activation(sinT[NOPE:QKH, :], rope[NOPE:QKH, 2, :], ACT.Sin).then_inc(sine, 1)
            act.wait_ge(angle, 2)
            act.activation(cosT[NOPE:QKH, :], rope[NOPE:QKH, 3, :], ACT.Sin).then_inc(sine, 1)
            act.wait_ge(splus, 1)
            act.activation(spt[:, 1, :], spt[:, 0, :], ACT.Exp, scale=-1.0).then_inc(splus_e, 1)

            for l in range(DEPTH):
                c0 = first_token(l)
                mix(l, *range(SPL))
                act.wait_ge(h_done, 1 + 3 * l)
                if l == 0:
                    settle()
                square(l, 0, 0)
                round_u(2 * KD * l, 0)
                for k, (name, c) in enumerate(IN_BLOCKS):
                    if name == "kr":
                        r = slice(NOPE, QKH)
                        take(B[l, "kr", 0], kr[r, 0, :], rows=r)
                    else:
                        dst = {"xr": xr[:, c, CONV - 1:], "gt": gt[:, c, :], "q": cq[:, c % QC, :], "kv": ckv[:, c % KVC, :]}[name]
                        take(B[l, name, c], dst)
                    if k + SPL < N_IN:
                        mix(l, k + SPL)
                settle()
                act.wait_ge(ulo_done, 2 * KD * l + KD)
                act.activation(u32[:, 0:QC, :], cq[:, :, :], ACT.Square).then_inc(squares, 1)
                act.activation(u32[:, QC:QC + KVC, :], ckv[:, :, :], ACT.Square).then_inc(squares, 1)
                act.wait_ge(hba_done, 1)
                for c in range(CH):
                    b = B[l, "wa", c]
                    n = l * CH + c
                    act.wait_ge(filled, b.ready())
                    act.activation(ta[:, c, :], bank(b), ACT.Tanh, bias=hba[:, n:n + 1], scale=0.5)\
                       .then_inc(emptied[b.bank], 1)
                settle()
                act.wait_ge(vec_done, 2)
                for c in range(CH):
                    n = l * CH + c
                    act.activation(ta[:, c, :], ta[:, c, :], ACT.Tanh, bias=sp2[:, n:n + 1], scale=sp2[:, n:n + 1])\
                       .then_inc(th_done, 1)
                for c in range(CH):
                    b = B[l, "wi", c]
                    n = l * CH + c
                    act.wait_ge(filled, b.ready())
                    act.activation(tb[:, c, :], bank(b), ACT.Tanh, bias=hbi[:, n:n + 1], scale=0.5)\
                       .then_inc(emptied[b.bank], 1)
                r = slice(0, QKH)
                for h in range(NH):
                    b = B[l, "uq", h]
                    act.wait_ge(filled, b.ready())
                    act.activation(qT[r, h, :], bank(b, r), ACT.Copy, scale=col("q_head_g", l, 0, r))
                    act.activation(u32[r, h, :], bank(b, r), ACT.Square).then_inc(emptied[b.bank], 1)
                act.activation(scr[:, :], scr[:, :], ACT.Copy).then_inc(qsq_done, 1)
                for h in range(NH):
                    b = B[l, "kn", h]
                    r = slice(0, NOPE)
                    act.wait_ge(filled, b.ready())
                    act.activation(kT[r, h, :], bank(b, r), ACT.Copy).then_inc(emptied[b.bank], 1)
                for t in range(3):
                    n = TILES[t][1]
                    take(B[l, "v", t], vt[0:n, t, :], rows=slice(0, n), cols=slice(0, DH2))
                act.wait_ge(kfull, l + 1)
                act.wait_ge(filled, B[l, "qss"].ready())
                act.activation(u32[0:QKH, :, :], kT[0:QKH, :, :], ACT.Square).then_inc(qksq, 1)
                act.wait_ge(w2_done, l + 1)
                act.activation(ta[:, :, :], ta[:, :, :], ACT.Sqrt, scale=-1.0).then_inc(root_done, 1)
                act.wait_ge(b_done, l + 1)
                act.activation(ta[:, :, :], gt[:, :, :], ACT.Square).then_inc(gsq_done, 1)
                act.wait_ge(ginner, l + 1)
                act.activation(ta[:, :, :], ta[:, :, :], ACT.Tanh, scale=0.7978845608028654).then_inc(gtanh, 1)
                act.wait_ge(rnn_done, l + 1)
                act.activation(ta[:, :, :], xc[:, :, :], ACT.Square).then_inc(squares, 1)
                mix(l, *range(N_IN, N_IN + SPL))
                for t in tiles(l):
                    k0 = tiles(l).index(t)
                    lead, n = TILES[t]
                    keys = lead + n
                    act.wait_ge(sc_done, len(tiles(0)) * l + k0 + 1)
                    for h in range(NH):
                        act.activation(u32[0:n, h, 0:keys], u32[0:n, h, 0:keys], ACT.Exp, bias=small[0:n, 1, h:h + 1],
                                       accum_out=small[0:n, 2, h:h + 1]).then_inc(exp_done, 1)
                    b = B[l, "ot", t]
                    act.wait_ge(filled, b.ready())
                    for c in range(CH):
                        act.activation(uhi[:, c, lead:lead + n], ps[:, b.bank, c * P:c * P + n], ACT.Copy,
                                       scale=col("attn_out_g", l, c)).then_inc(mixhi, 1)
                for c in range(CH):
                    act.wait_ge(rg_done, CH * l + c + 1)
                    act.activation(uhi[:, CH + c, c0:T], tb[:, c, c0:T], ACT.Copy).then_inc(mixhi, 1)
                mix(l, *range(N_IN + SPL, MIX_SPLIT))
                act.wait_ge(h_done, 2 + 3 * l)
                square(l, c0, 0)
                if l == 0:
                    for c in range(SPL):
                        ff(c)
                    round_u(KD, c0)

                    def tanh_gate(banks, at):
                        act.wait_ge(filled, at)
                        for q in range(2):
                            act.activation(tff[:, q, :], ps[:, banks[q], 0:T], ACT.Tanh, scale=0.5).then_inc(sgff, 1)

                    with act.Fori(0, 5) as i:
                        for g in range(2):
                            j = SPL + 4 * g
                            ff(j, i, 4)
                            ff(j + 1, i, 4)
                            tanh_gate([4, 5] if g else [0, 1], FFB + 2 + 4 * g + 8 * i)
                            ff(j + 2, i, 4)
                            ff(j + 3, i, 4)
                            act.wait_ge(aff_done, 2 * i + g + 1)
                            act.activation(ahi[:, bass.ds(4 * i + 2 * g, 2), :], aff[:, :, :], ACT.Copy).then_inc(ahi_done, 1)
                    ff(44)
                    ff(45)
                    tanh_gate([0, 1], FFB + 42)
                    ff(46)
                    ff(47)
                    act.wait_ge(aff_done, 11)
                    act.activation(ahi[:, 20:22, :], aff[:, :, :], ACT.Copy).then_inc(ahi_done, 1)
                    for c in range(48, 44 + 2 * KD):
                        ff(c)

            act.wait_ge(top_done, 1)
            act.activation(rtmp[:, 1, 0:2], rtmp[:, 0, 0:2], ACT.Exp).then_inc(topx, 1)
            for t in range(2):
                for hf in range(2):
                    b = B["ut", t, hf]
                    act.wait_ge(filled, b.ready())
                    act.activation(uhi[:, :, :].rearrange("p k t -> p (k t)")[:, t * D + hf * 512:t * D + hf * 512 + 512],
                                   ps[:, b.bank, :], ACT.Copy).then_inc(tok_hi, 1)
            for t in range(2):
                for hf in range(2):
                    take(B["ht", t, hf], acc[:, t, hf * 512:hf * 512 + 512], cols=slice(0, 512))

            def experts(p):
                e0 = NE * p
                base = [(XB[b] * NE + 4) * p for b in range(2)]
                def tokens(low, n_full):
                    for q in range(2):
                        bk = 1 - q
                        act.wait_ge(xr_full[bk], n_full[bk])
                        act.activation((xel if low else xeh)[:, 4 * q:4 * q + 4, :],
                                       ps[:, 6 + bk, :].rearrange("p (k n) -> p k n", k=4), ACT.Copy).then_inc(xr_free[bk], 1)

                def result(n_used):
                    act.wait_ge(w_used, n_used)
                    act.activation(yhi[:, :], ps[:, 4:6, :].rearrange("p b n -> p (b n)"), ACT.Copy).then_inc(yhi_done, 1)

                tokens(False, [base[0] + 1, base[1] + 1])
                tokens(True, [base[0] + 2, base[1] + 2])
                base = [b + 2 for b in base]
                with act.Fori(0, NE) as e:
                    n0 = [base[bk] + XB[bk] * e for bk in range(2)]
                    used = W0 + EP * (e + e0)

                    def w(*js):
                        for j in js:
                            land, src = expert_piece(j)
                            split(MOES0 + j + EP * e0, land + PER_EXPERT * e0, src, e, PER_EXPERT)

                    def sigmoid(hf, width):
                        act.wait_ge(w_used, used + 8 * hf + 4)
                        act.activation(sg[:, 0:2 * width].rearrange("p (b n) -> p b n", b=2), ps[:, 0:2, 0:width],
                                       ACT.Tanh, scale=0.5).then_inc(sg_done, 1)

                    def turned(k0, bks):
                        for bk, cnt, blk in bks:
                            act.wait_ge(xr_full[bk], n0[bk] + blk)
                            act.activation(heh[:, k0:k0 + cnt, :], ps[:, 6 + bk, 0:cnt * P].rearrange("p (k n) -> p k n", k=cnt),
                                           ACT.Copy).then_inc(xr_hi[bk], 1)
                            k0 += cnt

                    w(0, 1, 2)
                    result(used)
                    w(3, 4, 5, 6)
                    sigmoid(0, HALF_A // 2)
                    w(7, 8, 9, 10, 11, 12, 13, 14)
                    sigmoid(1, HALF_B // 2)
                    w(15)
                    turned(0, TURN_A)
                    w(16, 17, 18)
                    act.wait_ge(w_used, used + 16)
                    tokens(False, [n0[0] + 5, n0[1] + 4])
                    w(19, 20)
                    tokens(True, [n0[0] + 6, n0[1] + 5])
                    w(21, 22)
                    turned(6, TURN_B)
                    w(23)
                result(W0 + EP * (NE + e0))

            experts(0)
            act.wait_ge(flag_done, 1)
            more = act.value_load(flag[0:1, 0:1], min_val=0, max_val=1)
            with act.If(more > 0):
                experts(1)
            with act.Else():
                act.nop()
            act.nop()

        @block.vector
        def _(dve):
            ch = Chain(dve, d_link)
            link = ch.link

            dve.memset(vrow[:, :], 0.0)
            dve.memset(gdiag[:, :, :, :], 0.0).then_inc(zeroed, 1)
            dve.memset(rt[:, :], 1.0)
            dve.memset(one[:, :], 1.0)
            dve.memset(spt[:, :, :], 0.0)
            dve.memset(scr[:, :], 0.0)
            dve.memset(small[:, :, :], 0.0)
            dve.memset(mhalf[:, :], -0.5).then_inc(ready0, 1)
            dve.wait_ge(ready0, 1)

            def lo(s, land, src, i=0, chunks=0):
                dve.wait_ge(hi_done, s + 1 + 2 * chunks * i)
                dve.tensor_tensor(placed(wlo, s, src), src, placed(whi, s, src).bitcast(F32), ALU.subtract).then_inc(lo_done, 1)

            def mix(l, *js):
                for j in js:
                    lo(SPLIT0[l] + j, *mix_piece(l, j))

            def ff(c, i=0, chunks=0):
                lo(FFS0 + c, *ff_piece(c), i, chunks)

            def sumsq(b, at, tl, width, k0=0, close=True, bank_cols=0):
                dve.wait_ge(filled, b.ready())
                for t in tl:
                    n = TILES[t][1]
                    q = dve.tensor_scalar(rt[0:n, at + t:at + t + 1], ps[0:n, b.bank, at + t:at + t + 1],
                                          1.0 / width, EPS, ALU.mult, ALU.add)
                return q

            def normed(l, name, c0, n0, g):
                tl = (0, 1, 2) if c0 == 0 else (1, 2)
                b = B[l, name + "ss"]
                sumsq(b, 0, tl, D).then_inc(var_done, 1)
                dve.engine_nop().then_inc(emptied[b.bank], 1)
                b = B[l, name + "bc"]
                dve.wait_ge(filled, b.ready())
                for c in range(KD):
                    q = dve.scalar_tensor_tensor(u32[:, c, c0:T], hT[:, c, c0:T], col(g, l, c), bank(b, cols=slice(c0, T)),
                                                 ALU.mult, ALU.mult)
                    q.then_inc(u_done, 1)
                dve.engine_nop().then_inc(emptied[b.bank], 1)

            def lows(n0, c0):
                for c in range(KD):
                    dve.wait_ge(uhi_done, n0 + c + 1)
                    dve.tensor_tensor(ulo[:, c, c0:T], u32[:, c, c0:T], uhi[:, c, c0:T].bitcast(F32), ALU.subtract)\
                       .then_inc(ulo_done, 1)

            for c in range(0, KD, 2):
                b = B["x", c]
                dve.wait_ge(filled, b.ready())
                q = dve.tensor_copy(hT[:, c, :], bank(b))
                q.then_inc(emptied[b.bank], 1)
            b = B["vec"]
            dve.wait_ge(filled, b.ready())
            dve.tensor_copy(vec[:, :], ps[:, b.bank, 0:P]).then_inc(emptied[b.bank], 1)
            dve.wait_ge(emptied[0], 3)
            dve.wait_ge(emptied[1], 2)
            dve.wait_ge(emptied[3], 2)
            dve.engine_nop().then_inc(h_done, 1)
            dve.engine_nop().then_inc(vec_done, 1)
            n = DEPTH * CH
            fa, fi, fl_ = ROWS["b_a"][0], ROWS["b_i"][0], ROWS["lru_lambda"][0]
            dve.tensor_scalar(hba[:, :], vec[:, fa:fa + n], 0.5, None, ALU.mult)
            dve.tensor_scalar(hbi[:, :], vec[:, fi:fi + n], 0.5, None, ALU.mult).then_inc(hba_done, 1)
            link(dve.tensor_scalar(spt[:, 0, :], vec[:, fl_:fl_ + n], -1.0, None, ALU.mult))
            dve.tensor_tensor(spt[:, 0, :], spt[:, 0, :], vec[:, fl_:fl_ + n], ALU.max).then_inc(splus, 1)
            r = slice(NOPE, QKH)
            dve.wait_ge(con_in, 16)
            dve.wait_ge(pos_in, 16)
            dve.tensor_copy(rope[r, 0, 0:NMETA], con[r, C_IOTA:C_IOTA + NMETA])
            link(dve.tensor_copy(rope[r, 0, NMETA:T], posi[r, :]))
            link(dve.tensor_scalar(rope[r, 0, NMETA:T], rope[r, 0, NMETA:T], float(NMETA), None, ALU.add))
            link(dve.tensor_scalar(rope[r, 0, :], rope[r, 0, :], con[r, C_FREQ:C_FREQ + 1], None, ALU.mult))
            magic = 12582912.0
            link(dve.tensor_scalar(rope[r, 1, :], rope[r, 0, :], 0.15915494309189535, magic, ALU.mult, ALU.add))
            link(dve.tensor_scalar(rope[r, 1, :], rope[r, 1, :], magic, None, ALU.subtract))
            for part in (6.28125, 0.0019350051879882812, 3.019916050561733e-07):
                link(dve.scalar_tensor_tensor(rope[r, 0, :], rope[r, 1, :], -part, rope[r, 0, :], ALU.mult, ALU.add))
            pi = 3.1415925
            dve.tensor_scalar(rope[r, 2, :], rope[r, 0, :], pi, -pi, ALU.min, ALU.max).then_inc(angle, 1)
            dve.wait_ge(angle, 1)
            link(dve.tensor_scalar(rope[r, 3, :], rope[r, 2, :], -1.0, None, ALU.mult))
            link(dve.tensor_tensor(rope[r, 3, :], rope[r, 3, :], rope[r, 2, :], ALU.max))
            dve.tensor_scalar(rope[r, 3, :], rope[r, 3, :], -1.0, 1.5707963267948966, ALU.mult, ALU.add).then_inc(angle, 1)
            e, z, z2, w = spt[:, 1, :], spt[:, 2, :], spt[:, 3, :], spt[:, 0, :]
            dve.wait_ge(splus_e, 1)
            link(dve.tensor_scalar(z, e, 2.0, None, ALU.add))
            link(dve.reciprocal(z, z))
            link(dve.tensor_tensor(z, z, e, ALU.mult))
            link(dve.tensor_tensor(z2, z, z, ALU.mult))
            link(dve.tensor_scalar(w, z2, 1.0 / 17, 1.0 / 15, ALU.mult, ALU.add))
            for k in (13, 11, 9, 7, 5, 3, 1):
                link(dve.tensor_tensor(w, w, z2, ALU.mult))
                link(dve.tensor_scalar(w, w, 1.0 / k, None, ALU.add))
            link(dve.tensor_tensor(w, w, z, ALU.mult))
            link(dve.tensor_scalar(e, vec[:, fl_:fl_ + n], -1.0, 0.0, ALU.mult, ALU.max))
            link(dve.scalar_tensor_tensor(e, w, 2.0, e, ALU.mult, ALU.add))
            dve.tensor_scalar(sp2[:, :], e, 2.0, None, ALU.mult).then_inc(vec_done, 1)
            dve.wait_ge(sine, 2)

            for l in range(DEPTH):
                c0 = first_token(l)
                mix(l, *range(SPL))
                dve.wait_ge(h_done, 1 + 3 * l)
                normed(l, "n1", 0, 2 * KD * l, "norm_mix_g")
                lows(2 * KD * l, 0)
                link(dve.memset(xr[:, :, 0:CONV - 1], 0.0))
                for c in range(CH):
                    mix(l, SPL + c)
                    b = B[l, "xr", c]
                    dve.wait_ge(emptied[b.bank], b.before + 1)
                    cw = [vec[:, ROWS["conv_w"][0] + (l * CONV + j) * CH + c:][:, 0:1] for j in range(CONV)]
                    link(dve.tensor_scalar(xc[:, c, :], xr[:, c, 0:T], cw[0], col("conv_b", l, c), ALU.mult, ALU.add))
                    for j in range(1, CONV):
                        q = dve.scalar_tensor_tensor(xc[:, c, :], xr[:, c, j:j + T], cw[j], xc[:, c, :], ALU.mult, ALU.add)
                        if j < CONV - 1:
                            link(q)
                    q.then_inc(xc_done, 1)
                mix(l, *range(SPL + CH, N_IN))
                b = B[l, "cqss"]
                dve.wait_ge(filled, b.ready())
                for t in range(3):
                    k = TILES[t][1]
                    dve.tensor_scalar(rt[0:k, t:t + 1], ps[0:k, b.bank, t:t + 1], 1.0 / QL, EPS, ALU.mult, ALU.add)
                    q = dve.tensor_scalar(rt[0:k, 3 + t:4 + t], ps[0:k, b.bank, 3 + t:4 + t], 1.0 / KVL, EPS, ALU.mult, ALU.add)
                q.then_inc(var_done, 1)
                dve.engine_nop().then_inc(emptied[b.bank], 1)
                b = B[l, "cqbc"]
                dve.wait_ge(filled, b.ready())
                for c in range(QC):
                    q = dve.scalar_tensor_tensor(cq[:, c, :], cq[:, c, :], col("q_norm_g", l, c), bank(b), ALU.mult, ALU.mult)
                    q.then_inc(lat_done, 1)
                dve.engine_nop().then_inc(emptied[b.bank], 1)
                b = B[l, "kvbc"]
                dve.wait_ge(filled, b.ready())
                for c in range(KVC):
                    q = dve.scalar_tensor_tensor(ckv[:, c, :], ckv[:, c, :], col("kv_norm_g", l, c), bank(b), ALU.mult, ALU.mult)
                    q.then_inc(lat_done, 1)
                dve.engine_nop().then_inc(emptied[b.bank], 1)
                r = slice(NOPE, QKH)
                bb = B[l, "kr", 0]
                dve.wait_ge(emptied[bb.bank], bb.before + 1)
                for h in range(NH):
                    q = dve.tensor_copy(kT[r, h, :], kr[r, 0, :])
                link(q)
                dve.tensor_scalar(kr[r, 0, :], kr[r, 0, :], col("k_head_g", l, 0, r), None, ALU.mult).then_inc(krg_done, 1)
                for h in range(NH):
                    b = B[l, "kn", h]
                    dve.wait_ge(emptied[b.bank], b.before + 1)
                dve.engine_nop().then_inc(kfull, 1)
                dve.wait_ge(krg_done, l + 1)
                link(dve.tensor_tensor(kr[r, 1, :], kr[r, 0, :], cosT[r, :], ALU.mult))
                b = B[l, "krr"]
                dve.wait_ge(filled, b.ready())
                q = dve.tensor_tensor(kr[r, 0, :], bank(b, r), sinT[r, :], ALU.mult)
                q.then_inc(emptied[b.bank], 1)
                dve.wait_ge(emptied[b.bank], b.before + 1)
                link(dve.tensor_tensor(kr[r, 1, :], kr[r, 0, :], kr[r, 1, :], ALU.add))
                tmp = xr[:, :, 0:T]
                dve.wait_ge(th_done, CH * (l + 1))
                link(dve.tensor_scalar(tmp, ta[:, :, :], 1.0, None, ALU.add))
                link(dve.reciprocal(tmp, tmp))
                link(dve.tensor_tensor(ta[:, :, :], ta[:, :, :], tmp, ALU.mult))
                link(dve.tensor_scalar(tmp, ta[:, :, :], -2.0, 1.0, ALU.mult, ALU.add))
                dve.scalar_tensor_tensor(ta[:, :, :], ta[:, :, :], 1.0, ta[:, :, :], ALU.subtract, ALU.mult).then_inc(w2_done, 1)
                for c in range(CH):
                    b = B[l, "wi", c]
                    dve.wait_ge(emptied[b.bank], b.before + 1)
                link(dve.scalar_tensor_tensor(tb[:, :, :], tb[:, :, :], 1.0, xc[:, :, :], ALU.add, ALU.mult))
                for h in range(NH):
                    b = B[l, "uq", h]
                    dve.wait_ge(emptied[b.bank], b.before + 1)
                r = slice(NOPE, QKH)
                dve.wait_ge(qksq, l + 1)
                for h in range(NH):
                    dve.tensor_copy(kT[r, h, :], kr[r, 1, :])
                link(dve.tensor_scalar(kT[0:NOPE, :, :], kT[0:NOPE, :, :], col("k_head_g", l, 0, slice(0, NOPE)), None, ALU.mult))
                for name, off, mul, add in (("qss", 0, 1.0, EPS * QKH), ("kss", NH, 1.0 / QKH, EPS)):
                    b = B[l, name]
                    dve.wait_ge(filled, b.ready())
                    for t in range(3):
                        k = TILES[t][1]
                        at = 6 + 16 * t + off
                        q = dve.tensor_scalar(rt[0:k, at:at + NH], ps[0:k, b.bank, 16 * t:16 * t + NH], mul, add,
                                              ALU.mult, ALU.add)
                    if off:
                        q.then_inc(var_done, 1)
                        dve.engine_nop().then_inc(emptied[b.bank], 1)
                    else:
                        q.then_inc(emptied[b.bank], 1)
                for h in range(NH):
                    b = B[l, "qr", h]
                    dve.wait_ge(filled, b.ready())
                    dve.tensor_tensor(u32[r, h, :], bank(b, r), sinT[r, :], ALU.mult).then_inc(emptied[b.bank], 1)
                    q = dve.tensor_tensor(qT[r, h, :], qT[r, h, :], cosT[r, :], ALU.mult)
                link(q)
                dve.tensor_tensor(qT[r, :, :], qT[r, :, :], u32[r, :, :], ALU.add).then_inc(qrot_done, 1)
                r = slice(0, QKH)
                for h in range(NH):
                    b = B[l, "kbc", h]
                    dve.wait_ge(filled, b.ready())
                    dve.tensor_tensor(kT[r, h, :], kT[r, h, :], bank(b, r), ALU.mult).then_inc(emptied[b.bank], 1)
                dve.wait_ge(root_done, l + 1)
                dve.tensor_tensor(tb[:, :, :], tb[:, :, :], ta[:, :, :], ALU.mult).then_inc(b_done, 1)
                dve.wait_ge(b_done, l + 1)
                for c in range(CH):
                    q = dve.tensor_tensor_scan(xc[:, c, :], tmp[:, c, :], tb[:, c, :], 0.0, ALU.mult, ALU.add)
                dve.wait_ge(gsq_done, l + 1)
                link(dve.tensor_scalar(ta[:, :, :], ta[:, :, :], 0.044715, 1.0, ALU.mult, ALU.add))
                dve.tensor_tensor(ta[:, :, :], ta[:, :, :], gt[:, :, :], ALU.mult).then_inc(ginner, 1)
                dve.wait_ge(gtanh, l + 1)
                link(dve.scalar_tensor_tensor(ta[:, :, :], ta[:, :, :], 1.0, gt[:, :, :], ALU.add, ALU.mult))
                dve.scalar_tensor_tensor(xc[:, :, :], ta[:, :, :], 0.5, xc[:, :, :], ALU.mult, ALU.mult).then_inc(rnn_done, 1)
                mix(l, *range(N_IN, N_IN + SPL))
                dve.wait_ge(rstd_done, POWERS[l, "qk"])
                for t in tiles(l):
                    k0 = tiles(l).index(t)
                    lead, n = TILES[t]
                    keys = lead + n
                    m0 = C_MASK + T - P - lead
                    at = 6 + 16 * t
                    for h in range(NH):
                        b = B[l, "s", t, h]
                        dve.wait_ge(filled, b.ready())
                        q = dve.tensor_tensor_reduce(out=u32[0:n, h, 0:keys], in0=ps[0:n, b.bank, 0:keys],
                                                     in1=con[0:n, m0:m0 + keys], scale=rt[0:n, at + h:at + h + 1],
                                                     scalar=-3e38, op0=ALU.add, op1=ALU.max,
                                                     accum_out=small[0:n, 0, h:h + 1])
                        q.then_inc(emptied[b.bank], 1)
                    dve.wait_ge(emptied[b.bank], b.before + 1)
                    dve.tensor_scalar(small[0:n, 1, :], small[0:n, 0, :], -1.0, None, ALU.mult).then_inc(sc_done, 1)
                    for h in range(NH):
                        b = B[l, "p", t, h]
                        dve.wait_ge(filled, b.ready())
                        if h >= 2:
                            dve.wait_ge(pv_done, (NH - 1) * (len(tiles(0)) * l + k0) + h - 1)
                        q = dve.tensor_copy(pT[0:NMETA, h % 2, 0:n], ps[0:NMETA, b.bank, 0:n])
                        if t:
                            q = dve.tensor_copy(pT[:, h % 2, P:(t + 1) * P], ps[:, b.bank, P:(t + 1) * P])
                        q.then_inc(emptied[b.bank], 1)
                    link(dve.reciprocal(small[0:n, 3, :], small[0:n, 2, :]))
                    b = B[l, "o", t]
                    dve.wait_ge(filled, b.ready())
                    q = dve.tensor_tensor(osb[0:n, :].rearrange("p (h d) -> p h d", h=NH),
                                          ps[0:n, b.bank, :].rearrange("p (h d) -> p h d", h=NH),
                                          small[0:n, 3, :].rearrange("p (h o) -> p h o", o=1).to_broadcast([n, NH, VH]), ALU.mult)
                    q.then_inc(emptied[b.bank], 1)
                    dve.wait_ge(emptied[b.bank], b.before + 1)
                    link(dve.tensor_tensor_reduce(out=u32[0:n, 0:2, 0:256], in0=osb[0:n, :].rearrange("p (a b) -> p a b", a=2),
                                                  in1=osb[0:n, :].rearrange("p (a b) -> p a b", a=2), scale=1.0, scalar=0.0,
                                                  op0=ALU.mult, op1=ALU.add, accum_out=small[0:n, 4, 1:2]))
                    dve.tensor_scalar(rt[0:n, 54:55], small[0:n, 4, 1:2], 1.0 / DH2, EPS, ALU.mult, ALU.add).then_inc(var_done, 1)
                    dve.wait_ge(rstd_done, POWERS[l, ("att", t)])
                    dve.tensor_scalar(osb[0:n, :], osb[0:n, :], rt[0:n, 54:55], None, ALU.mult).then_inc(on_done, 1)
                    b = B[l, "ot", t]
                    dve.wait_ge(filled, b.ready())
                    mh = MIXHI[l] + CH * k0
                    dve.wait_ge(mixhi, mh + CH)
                    for c in range(CH):
                        q = dve.scalar_tensor_tensor(ulo[:, c, lead:lead + n], ps[:, b.bank, c * P:c * P + n],
                                                     col("attn_out_g", l, c), uhi[:, c, lead:lead + n].bitcast(F32),
                                                     ALU.mult, ALU.subtract)
                    q.then_inc(emptied[b.bank], 1)
                b = B[l, "rnss"]
                sumsq(b, 0, tiles(l), DH2).then_inc(var_done, 1)
                dve.engine_nop().then_inc(emptied[b.bank], 1)
                b = B[l, "rnbc"]
                dve.wait_ge(filled, b.ready())
                for c in range(CH):
                    dve.scalar_tensor_tensor(tb[:, c, c0:T], xc[:, c, c0:T], col("rnn_out_g", l, c),
                                             bank(b, cols=slice(c0, T)), ALU.mult, ALU.mult).then_inc(rg_done, 1)
                dve.engine_nop().then_inc(emptied[b.bank], 1)
                mh = MIXHI[l] + CH * len(tiles(l))
                for c in range(CH):
                    dve.wait_ge(mixhi, mh + c + 1)
                    q = dve.tensor_tensor(ulo[:, CH + c, c0:T], tb[:, c, c0:T], uhi[:, CH + c, c0:T].bitcast(F32), ALU.subtract)
                q.then_inc(mixlo, 1)
                for m in range(KD):
                    if N_IN + SPL + m < MIX_SPLIT:
                        mix(l, N_IN + SPL + m)
                    b = B[l, "wo", m]
                    dve.wait_ge(filled, b.ready())
                    dve.tensor_tensor(hT[:, m, c0:T], hT[:, m, c0:T], bank(b, cols=slice(c0, T)), ALU.add)\
                       .then_inc(emptied[b.bank], 1)
                for m in range(4, KD):
                    b = B[l, "wo", m]
                    dve.wait_ge(emptied[b.bank], b.before + 1)
                dve.engine_nop().then_inc(h_done, 1)
                if l == 0:
                    for c in range(SPL):
                        ff(c)
                dve.wait_ge(h_done, 2 + 3 * l)
                normed(l, "n2", c0, KD + 2 * KD * l, "norm_ffn_g")
                if l == 0:
                    lows(KD, c0)

                    def group(banks, k, rd, mid, m, lows):
                        for q in range(2):
                            dve.wait_ge(sgff, 2 * k + q + 1)
                            if q == 0:
                                dve.wait_ge(alo_done, k + 1)
                            dve.scalar_tensor_tensor(aff[:, q, :], tff[:, q, :], 1.0, ps[:, banks[q], 0:T], ALU.add, ALU.mult)\
                               .then_inc(emptied[banks[q]], 1)
                        lows()
                        dve.wait_ge(filled, rd)
                        dve.wait_ge(emptied[banks[1]], mid)
                        for q in range(2):
                            x2 = dve.scalar_tensor_tensor(aff[:, q, :], aff[:, q, :], 0.5, ps[:, banks[2 + q], 0:T], ALU.mult, ALU.mult)
                            x2.then_inc(emptied[banks[2 + q]], 1)
                        dve.engine_nop().then_inc(aff_done, 1)
                        dve.wait_ge(ahi_done, k + 1)
                        dve.tensor_tensor(alo[:, bass.ds(m, 2), :], aff[:, :, :], ahi[:, bass.ds(m, 2), :].bitcast(F32),
                                          ALU.subtract).then_inc(alo_done, 1)

                    dve.engine_nop().then_inc(alo_done, 1)
                    with dve.Fori(0, 5) as i:
                        for g, banks in enumerate(([0, 1, 2, 3], [4, 5, 6, 7])):
                            j = SPL + 4 * g
                            ff(j, i, 4)
                            ff(j + 1, i, 4)
                            mid = B[("ff", 1) if g else ("ff0", 1)].before + 1 + i
                            group(banks, 2 * i + g, FFB + 4 + 4 * g + 8 * i, mid, 4 * i + 2 * g,
                                  lambda: (ff(j + 2, i, 4), ff(j + 3, i, 4)))
                    ff(44)
                    ff(45)
                    group([0, 1, 2, 3], 10, FFB + 44, B["ff0", 1].before + 6, 20, lambda: (ff(46), ff(47)))
                    for m in range(KD):
                        if m < KD - 2:
                            ff(48 + 2 * m)
                            ff(49 + 2 * m)
                        i, q = divmod(m, 4)
                        b = B["dn", q]
                        dve.wait_ge(filled, b.ready(i))
                        dve.tensor_tensor(hT[:, m, :], hT[:, m, :], bank(b), ALU.add).then_inc(emptied[b.bank], 1)
                    dve.engine_nop().then_inc(h_done, 2)

            b = B["lg"]
            dve.wait_ge(filled, b.ready())
            dve.memset(sel[:, :, :], 0.0)
            dve.memset(gate[:, :, :], 0.0)
            dve.memset(pos[:, :, :], 0.0)
            dve.tensor_copy(identr[:, :], ident)
            link(dve.tensor_copy(lgt[:, :, :], ps[:, b.bank, 0:2 * NE].rearrange("p (t e) -> p t e", t=2)))
            dve.engine_nop().then_inc(emptied[b.bank], 1)
            for t in range(2):
                q = dve.max(top[:, t, :], lgt[:, t, :])
            link(q)
            for t in range(2):
                q = dve.max_index(topi[:, t, :], top[:, t, :], lgt[:, t, :])
            link(q)
            link(dve.tensor_copy(topf[:, :, :], topi[:, :, :]))
            for t in range(2):
                q = dve.tensor_tensor(rtmp[:, 0, t:t + 1], top[:, t, 1:2], top[:, t, 0:1], ALU.subtract)
            q.then_inc(top_done, 1)
            dve.wait_ge(topx, 1)
            link(dve.tensor_scalar(rtmp[:, 2, 0:2], rtmp[:, 1, 0:2], 1.0, None, ALU.add))
            link(dve.reciprocal(rtmp[:, 2, 0:2], rtmp[:, 2, 0:2]))
            link(dve.tensor_tensor(rtmp[:, 3, 0:2], rtmp[:, 2, 0:2], rtmp[:, 1, 0:2], ALU.mult))
            e8 = con[:, C_E8:C_E8 + NE]
            for t in range(2):
                dve.tensor_scalar(rtmp[:, 4, :], e8, topf[:, t, 0:1], None, ALU.is_equal)
                link(dve.tensor_scalar(rtmp[:, 5, :], e8, topf[:, t, 1:2], None, ALU.is_equal))
                dve.tensor_tensor(sel[:, t, 0:NE], rtmp[:, 4, :], rtmp[:, 5, :], ALU.add)
                link(dve.tensor_scalar(rtmp[:, 4, :], rtmp[:, 4, :], rtmp[:, 2, t:t + 1], None, ALU.mult))
                link(dve.scalar_tensor_tensor(gate[:, t, 1:NE + 1], rtmp[:, 5, :], rtmp[:, 3, t:t + 1], rtmp[:, 4, :],
                                              ALU.mult, ALU.add))
            dve.engine_nop().then_inc(sel_done, 1)
            b = B["cum"]
            dve.wait_ge(filled, b.ready())
            for t in range(2):
                dve.tensor_copy(pos[:, t, 0:NE], ps[:, b.bank, t * NE:t * NE + NE])
            link(dve.tensor_reduce(rtmp[:, 0, 0:1], ps[:, b.bank, 2 * NE:3 * NE], AX.X, ALU.max))
            dve.engine_nop().then_inc(emptied[b.bank], 1)
            dve.tensor_scalar(flag[:, :], rtmp[:, 0, 0:1], float(P), None, ALU.is_gt).then_inc(flag_done, 1)
            for t in range(2):
                for hf in range(2):
                    b = B["ut", t, hf]
                    n = 2 * t + hf
                    dve.wait_ge(tok_hi, n + 1)
                    v = slice(t * D + hf * 512, t * D + hf * 512 + 512)
                    dve.tensor_tensor(ulo[:, :, :].rearrange("p k t -> p (k t)")[:, v], ps[:, b.bank, :],
                                      uhi[:, :, :].rearrange("p k t -> p (k t)")[:, v].bitcast(F32), ALU.subtract)\
                       .then_inc(emptied[b.bank], 1)
            dve.engine_nop().then_inc(tok_lo, 1)
            dve.memset(onehT[:, :, :].bitcast(F32), 0.0)
            dve.memset(ylo[:, :].bitcast(F32), 0.0)
            for t in range(2):
                for hf in range(2):
                    b = B["ht", t, hf]
                    dve.wait_ge(emptied[b.bank], b.before + 1)
            dve.memset(yhi[:, :].bitcast(F32), 0.0)
            dve.engine_nop().then_inc(hact_done, 1)
            dve.engine_nop().then_inc(gate_read, 1)

            def hot(e, p):
                for t in range(2):
                    q = dve.tensor_scalar(onehot[:, t, :], con[:, C_IOTA + P * p:C_IOTA + P * p + P],
                                          pos[:, t, bass.ds(e, 1)], sel[:, t, bass.ds(e, 1)], ALU.is_equal, ALU.mult)
                q.then_inc(hot_done, 1)

            def experts(p):
                e0 = NE * p
                hot(0, p)
                base = [(XB[b] * NE + 4) * p for b in range(2)]
                hbase = [XH[b] * NE * p for b in range(2)]
                base = [b + 2 for b in base]

                def add_expert(t, n_full, gcol):
                    for bk in range(2):
                        dve.wait_ge(xr_full[bk], n_full[bk])
                        v = slice(bk * 512, bk * 512 + 512)
                        dve.scalar_tensor_tensor(acc[:, t, v], ps[:, 6 + bk, :], gate[:, t, bass.ds(gcol, 1)],
                                                 acc[:, t, v], ALU.mult, ALU.add).then_inc(xr_free[bk], 1)

                def result(n_y):
                    dve.wait_ge(yhi_done, n_y)
                    dve.tensor_tensor(ylo[:, :], ps[:, 4:6, :].rearrange("p b n -> p (b n)"), yhi[:, :].bitcast(F32),
                                      ALU.subtract).then_inc(ylo_done, 1)

                with dve.Fori(0, NE) as e:
                    n0 = [base[bk] + XB[bk] * e for bk in range(2)]
                    used = W0 + EP * (e + e0)
                    two = "p (b n) -> p b n"

                    def w(*js):
                        for j in js:
                            land, src = expert_piece(j)
                            lo(MOES0 + j + EP * e0, land + PER_EXPERT * e0, src, e, PER_EXPERT)

                    def turned(k0, bks, k):
                        for bk, cnt, blk in bks:
                            dve.wait_ge(xr_hi[bk], hbase[bk] + k + XH[bk] * e)
                            dve.tensor_tensor(hel[:, k0:k0 + cnt, :], ps[:, 6 + bk, 0:cnt * P].rearrange("p (k n) -> p k n", k=cnt),
                                              heh[:, k0:k0 + cnt, :].bitcast(F32), ALU.subtract).then_inc(xr_free[bk], 1)
                            k0 += cnt

                    def silu(hf, width):
                        dve.wait_ge(sg_done, 2 * (e + e0) + hf + 1)
                        dve.scalar_tensor_tensor(act1[:, 0:2 * width].rearrange(two, b=2), sg[:, 0:2 * width].rearrange(two, b=2),
                                                 1.0, ps[:, 0:2, 0:width], ALU.add, ALU.mult).then_inc(gate_read, 1)

                    def times_up(hf, width):
                        dve.wait_ge(w_used, used + 8 * hf + 8)
                        dve.wait_ge(gate_read, 2 * (e + e0) + hf + 2)
                        half = slice(HALF_A * hf, HALF_A * hf + 2 * width)
                        dve.scalar_tensor_tensor(hact[:, half].rearrange(two, b=2), act1[:, 0:2 * width].rearrange(two, b=2), 0.5,
                                                 ps[:, 2:4, 0:width], ALU.mult, ALU.mult).then_inc(hact_done, 1)

                    w(0, 1, 2)
                    result((NE + 1) * p + e + 1)
                    w(3, 4, 5, 6)
                    silu(0, HALF_A // 2)
                    add_expert(0, [n0[0] + 1, n0[1] + 1], e)
                    w(7, 8, 9)
                    add_expert(1, [n0[0] + 2, n0[1] + 2], e)
                    w(10)
                    times_up(0, HALF_A // 2)
                    w(11)
                    dve.wait_ge(xr_full[0], n0[0] + 3)
                    dve.tensor_copy(onehT[:, :, :], ps[:, 6, 0:2 * P].rearrange("p (t n) -> p t n", t=2)).then_inc(xr_free[0], 1)
                    hot(e + 1, p)
                    w(12, 13, 14)
                    silu(1, HALF_B // 2)
                    w(15)
                    turned(0, TURN_A, 1)
                    w(16, 17, 18)
                    times_up(1, HALF_B // 2)
                    w(19, 20, 21, 22)
                    turned(6, TURN_B, 2)
                    w(23)
                result((NE + 1) * (p + 1))
                for t in range(2):
                    add_expert(t, [base[bk] + XB[bk] * NE + t + 1 for bk in range(2)], NE)

            experts(0)
            more = dve.value_load(flag[0:1, 0:1], min_val=0, max_val=1)
            with dve.If(more > 0):
                experts(1)
            with dve.Else():
                dve.nop()
            dve.nop()
            dve.engine_nop().then_inc(acc_done, 1)

        @block.tensor
        def _(pe):
            pe.wait_ge(ready0, 1)
            pe.wait_ge(con_in, 16)
            pe.wait_ge(x_in, 32)
            for c in range(KD):
                b = B["x", c]
                fill(pe, b)
                for t, (lead, n) in enumerate(TILES):
                    q = pe.transpose(ps[:, b.bank, lead:lead + n], xin[0:n, t, c * P:(c + 1) * P], ident[0:n, 0:n])
                q.then_inc(filled, 1)
            pe.wait_ge(vec_in, 16 * len(ROWS))
            b = B["vec"]
            fill(pe, b)
            pe.transpose(ps[:, b.bank, 0:P], vrow[:, :], ident).then_inc(filled, 1)

            def ones(rows, n):
                return one[rows, :].to_broadcast([rows.stop - rows.start, n])

            def sums(b, at, chunks, src, tl, first=True):
                tl = [t for t in tl if t] + [t for t in tl if not t]
                for t in tl:
                    lead, n = TILES[t]
                    for k, c in enumerate(chunks):
                        q = pe.matmul(ps[0:n, b.bank, at + t:at + t + 1], src[:, c, lead:lead + n], one[:, :],
                                      start=(k == 0), stop=(k == len(chunks) - 1))
                return q

            def spread(b, at, tl, width=P):
                for t in tl:
                    lead, n = TILES[t]
                    q = pe.matmul(ps[0:width, b.bank, lead:lead + n], rt[0:n, at(t):at(t) + 1].to_broadcast([n, width]),
                                  ident[0:n, 0:n], start=True, stop=True)
                return q

            def norm(l, name, tl, nsq):
                b = B[l, name + "ss"]
                fill(pe, b)
                pe.wait_ge(squares, nsq)
                sums(b, 0, range(KD), u32, tl).then_inc(filled, 1)
                b = B[l, name + "bc"]
                fill(pe, b)
                pe.wait_ge(rstd_done, POWERS[l, name])
                spread(b, lambda t: t, tl).then_inc(filled, 1)

            def chunk_ready(s, i=0, per=0):
                pe.wait_ge(lo_done, s + 1 + per * i)

            def dense_block(b, s, k, n, c0, xs, k0=0, start=True, stop=True, wait_x=None):
                xh, xl = xs
                chunk_ready(s)
                for kk in range(k):
                    if wait_x is not None:
                        pe.wait_ge(ulo_done, wait_x + kk + 1)
                    at = kk * n
                    w = (whi[:, s % SPL, at:at + n], wlo[:, s % SPL, at:at + n])
                    q = matmul3(pe, ps[0:n, b.bank, c0:T], w, (xh[:, k0 + kk, c0:T], xl[:, k0 + kk, c0:T]),
                                start and kk == 0, stop and kk == k - 1)
                return q

            for l in range(DEPTH):
                c0 = first_token(l)
                norm(l, "n1", (0, 1, 2), SQUARES[l, "n1"])
                for j, (name, c) in enumerate(IN_BLOCKS):
                    b = B[l, name, c]
                    fill(pe, b)
                    dense_block(b, SPLIT0[l] + j, KD, W_IN_PIECES[j][2], 0, (uhi, ulo), wait_x=2 * KD * l if j == 0 else None)\
                        .then_inc(filled, 1)
                b = B[l, "cqss"]
                fill(pe, b)
                pe.wait_ge(squares, SQUARES[l, "lat"])
                sums(b, 0, range(QC), u32, (0, 1, 2))
                sums(b, 3, range(QC, QC + KVC), u32, (0, 1, 2)).then_inc(filled, 1)
                pe.wait_ge(rstd_done, POWERS[l, "lat"])
                for name, at in (("cqbc", 0), ("kvbc", 3)):
                    b = B[l, name]
                    fill(pe, b)
                    spread(b, lambda t: at + t, (0, 1, 2)).then_inc(filled, 1)
                pe.wait_ge(gdiag_in, 64 * (l + 1))
                for kind, name in enumerate(("wa", "wi")):
                    for c in range(CH):
                        b = B[l, name, c]
                        fill(pe, b)
                        pe.wait_ge(xc_done, CH * l + c + 1)
                        pe.matmul(bank(b), gdiag[:, kind, c, :], xc[:, c, :], start=True, stop=True).then_inc(filled, 1)
                n = MIX0[l] + 6
                wq = raw[:, n % RAW, 0:QC * NH * QKH].rearrange("p (k c) -> p k c", k=QC)
                pe.wait_ge(landed[n % RAW], 16 * (n // RAW + 1))
                pe.wait_ge(lat_done, 5 * l + 3)
                for h in range(NH):
                    b = B[l, "uq", h]
                    fill(pe, b)
                    for k in range(QC):
                        q = pe.matmul(bank(b, slice(0, QKH)), wq[:, k, h * QKH:(h + 1) * QKH], cq[:, k, :],
                                      start=(k == 0), stop=(k == QC - 1))
                    q.then_inc(filled, 1)
                n += 1
                wkv = raw[:, n % RAW, 0:KVC * NH * (NOPE + VH)].rearrange("p (k c) -> p k c", k=KVC)
                pe.wait_ge(landed[n % RAW], 16 * (n // RAW + 1))
                pe.wait_ge(lat_done, 5 * l + 5)
                for h in range(NH):
                    b = B[l, "kn", h]
                    fill(pe, b)
                    for k in range(KVC):
                        at = h * (NOPE + VH)
                        q = pe.matmul(bank(b, slice(0, NOPE)), wkv[:, k, at:at + NOPE], ckv[:, k, :],
                                      start=(k == 0), stop=(k == KVC - 1))
                    q.then_inc(filled, 1)
                for t, (lead, m) in enumerate(TILES):
                    b = B[l, "v", t]
                    fill(pe, b)
                    for k in range(KVC):
                        wv = wkv[:, k, :].rearrange("p (h d) -> p h d", h=NH)[:, :, NOPE:]
                        q = pe.matmul(ps[0:m, b.bank, :].rearrange("p (h d) -> p h d", h=NH), ckv[:, k, lead:lead + m], wv,
                                      start=(k == 0), stop=(k == KVC - 1))
                    q.then_inc(filled, 1)
                r = slice(NOPE, QKH)
                rot = con[r, C_ROT:C_ROT + ROPE]
                b = B[l, "krr"]
                fill(pe, b)
                pe.wait_ge(krg_done, l + 1)
                pe.matmul(bank(b, r), rot, kr[r, 0, :], start=True, stop=True).then_inc(filled, 1)
                for name, done in (("qss", qsq_done), ("kss", qksq)):
                    b = B[l, name]
                    fill(pe, b)
                    pe.wait_ge(done, l + 1)
                    for t in (1, 2, 0):
                        lead, n = TILES[t]
                        for h in range(NH):
                            q = pe.matmul(ps[0:n, b.bank, 16 * t + h:16 * t + h + 1], u32[0:QKH, h, lead:lead + n],
                                          one[0:QKH, :], start=True, stop=True)
                    q.then_inc(filled, 1)
                for h in range(NH):
                    u = B[l, "uq", h]
                    pe.wait_ge(emptied[u.bank], u.before + 1)
                    b = B[l, "qr", h]
                    fill(pe, b)
                    pe.matmul(bank(b, r), rot, qT[r, h, :], start=True, stop=True).then_inc(filled, 1)
                pe.wait_ge(rstd_done, POWERS[l, "qk"])
                for h in range(NH):
                    b = B[l, "kbc", h]
                    fill(pe, b)
                    spread(b, lambda t: 6 + 16 * t + NH + h, (0, 1, 2), QKH).then_inc(filled, 1)
                pe.wait_ge(qrot_done, l + 1)
                for k0, t in enumerate(tiles(l)):
                    lead, n = TILES[t]
                    keys = lead + n
                    turn = len(tiles(0)) * l + k0
                    for h in range(NH):
                        b = B[l, "s", t, h]
                        fill(pe, b)
                        kb = B[l, "kbc", h]
                        pe.wait_ge(emptied[kb.bank], kb.before + 1)
                        pe.matmul(ps[0:n, b.bank, 0:keys], qT[0:QKH, h, lead:lead + n], kT[0:QKH, h, 0:keys],
                                  start=True, stop=True).then_inc(filled, 1)
                    fill(pe, B[l, "o", t])
                    for h in range(NH + 1):
                        if h < NH:
                            b = B[l, "p", t, h]
                            fill(pe, b)
                            pe.wait_ge(exp_done, NH * turn + h + 1)
                            for j in range(t + 1):
                                kl, kn = TILES[j]
                                q = pe.transpose(ps[0:kn, b.bank, j * P:j * P + n], u32[0:n, h, kl:kl + kn], ident[0:n, 0:n])
                            q.then_inc(filled, 1)
                        if h:
                            g = h - 1
                            b = B[l, "p", t, g]
                            pe.wait_ge(emptied[b.bank], b.before + 1)
                            for j in range(t + 1):
                                kn = TILES[j][1]
                                q = pe.matmul(ps[0:n, B[l, "o", t].bank, g * VH:(g + 1) * VH], pT[0:kn, g % 2, j * P:j * P + n],
                                              vt[0:kn, j, g * VH:(g + 1) * VH], start=(j == 0), stop=(j == t))
                            q.then_inc(pv_done if g < NH - 1 else filled, 1)
                    b = B[l, "ot", t]
                    fill(pe, b)
                    pe.wait_ge(on_done, turn + 1)
                    for c in range(CH):
                        q = pe.transpose(ps[:, b.bank, c * P:c * P + n], osb[0:n, c * P:(c + 1) * P], ident[0:n, 0:n])
                    q.then_inc(filled, 1)
                b = B[l, "rnss"]
                fill(pe, b)
                pe.wait_ge(squares, SQUARES[l, "rnn"])
                sums(b, 0, range(CH), ta, tiles(l)).then_inc(filled, 1)
                b = B[l, "rnbc"]
                fill(pe, b)
                pe.wait_ge(rstd_done, POWERS[l, "rnn"])
                spread(b, lambda t: t, tiles(l)).then_inc(filled, 1)
                pe.wait_ge(mixlo, l + 1)
                for m in range(KD):
                    b = B[l, "wo", m]
                    fill(pe, b)
                    dense_block(b, SPLIT0[l] + N_IN + m, KD, P, c0, (uhi, ulo)).then_inc(filled, 1)
                if l == 1:
                    pe.matmul(ps[0:1, B[l, "n2ss"].bank, 511:512], one[:, :], one[:, :], start=True, stop=True)\
                      .then_inc(w_used, W0)
                norm(l, "n2", tiles(l), SQUARES[l, "n2"])
                if l == 0:
                    def group(banks, s, per, i, emp):
                        for m in range(4):
                            chunk_ready(s + m, i, per)
                            pe.wait_ge(emptied[banks[m]], emp[m])
                            for kk in range(KD):
                                if m == 0 and not per:
                                    pe.wait_ge(ulo_done, KD + kk + 1)
                                sl = (s + m) % SPL
                                at = kk * P
                                q = matmul3(pe, ps[:, banks[m], 0:T], (whi[:, sl, at:at + P], wlo[:, sl, at:at + P]),
                                            (uhi[:, kk, :], ulo[:, kk, :]), kk == 0, kk == KD - 1)
                            q.then_inc(filled, 1)

                    group([0, 1, 2, 3], FFS0, 0, 0, [B["ff0", q].before for q in range(4)])
                    with pe.Fori(0, 5) as i:
                        group([4, 5, 6, 7], FFS0 + 4, 8, i, [B["ff", q].emptied(i) for q in range(4)])
                        group([0, 1, 2, 3], FFS0 + 8, 8, i, [B["ff", q].emptied(i) for q in range(4, 8)])
                    pe.wait_ge(alo_done, 12)
                    for m in range(KD):
                        i, q = divmod(m, 4)
                        b = B["dn", q]
                        pe.wait_ge(emptied[b.bank], b.emptied(i))
                        for hf in range(2):
                            q = dense_block(b, FFS0 + 44 + 2 * m + hf, FC // 2, P, 0, (ahi, alo), k0=hf * FC // 2,
                                            start=hf == 0, stop=hf == 1)
                        q.then_inc(filled, 1)

            b = B["lg"]
            fill(pe, b)
            pe.wait_ge(rw_in, 16)
            pe.wait_ge(u_done, 4 * KD)
            for t in range(2):
                lead, n = TILES[t + 1]
                for k in range(KD):
                    q = pe.matmul(ps[:, b.bank, t * NE:(t + 1) * NE], u32[:, k, lead:lead + n], rw[:, k, :],
                                  start=(k == 0), stop=(k == KD - 1))
            q.then_inc(filled, 1)
            b = B["cum"]
            fill(pe, b)
            pe.wait_ge(sel_done, 1)
            before = con[:, C_LT:C_LT + P]
            every = one[:, :].to_broadcast([P, P])
            pe.matmul(ps[:, b.bank, 0:NE], before, sel[:, 0, 0:NE], start=True, stop=True)
            pe.matmul(ps[:, b.bank, NE:2 * NE], every, sel[:, 0, 0:NE], start=True, stop=False)
            pe.matmul(ps[:, b.bank, NE:2 * NE], before, sel[:, 1, 0:NE], start=False, stop=True)
            pe.matmul(ps[:, b.bank, 2 * NE:3 * NE], every, sel[:, 0, 0:NE], start=True, stop=False)
            pe.matmul(ps[:, b.bank, 2 * NE:3 * NE], every, sel[:, 1, 0:NE], start=False, stop=True).then_inc(filled, 1)
            for name, src in (("ut", u32), ("ht", hT)):
                for t in range(2):
                    lead, n = TILES[t + 1]
                    for hf in range(2):
                        b = B[name, t, hf]
                        fill(pe, b)
                        for c in range(4):
                            q = pe.transpose(ps[:, b.bank, c * P:(c + 1) * P], src[:, 4 * hf + c, lead:lead + n], ident)
                        q.then_inc(filled, 1)

            tokh = uhi[:, :, :].rearrange("p k t -> p (k t)")
            tokl = ulo[:, :, :].rearrange("p k t -> p (k t)")
            pe.wait_ge(tok_lo, 1)
            for hf in range(2):
                b = B["ht", 1, hf]
                pe.wait_ge(emptied[b.bank], b.before + 1)
            for b in (4, 5, 6, 7):
                pe.wait_ge(emptied[b], pl.before[b])

            def experts(p):
                e0 = NE * p
                base = [(XB[b] * NE + 4) * p for b in range(2)]

                def room(bk, k):
                    if isinstance(k, int) and k == 0:
                        return
                    pe.wait_ge(xr_free[bk], k)

                def gather(part, blk7, blk6):
                    for q, (bk, k) in enumerate(((1, blk7), (0, blk6))):
                        room(bk, k - 1)
                        for c in range(4):
                            at = (4 * q + c) * P
                            for t in range(2):
                                m = pe.matmul(ps[:, 6 + bk, c * P:(c + 1) * P], part[:, t * D + at:t * D + at + P],
                                              onehot[:, t, :], start=(t == 0), stop=(t == 1))
                        m.then_inc(xr_full[bk], 1)

                def combine(t, blk6, blk7):
                    for hf in range(2):
                        room(hf, (blk6, blk7)[hf] - 1)
                        v = slice(hf * 512, hf * 512 + 512)
                        pe.matmul(ps[:, 6 + hf, :], onehT[:, t, :], yhi[:, v], start=True, stop=False)
                        pe.matmul(ps[:, 6 + hf, :], onehT[:, t, :], ylo[:, v], start=False, stop=True)\
                          .then_inc(xr_full[hf], 1)

                pe.wait_ge(hot_done, (NE + 1) * p + 1)
                gather(tokh, base[1] + 1, base[0] + 1)
                gather(tokl, base[1] + 2, base[0] + 2)
                base = [b + 2 for b in base]
                with pe.Fori(0, NE) as e:
                    n0 = [base[b] + XB[b] * e for b in range(2)]

                    def weights(j):
                        pe.wait_ge(lo_done, MOES0 + j + 1 + EP * (e + e0))
                        return j % SPL

                    def hidden(hf, kind, width, js):
                        for c in js:
                            sl = weights(8 * hf + 4 * kind + c)
                            if c == 0:
                                pe.wait_ge((gate_read, hact_done)[kind], 2 * (e + e0) + hf + 1)
                            for k in range(2):
                                kk = 2 * c + k
                                for xs, ws in ((xeh, (whi, wlo)), (xel, (whi,))):
                                    for w in ws:
                                        for n in range(2):
                                            at = k * 2 * width + n * width
                                            q = pe.matmul(ps[:, 2 * kind + n, 0:width], xs[:, kk, :], w[:, sl, at:at + width],
                                                          start=(kk == 0 and xs is xeh and w is whi),
                                                          stop=(kk == KD - 1 and xs is xel), skip_group_check=True)
                            q.then_inc(w_used, 1)

                    def turn(k0, bks):
                        for bk, cnt, blk in bks:
                            room(bk, n0[bk] + blk - 1)
                            for j in range(cnt):
                                at = (k0 + j) * P
                                q = pe.transpose(ps[:, 6 + bk, j * P:(j + 1) * P], hact[:, at:at + P], ident)
                            q.then_inc(xr_full[bk], 1)
                            k0 += cnt

                    def down(*js):
                        for j in js:
                            sl = weights(j)
                            c, n = divmod(j - 16, 2)
                            for k in range(2 if c == 3 else 3):
                                kk = 3 * c + k
                                for xs, w in ((heh, whi), (heh, wlo), (hel, whi)):
                                    at = k * 512
                                    q = pe.matmul(ps[:, 4 + n, :], xs[:, kk, :], w[:, sl, at:at + 512],
                                                  start=(kk == 0 and xs is heh and w is whi),
                                                  stop=(kk == FEC - 1 and xs is hel), skip_group_check=True)
                            q.then_inc(w_used, 1)

                    for bk in range(2):
                        pe.wait_ge(xr_free[bk], n0[bk])
                    hidden(0, 0, HALF_A // 2, range(4))
                    pe.wait_ge(ylo_done, (NE + 1) * p + e + 1)
                    combine(0, n0[0] + 1, n0[1] + 1)
                    hidden(0, 1, HALF_A // 2, (0, 1))
                    combine(1, n0[0] + 2, n0[1] + 2)
                    hidden(0, 1, HALF_A // 2, (2, 3))
                    room(0, n0[0] + 2)
                    for t in range(2):
                        q = pe.matmul(ps[:, 6, t * P:(t + 1) * P], onehot[:, t, :], identr[:, :], start=True, stop=True)
                    q.then_inc(xr_full[0], 1)
                    hidden(1, 0, HALF_B // 2, range(4))
                    pe.wait_ge(hact_done, 2 * (e + e0) + 2)
                    turn(0, TURN_A)
                    hidden(1, 1, HALF_B // 2, range(4))
                    pe.wait_ge(hot_done, (NE + 1) * p + e + 2)
                    gather(tokh, n0[1] + 4, n0[0] + 5)
                    pe.wait_ge(xr_free[1], n0[1] + 3)
                    pe.wait_ge(xr_free[0], n0[0] + 4)
                    down(16)
                    gather(tokl, n0[1] + 5, n0[0] + 6)
                    down(17, 18)
                    pe.wait_ge(hact_done, 2 * (e + e0) + 3)
                    turn(6, TURN_B)
                    down(19)
                    pe.wait_ge(xr_free[1], n0[1] + 6)
                    pe.wait_ge(xr_free[0], n0[0] + 7)
                    down(20, 21, 22, 23)
                pe.wait_ge(ylo_done, (NE + 1) * (p + 1))
                for t in range(2):
                    combine(t, base[0] + XB[0] * NE + t + 1, base[1] + XB[1] * NE + t + 1)

            experts(0)
            pe.wait_ge(flag_done, 1)
            more = pe.value_load(flag[0:1, 0:1], min_val=0, max_val=1)
            with pe.If(more > 0):
                experts(1)
            with pe.Else():
                pe.nop()
            pe.nop()


_INS = ["x", "positions", "meta_tokens", "norm_mix_g", "w_in", "q_norm_g", "w_uq", "kv_norm_g", "w_ukv", "q_head_g",
        "k_head_g", "conv_w", "conv_b", "w_a", "b_a", "w_i", "b_i", "lru_lambda", "attn_out_g", "rnn_out_g", "w_out",
        "norm_ffn_g", "ffn_w_gate", "ffn_w_up", "ffn_w_down", "router_w", "moe_w_gate", "moe_w_up", "moe_w_down"]


def kernel(**inputs):
    import concourse.bacc as _bacc
    from concourse.bass_utils import run_bass_kernel_spmd as _run

    nc = _bacc.Bacc("TRN2", target_bir_lowering=False, num_devices=1)
    arrays, aps = {}, {}
    given = {name: np.ascontiguousarray(inputs[name]) for name in _INS}
    given["constants"] = constants()
    for name, a in given.items():
        arrays[f"in_{name}_dram"] = a
        aps[name] = nc.dram_tensor(f"in_{name}_dram", a.shape, mybir.dt.from_np(a.dtype), kind="ExternalInput").ap()
    out = nc.dram_tensor("out_0_dram", (1, SEQ, D), F32, kind="ExternalOutput").ap()
    build(nc, aps, out)
    r = _run(nc, [arrays], core_ids=[0])
    return r.results[0]["out_0_dram"]
```

```python
import concourse.bass as bass
from concourse import mybir
from concourse.alu_op_type import AluOpType as ALU
from contextlib import ExitStack, contextmanager
import numpy as np

F32 = mybir.dt.float32
F32R = mybir.dt.float32r
I32 = mybir.dt.int32
U32 = mybir.dt.uint32
ACT = mybir.ActivationFunctionType
AX = mybir.AxisListType

P = 128
D = 1024
KD = D // P
SEQ, NMETA = 256, 16
T = SEQ + NMETA
DEPTH = 2
DH2 = D // 2
CH = DH2 // P
NH, NOPE, ROPE = 8, 64, 32
QKH = NOPE + ROPE
VH = DH2 // NH
QL, KVL = 384, 256
QC, KVC = QL // P, KVL // P
D_IN = QL + KVL + ROPE + 2 * DH2
CONV = 4
FF = 2816
FC = FF // P
NE, FE = 8, 1408
FEC = FE // P
EPS = 1e-6
TILES = [(0, NMETA), (NMETA, P), (NMETA + P, P)]

RAW = 4
SLOT = 3072
SPL = 4
PIECE = 1536
GC = 256
HALF_A = 6 * P
HALF_B = FE - HALF_A

C_ID, C_LT = 0, P
C_MASK = 2 * P
C_IOTA = C_MASK + T
C_E8 = C_IOTA + 2 * P
C_ROT = C_E8 + NE
C_FREQ = C_ROT + ROPE
C_HEAD = C_FREQ + 1
C_KR = C_HEAD + 31
C_LATQ, C_LATK = C_KR + 2 * NH, C_KR + 2 * NH + 2
C_D, C_DH2 = C_LATK + 2, C_LATK + 3
C_ALL = C_DH2 + 1


def constants():
    c = np.zeros((P, C_ALL), np.float32)
    c[:, C_ID:C_ID + P] = np.eye(P)
    c[:, C_LT:C_LT + P] = np.triu(np.ones((P, P)), 1)
    c[:, C_MASK + T - P:C_MASK + T] = np.triu(np.full((P, P), -1e30), 1)
    c[:, C_IOTA:C_IOTA + 2 * P] = np.arange(2 * P)
    c[:, C_E8:C_E8 + NE] = np.arange(NE)
    for m in range(ROPE // 2):
        c[NOPE + m + ROPE // 2, C_ROT + m] = -1.0
        c[NOPE + m, C_ROT + m + ROPE // 2] = 1.0
    freq = np.float32(10000.0) ** (-np.arange(0, ROPE, 2, dtype=np.float32) / np.float32(ROPE))
    c[NOPE:QKH, C_FREQ] = np.concatenate([freq, freq])
    c[:, C_HEAD + 15] = 1 / QKH
    c[:, C_KR + NH:C_KR + 2 * NH] = 1 / QKH
    c[:, C_LATQ], c[:, C_LATK + 1] = 1 / QL, 1 / KVL
    c[:, C_D], c[:, C_DH2] = 1 / D, 1 / DH2
    return c


ROWS = {}
_n = 0
for _name, _k in (("norm_mix_g", KD), ("norm_ffn_g", KD), ("q_norm_g", QC), ("kv_norm_g", KVC), ("attn_out_g", CH),
                  ("rnn_out_g", CH), ("conv_w", CONV * CH), ("conv_b", CH), ("b_a", CH), ("b_i", CH),
                  ("lru_lambda", CH), ("q_head_g", 1), ("k_head_g", 1)):
    ROWS[_name] = (_n, _k)
    _n += DEPTH * _k
NROWS = _n


def tiles(l):
    return (0, 1, 2) if l < DEPTH - 1 else (1, 2)


def first_token(l):
    return TILES[tiles(l)[0]][0]


class Block:

    def __init__(self, bank, order, before, per_order=0, per_before=0):
        self.bank, self.order, self.before = bank, order, before
        self.per_order, self.per_before = per_order, per_before

    def ready(self, i=0):
        return self.order + 1 + self.per_order * i

    def emptied(self, i=0):
        return self.before + self.per_before * i


class Plan:

    def __init__(self):
        self.order, self.before, self.blocks, self.turn = 0, [0] * 8, {}, 0

    def add(self, name, bank=None):
        if bank is None:
            bank, self.turn = self.turn % 4, self.turn + 1
        self.blocks[name] = Block(bank, self.order, self.before[bank])
        self.order += 1
        self.before[bank] += 1

    def loop(self, name, banks, times):
        per = [banks.count(b) for b in range(8)]
        for j, b in enumerate(banks):
            self.blocks[name, j] = Block(b, self.order + j, self.before[b] + banks[:j].count(b), len(banks), per[b])
        self.order += len(banks) * times
        for b in range(8):
            self.before[b] += per[b] * times


class Chain:

    def __init__(self, eng, sem):
        self.eng, self.sem, self.base, self.n = eng, sem, 0, 0

    def link(self, ins):
        ins.then_inc(self.sem, 1)
        self.n += 1
        self.eng.wait_ge(self.sem, self.base + self.n)

    @contextmanager
    def loop(self, times, per):
        start = self.base + self.n
        with self.eng.Fori(0, times) as i:
            self.base, self.n = start + per * i, 0
            yield i
            assert self.n == per, self.n
        self.base, self.n = start + per * times, 0


PER_MIX = 12
MIX_SPLIT = 22
XR0 = QL + KVL + ROPE
W_IN_COLS = [(0, QL), (QL, KVL + ROPE), (XR0, GC), (XR0 + GC, GC), (XR0 + DH2, GC), (XR0 + DH2 + GC, GC)]
CHUNK_OF_IN = [0, 1, 2, 3, 6, 7]
UQ, UKV, WO = 4, 5, 8
W_IN_PIECES = [(0, m * P, P) for m in range(QC)] + [(1, 0, P), (1, P, P), (1, KVL + ROPE - QKH, QKH)]
W_IN_PIECES += [(j, m * P, P) for j in range(2, 6) for m in range(2)]
IN_BLOCKS = [("q", c) for c in range(QC)] + [("kv", 0), ("kv", 1), ("kr", 0)]
IN_BLOCKS += [("xr", c) for c in range(CH)] + [("gt", c) for c in range(CH)]
N_IN = len(W_IN_PIECES)
ATTENTION = [[("scores", 0), ("scores", 1), ("values", 0), ("scores", 2), ("out", 0), ("values", 1), ("rnss", None),
              ("out", 1), ("rnbc", None), ("values", 2), ("out", 2)],
             [("scores", 1), ("scores", 2), ("values", 1), ("rnss", None), ("out", 1), ("rnbc", None), ("values", 2),
              ("out", 2)]]
N_FF = 2 * (FF // GC) + KD
MIX0 = [0, PER_MIX + N_FF]
SPLIT0 = [0, MIX_SPLIT + 2 * N_FF]
FF0, FFS0 = PER_MIX, MIX_SPLIT
MOE0, MOES0 = MIX0[1] + PER_MIX, SPLIT0[1] + MIX_SPLIT


def plan_blocks():
    pl = Plan()
    for c in range(KD):
        pl.add(("x", c))
    pl.add("vec")
    for l in range(DEPTH):
        def add(*name, bank=None):
            pl.add((l, *name), bank)
        for k, (n, c) in enumerate(IN_BLOCKS[:N_IN - CH]):
            add(n, c)
            if k == 0:
                add("n1ss", bank=4)
            if k == 2:
                add("n1bc", bank=4)
            if (n, c) == ("xr", 0):
                add("latss", bank=4)
            if (n, c) == ("xr", 2):
                add("cqbc", bank=4)
                add("kvbc", bank=5)
        for h in range(NH // 2):
            add("uq", h)
        for n in ("wa", "wi"):
            for c in range(CH):
                add(n, c)
        for h in range(NH // 2, NH):
            add("uq", h)
        add("krr")
        for h in range(NH):
            add("kn", h)
        for h in range(NH):
            add("qr", h)
        for t in range(3):
            add("v", t)
        add("qkss", bank=4)
        add("gt", 0, bank=5)
        add("qrt", bank=4)
        for h in range(NH):
            add("kbc", h)
        for c in range(1, CH):
            add("gt", c, bank=(5, 6, 7, 5)[c])
        for what, t in ATTENTION[l]:
            if what == "scores":
                for h in range(NH):
                    add("s", t, h)
            elif what == "values":
                for h in range(NH):
                    add("p", t, h, bank=6 + h % 2)
                add("o", t, bank=5)
            elif what == "out":
                add("ot", t, bank=4)
            else:
                add(what, bank=4)
        for m in range(KD):
            add("wo", m)
        if l == 0:
            for j, b in enumerate((0, 1, 2, 3)):
                pl.add(("ff0", j), b)
            pl.loop("ff", [4, 5, 6, 7, 0, 1, 2, 3], 5)
            pl.loop("dn", [4, 5, 6, 7], 2)

        else:
            add("n2ss", bank=4)
            pl.add("lg", 0)
            for n in ("ut", "ht"):
                for t in range(2):
                    for hf in range(2):
                        pl.add((n, t, hf))
            pl.add("cum", 4)
    return pl


PER_EXPERT = 12
EP = 2 * PER_EXPERT
W0 = SPL
XB, XH = (7, 6), (2, 2)
TURN_A, TURN_B = ((1, 4, 3), (0, 2, 4)), ((1, 4, 6), (0, 1, 7))

POWERS, _k = {}, 0
for _l in range(DEPTH):
    for _name in [("att", _t) for _t in tiles(_l)] + ["n2"] * _l:
        _k += 1
        POWERS[_l, _name] = _k
ROWS_DONE = {}
for _l in range(DEPTH):
    for _name in ["n1", "lat", "qk", "rnn"] + ["n2"] * (1 - _l):
        ROWS_DONE[_l, _name] = len(ROWS_DONE) + 1
MIXHI = [0, CH * (len(tiles(0)) + 1)]


def build(nc, ins, out):
    pl = plan_blocks()
    B = pl.blocks
    x, positions, meta = ins["x"], ins["positions"], ins["meta_tokens"]

    with ExitStack() as ctx:
        def sem(name):
            return ctx.enter_context(nc.semaphore(name))

        def sb(name, shape, dt=F32, to=ctx):
            return to.enter_context(nc.sbuf_tensor(name, shape, dt))

        ps = ctx.enter_context(nc.psum_tensor("ps", [P, 8, 512], F32))
        raw = sb("raw", [P, RAW, SLOT])
        whi = sb("whi", [P, SPL, PIECE], F32R)
        wlo = sb("wlo", [P, SPL, PIECE], F32R)
        con = sb("con", [P, C_ALL])
        vrow = sb("vrow", [P, P])
        vec = sb("vec", [P, P])
        hT = sb("hT", [P, KD, T])
        u32 = sb("u32", [P, KD, T])
        other = ExitStack()
        score1 = sb("score1", [P, NH, T], to=other)
        score2 = sb("score2", [P, NH, T], to=other)
        other.close()
        uhi = sb("uhi", [P, KD, T], F32R)
        ulo = sb("ulo", [P, KD, T], F32R)
        one = sb("one", [P, 1])
        mhalf = sb("mhalf", [P, 1])
        cosT = sb("cosT", [P, T])
        sinT = sb("sinT", [P, T])
        rt = sb("rt", [P, 3, NH])
        rv = sb("rv", [P, 5])
        gdiag = sb("gdiag", [P, 2, CH, P])
        hba = sb("hba", [P, DEPTH * CH])
        hbi = sb("hbi", [P, DEPTH * CH])
        sp4 = sb("sp4", [P, DEPTH * CH])
        spt = sb("spt", [P, 4, DEPTH * CH])
        small = sb("small", [P, 3, 5, NH])
        eps = sb("eps", [P, 1])
        rr = sb("rr", [P, T])
        rsb = sb("rsb", [P, T])
        nsp4 = sb("nsp4", [P, DEPTH * CH])
        scr = sb("scr", [P, 32])
        rw = sb("rw", [P, KD, NE])
        mixer = ExitStack()
        xr = sb("xr", [P, CH, T + CONV - 1], to=mixer)
        gt = sb("gt", [P, CH, T], to=mixer)
        xc = sb("xc", [P, CH, T], to=mixer)
        ta = sb("ta", [P, CH, T], to=mixer)
        tb = sb("tb", [P, CH, T], to=mixer)
        kr = sb("kr", [P, 3, T], to=mixer)
        qT = sb("qT", [P, NH, T], to=mixer)
        kT = sb("kT", [P, NH, T], to=mixer)
        vt = sb("vt", [P, 3, DH2], to=mixer)
        other = ExitStack()
        ksq = sb("ksq", [P, NH, T], to=other)
        other.close()
        mx = sb("mx", [P, 2, CH, T], F32R, to=mixer)
        latent = ExitStack()
        cq = sb("cq", [P, QC, T], to=latent)
        ckv = sb("ckv", [P, KVC, T], to=latent)
        latent.close()
        pT = sb("pT", [P, 2, 3 * P], to=mixer)
        osb = sb("osb", [P, 2, DH2], to=mixer)
        mixer.close()
        other = ExitStack()
        rnh = sb("rnh", [P, CH, T + CONV - 1], F32R, to=other)
        rnl = sb("rnl", [P, CH, T], F32R, to=other)
        other.close()
        dense = ExitStack()
        ahi = sb("ahi", [P, FC, T], F32R, to=dense)
        alo = sb("alo", [P, FC, T], F32R, to=dense)
        aff = sb("aff", [P, 2, T], to=dense)
        tff = sb("tff", [P, 2, T], to=dense)
        gsf = sb("gsf", [P, 2, T], to=dense)
        dense.close()
        load = ExitStack()
        xin = sb("xin", [P, 3, D], to=load)
        posi = sb("posi", [P, SEQ], I32, to=load)
        rope = sb("rope", [P, 4, T], to=load)
        load.close()
        moe = ExitStack()
        acc = sb("acc", [P, 2, D], to=moe)
        sel = sb("sel", [P, 2, NE + 1], to=moe)
        gate = sb("gate", [P, 2, NE + 1], to=moe)
        pos = sb("pos", [P, 2, NE + 1], to=moe)
        lgt = sb("lgt", [P, 2, NE], to=moe)
        top = sb("top", [P, 2, 8], to=moe)
        topi = sb("topi", [P, 2, 8], U32, to=moe)
        topf = sb("topf", [P, 2, 8], to=moe)
        rtmp = sb("rtmp", [P, 6, NE], to=moe)
        flag = sb("flag", [P, 1], I32, to=moe)
        onehot = sb("onehot", [P, 2, P], F32R, to=moe)
        onehT = sb("onehT", [P, 2, P], F32R, to=moe)
        identr = sb("identr", [P, P], F32R, to=moe)
        xeh = sb("xeh", [P, KD, P], F32R, to=moe)
        xel = sb("xel", [P, KD, P], F32R, to=moe)
        sg = sb("sg", [P, HALF_A], to=moe)
        act1 = sb("act1", [P, HALF_A], to=moe)
        hact = sb("hact", [P, FE], to=moe)
        heh = sb("heh", [P, FEC, P], F32R, to=moe)
        hel = sb("hel", [P, FEC, P], F32R, to=moe)
        yhi = sb("yhi", [P, D], F32R, to=moe)
        ylo = sb("ylo", [P, D], F32R, to=moe)
        moe.close()

        landed = [sem(f"landed{n}") for n in range(RAW)]
        hi_done = sem("hi_done")
        lo_done = sem("lo_done")
        w_used = sem("w_used")
        filled = sem("filled")
        emptied = [sem(f"emptied{b}") for b in range(8)]
        x_in = sem("x_in")
        con_in = sem("con_in")
        vec_in = sem("vec_in")
        pos_in = sem("pos_in")
        rw_in = sem("rw_in")
        gdiag_in = sem("gdiag_in")
        out_done = sem("out_done")
        zeroed = sem("zeroed")
        ready0 = sem("ready0")
        vec_done = sem("vec_done")
        hba_done = sem("hba_done")
        h_done = sem("h_done")
        nsq_done = sem("nsq_done")
        uhi_done = sem("uhi_done")
        ulo_done = sem("ulo_done")
        u_done = sem("u_done")
        squares = sem("squares")
        rows_root = sem("rows_root")
        rows_done = sem("rows_done")
        var_done = sem("var_done")
        rstd_done = sem("rstd_done")
        rsb_done = sem("rsb_done")
        cq_raw = sem("cq_raw")
        lat_done = sem("lat_done")
        krg_done = sem("krg_done")
        krsq_done = sem("krsq_done")
        xc_done = sem("xc_done")
        ti_done = sem("ti_done")
        th_done = sem("th_done")
        s_done = sem("s_done")
        root_done = sem("root_done")
        b_done = sem("b_done")
        gt_done = sem("gt_done")
        gsq_done = sem("gsq_done")
        ginner = sem("ginner")
        gtanh = sem("gtanh")
        rnn_done = sem("rnn_done")
        ksq_done = sem("ksq_done")
        qrot_done = sem("qrot_done")
        n2_filled = sem("n2_filled")
        qscale_done = sem("qscale_done")
        sc_done = sem("sc_done")
        exp_done = sem("exp_done")
        pv_done = sem("pv_done")
        on_done = sem("on_done")
        mixhi = sem("mixhi")
        mixlo = sem("mixlo")
        rnlo = sem("rnlo")
        rg_done = sem("rg_done")
        gs_done = sem("gs_done")
        sgff = sem("sgff")
        aff_done = sem("aff_done")
        ahi_done = sem("ahi_done")
        alo_done = sem("alo_done")
        angle = sem("angle")
        sine = sem("sine")
        splus = sem("splus")
        splus_e = sem("splus_e")
        top_done = sem("top_done")
        topx = sem("topx")
        sel_done = sem("sel_done")
        flag_done = sem("flag_done")
        tok_hi = sem("tok_hi")
        tok_lo = sem("tok_lo")
        hot_done = sem("hot_done")
        xr_full = [sem(f"x{b}_full") for b in range(2)]
        xr_hi = [sem(f"x{b}_hi") for b in range(2)]
        xr_free = [sem(f"x{b}_free") for b in range(2)]
        sg_done = sem("sg_done")
        gate_read = sem("gate_read")
        hact_done = sem("hact_done")
        yhi_done = sem("yhi_done")
        ylo_done = sem("ylo_done")
        acc_done = sem("acc_done")
        d_link = sem("d_link")
        a_link = sem("a_link")

        block = ctx.enter_context(nc.Block())
        ident = con[:, C_ID:C_ID + P]

        def col(name, l, k=0, rows=slice(0, P)):
            first, per = ROWS[name]
            n = first + l * per + k
            return vec[rows, n:n + 1]

        def fill(eng, b, i=0):
            if b.before or b.per_before:
                if isinstance(b.emptied(i), int) and b.emptied(i) == 0:
                    return
                eng.wait_ge(emptied[b.bank], b.emptied(i))

        def bank(b, rows=slice(0, P), cols=slice(0, T)):
            return ps[rows, b.bank, cols]

        FFB = B["ff0", 0].order

        def piece_used(s):
            for l in range(DEPTH):
                j = s - SPLIT0[l]
                if 0 <= j < N_IN:
                    return B[(l, *IN_BLOCKS[j])].ready()
                if N_IN <= j < MIX_SPLIT:
                    return B[l, "wo", j - N_IN].ready()
            c = s - FFS0
            if c < 44:
                return FFB + c + 1
            return B["dn", 0].order + (c - 44) // 2 + 1

        def piece_of(land, k, cols, at, n):
            return raw[:, land % RAW, 0:k * cols].rearrange("p (k c) -> p k c", k=k)[:, :, at:at + n]

        def mix_piece(l, j):
            if j < N_IN:
                n, at, w = W_IN_PIECES[j]
                land = MIX0[l] + CHUNK_OF_IN[n]
                return land, piece_of(land, KD, W_IN_COLS[n][1], at, w)
            n, m = divmod(j - N_IN, 2)
            return MIX0[l] + WO + n, piece_of(MIX0[l] + WO + n, KD, GC, m * P, P)

        def ff_piece(c):
            n, m = divmod(c, 2)
            if c < 44:
                return FF0 + n, piece_of(FF0 + n, KD, GC, m * P, P)
            return FF0 + n, piece_of(FF0 + n, FC, P, 0, P)[:, m * FC // 2:(m + 1) * FC // 2, :]

        def expert_piece(c):
            n, m = divmod(c, 2)
            if n < 8:
                w = HALF_A if n < 4 else HALF_B
                return MOE0 + n, piece_of(MOE0 + n, 4, w, 0, w)[:, 2 * m:2 * m + 2, :]
            return MOE0 + n, piece_of(MOE0 + n, 2 if n == 11 else 3, D, m * 512, 512)

        def placed(ring, s, src):
            k, n = src.shape[1], src.shape[2]
            return ring[:, s % SPL, 0:k * n].rearrange("p (k c) -> p k c", k=k)

        scores = [u32, score1, score2]

        def mix_in(kk, rows):
            if kk < CH:
                return mx[:, 0, kk, rows], mx[:, 1, kk, rows]
            return rnh[:, kk - CH, rows], rnl[:, kk - CH, rows]

        def matmul3(pe, dst, w, xs, start, stop, swap=False):
            (wh, wl), (xh, xl) = w, xs
            pe.matmul(dst, wh, xh, start=start, stop=False, skip_group_check=True)
            pe.matmul(dst, wh, xl, start=False, stop=False, skip_group_check=True)
            return pe.matmul(dst, wl, xh, start=False, stop=stop, skip_group_check=True)

        def w_in_src(l, n):
            c, k = W_IN_COLS[n]
            return ins["w_in"][l].rearrange("(k p) c -> p k c", p=P)[:, :, c:c + k], KD, k

        def slot_of(n, k, c):
            s = n % RAW
            return raw[:, s, 0:k * c].rearrange("p (k c) -> p k c", k=k)

        @block.sync
        def _(sp):
            def freed(n, need_lo=None, need_filled=None):
                if need_lo is not None:
                    sp.wait_ge(lo_done, need_lo)
                if need_filled is not None:
                    sp.wait_ge(filled, need_filled)

            def mixer_loads(l):
                pieces = {0: 3, 1: 6, 2: 8, 3: 10, 6: 12, 7: 14, 8: 16, 9: 18, 10: 20, 11: 22}
                for j in range(PER_MIX):
                    n = MIX0[l] + j
                    old = j - RAW
                    if l and old < 0:
                        freed(n, need_lo=SPLIT0[l] + 2 * (old + 1))
                    elif old in (UQ, UKV):
                        freed(n, need_filled=B[(l, "uq", NH - 1) if old == UQ else (l, "v", 2)].ready())
                    elif old >= 0:
                        freed(n, need_lo=SPLIT0[l] + pieces[old])
                    if j in CHUNK_OF_IN:
                        src, k, c = w_in_src(l, CHUNK_OF_IN.index(j))
                    elif j == UQ:
                        src, k, c = ins["w_uq"][l].rearrange("(k p) c -> p k c", p=P), QC, NH * QKH
                    elif j == UKV:
                        src, k, c = ins["w_ukv"][l].rearrange("(k p) c -> p k c", p=P), KVC, NH * (NOPE + VH)
                    else:
                        m = (j - WO) * GC
                        src, k, c = ins["w_out"][l].rearrange("(k p) c -> p k c", p=P)[:, :, m:m + GC], KD, GC
                    sp.dma_start(slot_of(n, k, c), src).then_inc(landed[n % RAW], 16)
                    if j == 3:
                        if l:
                            sp.wait_ge(filled, B[0, "wi", CH - 1].ready())
                        else:
                            sp.wait_ge(zeroed, 2)
                        for kind, name in enumerate(("w_a", "w_i")):
                            for s in range(2):
                                r = slice(64 * s, 64 * s + 64)
                                sp.dma_start(gdiag[r, kind, :, r],
                                             ins[name][l].rearrange("(c s) a b -> s a c b", s=2)[s]).then_inc(gdiag_in, 16)

            gsrc = [ins[n][0].rearrange("(k p) c -> p k c", p=P) for n in ("ffn_w_gate", "ffn_w_up")]
            dsrc = ins["ffn_w_down"][0].rearrange("(k p) c -> p k c", p=P)

            sp.dma_start(xin[:, 1:3, :], x[0].rearrange("(t p) d -> p t d", p=P)).then_inc(x_in, 16)
            sp.dma_start(con[:, :], ins["constants"]).then_inc(con_in, 16)
            sp.wait_ge(zeroed, 1)
            for name, (first, per) in ROWS.items():
                w = P if per > 1 else QKH
                src = ins[name]
                if name == "conv_w":
                    src = src.rearrange("l j (c p) -> (l j c) p", p=P)
                elif per > 1:
                    src = src.rearrange("l (c p) -> (l c) p", p=P)
                sp.dma_start(vrow[first:first + DEPTH * per, 0:w], src).then_inc(vec_in, 16)
            mixer_loads(0)
            sp.dma_start(rw[:, :, :], ins["router_w"][0].rearrange("(k p) e -> p k e", p=P)).then_inc(rw_in, 16)
            for j in range(2):
                n = FF0 + j
                freed(n, need_lo=FFS0 + 2 * (j - RAW + 1))
                sp.dma_start(slot_of(n, KD, GC), gsrc[j][:, :, 0:GC]).then_inc(landed[n % RAW], 16)
            with sp.Fori(0, 5) as i:
                for j in range(4):
                    n = FF0 + 2 + j
                    freed(n, need_lo=FFS0 + 2 * (2 + j - RAW + 1) + 8 * i)
                    sp.dma_start(slot_of(n, KD, GC), gsrc[j % 2][:, :, bass.ds((2 * i + j // 2 + 1) * GC, GC)])\
                      .then_inc(landed[n % RAW], 16)
            with sp.Fori(0, 2) as i:
                for j in range(4):
                    n = FF0 + 22 + j
                    freed(n, need_lo=FFS0 + 2 * (22 + j - RAW + 1) + 8 * i)
                    sp.dma_start(slot_of(n, FC, P), dsrc[:, :, bass.ds((4 * i + j) * P, P)])\
                      .then_inc(landed[n % RAW], 16)
            mixer_loads(1)

            eg = [ins[n][0].rearrange("e (k p) c -> e p k c", p=P) for n in ("moe_w_gate", "moe_w_up")]
            ed = ins["moe_w_down"][0].rearrange("e (k p) c -> e p k c", p=P)

            def expert_loads(done):
                with sp.Fori(0, NE) as e:
                    for j in range(PER_EXPERT):
                        n = MOE0 + j
                        freed(n, need_lo=MOES0 + 2 * (j - RAW + 1) + EP * (e + done))
                        if j < 8:
                            hf, kind, kk = j // 4, j // 2 % 2, j % 2
                            c0, c = (0, HALF_A) if hf == 0 else (HALF_A, HALF_B)
                            src = eg[kind][bass.ds(e, 1), :, 4 * kk:4 * kk + 4, c0:c0 + c]
                            k = 4
                        else:
                            k0, k = ((0, 3), (3, 3), (6, 3), (9, 2))[j - 8]
                            c = D
                            src = ed[bass.ds(e, 1), :, k0:k0 + k, :]
                        sp.dma_start(slot_of(n, k, c), src.rearrange("o p k c -> p (o k) c")).then_inc(landed[n % RAW], 16)

            expert_loads(0)
            sp.wait_ge(flag_done, 1)
            more = sp.value_load(flag[0:1, 0:1], min_val=0, max_val=1)
            with sp.If(more > 0):
                expert_loads(NE)
            with sp.Else():
                sp.nop()
            sp.nop()
            sp.wait_ge(acc_done, 1)
            sp.dma_start(out[0].rearrange("(t p) d -> p t d", p=P), acc[:, :, :]).then_inc(out_done, 16)
            sp.wait_ge(out_done, 16)

        @block.gpsimd
        def _(pool):
            n = [0]

            def power(ap):
                n[0] += 1
                pool.wait_ge(var_done, n[0])
                pool.tensor_tensor(ap, ap, mhalf[0:ap.shape[0], :].to_broadcast(list(ap.shape)), ALU.pow)\
                    .then_inc(rstd_done, 1)

            for l in range(DEPTH):
                for t in tiles(l):
                    power(rv[0:TILES[t][1], t:t + 1])
                if l:
                    power(rv[:, 3:5])

        @block.scalar
        def _(act):
            chain = Chain(act, a_link)

            marks = [0]

            def mark():
                marks[0] += 1
                return act.activation(scr[:, marks[0] - 1:marks[0]], one[:, :], ACT.Copy)

            def settle():
                chain.link(mark())

            act.dma_start(xin[0:NMETA, 0, :], meta).then_inc(x_in, 16)
            act.dma_start(posi[NOPE:QKH, :], positions.to_broadcast([ROPE, SEQ])).then_inc(pos_in, 16)
            act.wait_ge(ready0, 1)

            def split(s, land, src, i=0, chunks=0):
                act.wait_ge(landed[land % RAW], 16 * (land // RAW + 1) + 16 * (chunks // RAW) * i)
                if s >= MOES0:
                    act.wait_ge(w_used, s - MOES0 + 1 + 2 * chunks * i)
                elif s >= SPL:
                    act.wait_ge(filled, piece_used(s - SPL) + 2 * chunks * i)
                act.activation(placed(whi, s, src), src, ACT.Copy).then_inc(hi_done, 1)

            def mix(l, *js):
                for j in js:
                    split(SPLIT0[l] + j, *mix_piece(l, j))

            def ff(c, i=0, chunks=0):
                split(FFS0 + c, *ff_piece(c), i, chunks)

            def take(b, dst, func=ACT.Copy, rows=slice(0, P), cols=slice(0, T), done=None, i=0, **kw):
                act.wait_ge(filled, b.ready(i))
                act.activation(dst, bank(b, rows, cols), func, **kw).then_inc(emptied[b.bank], 1)

            def chunk(phase, c, c0, split_it=True):
                act.wait_ge(h_done, KD * phase + c + 1)
                l, g = divmod(phase, 2)
                if split_it:
                    act.activation(uhi[:, c, c0:T], hT[:, c, c0:T], ACT.Copy,
                                   scale=col(("norm_mix_g", "norm_ffn_g")[g], l, c)).then_inc(uhi_done, 1)
                dst = u32 if split_it else qT
                act.activation(dst[:, c, c0:T], hT[:, c, c0:T], ACT.Square).then_inc(nsq_done, 1)

            def broadcast(b):
                take(b, rsb[:, :])
                mark().then_inc(rsb_done, 1)

            def root_rows(b, rows):
                act.wait_ge(filled, b.ready())
                act.activation(rr[0:rows, :], bank(b, slice(0, rows)), ACT.Sqrt, bias=eps[0:rows, :])\
                    .then_inc(emptied[b.bank], 1)
                act.wait_ge(emptied[b.bank], b.before + 1)
                mark().then_inc(rows_root, 1)

            mix(0, *range(SPL))
            act.wait_ge(vec_done, 1)
            for c in range(KD):
                chunk(0, c, 0)
            act.wait_ge(angle, 1)
            act.activation(sinT[NOPE:QKH, :], rope[NOPE:QKH, 2, :], ACT.Sin).then_inc(sine, 1)
            act.wait_ge(angle, 2)
            act.activation(cosT[NOPE:QKH, :], rope[NOPE:QKH, 3, :], ACT.Sin).then_inc(sine, 1)
            act.wait_ge(splus, 1)
            act.activation(spt[:, 1, :], spt[:, 0, :], ACT.Exp, scale=-1.0).then_inc(splus_e, 1)

            for l in range(DEPTH):
                c0 = first_token(l)
                if l:
                    mix(l, 0, 1)
                    chunk(2, KD - 2, 0)
                    chunk(2, KD - 1, 0)
                    mix(l, 2, 3)
                root_rows(B[l, "n1ss"], 1)
                for k, (name, c) in enumerate(IN_BLOCKS[:N_IN - CH]):
                    if k == 2:
                        broadcast(B[l, "n1bc"])
                    if (name, c) == ("xr", 1):
                        root_rows(B[l, "latss"], 2)
                    if name == "xr" and c == 0:
                        act.wait_ge(cq_raw, 6 * l + 6)
                        act.activation(u32[:, 0:QC, :], cq[:, :, :], ACT.Square).then_inc(squares, 1)
                        act.activation(u32[:, QC:QC + KVC, :], ckv[:, :, :], ACT.Square).then_inc(squares, 1)
                        act.activation(kr[NOPE:QKH, 2, :], kr[NOPE:QKH, 0, :], ACT.Square).then_inc(krsq_done, 1)
                    mix(l, k + SPL)

                def queries(hs):
                    r = slice(0, QKH)
                    for h in hs:
                        b = B[l, "uq", h]
                        act.wait_ge(filled, b.ready())
                        act.activation(qT[r, h, :], bank(b, r), ACT.Copy, scale=col("q_head_g", l, 0, r))
                        act.activation(u32[r, h, :], bank(b, r), ACT.Square).then_inc(emptied[b.bank], 1)

                queries(range(NH // 2))
                act.wait_ge(hba_done, 1)
                for name, dst, bias in (("wa", ta, hba), ("wi", tb, hbi)):
                    for c in range(CH):
                        b = B[l, name, c]
                        n = l * CH + c
                        act.wait_ge(filled, b.ready())
                        act.activation(dst[:, c, :], bank(b), ACT.Tanh, bias=bias[:, n:n + 1], scale=0.5)\
                           .then_inc(emptied[b.bank], 1)
                mark().then_inc(ti_done, 1)
                act.wait_ge(vec_done, 2)
                act.wait_ge(xc_done, CH * (l + 1))
                def decays():
                    for c in range(CH):
                        n = l * CH + c
                        act.activation(xr[:, c, 0:T], ta[:, c, :], ACT.Exp, bias=nsp4[:, n:n + 1], scale=nsp4[:, n:n + 1])
                    settle()
                    for c in range(CH):
                        n = l * CH + c
                        act.activation(ta[:, c, :], ta[:, c, :], ACT.Tanh, bias=sp4[:, n:n + 1], scale=sp4[:, n:n + 1])\
                           .then_inc(th_done, 1)

                queries(range(NH // 2, NH))
                decays()
                for h in range(NH):
                    b = B[l, "kn", h]
                    r = slice(0, NOPE)
                    act.wait_ge(filled, b.ready())
                    act.activation(kT[r, h, :], bank(b, r), ACT.Copy)
                    act.activation(ksq[r, h, :], bank(b, r), ACT.Square).then_inc(emptied[b.bank], 1)
                mark().then_inc(ksq_done, 1)
                for t in range(3):
                    n = TILES[t][1]
                    take(B[l, "v", t], vt[0:n, t, :], rows=slice(0, n), cols=slice(0, DH2))
                act.wait_ge(s_done, l + 1)
                act.activation(ta[:, :, :], ta[:, :, :], ACT.Sqrt, scale=0.25).then_inc(root_done, 1)
                root_rows(B[l, "qkss"], 2 * NH)
                b = B[l, "qrt"]
                act.wait_ge(filled, b.ready())
                for t in range(3):
                    n = TILES[t][1]
                    q = act.activation(rt[0:n, t, :], ps[0:n, b.bank, NH * t:NH * t + NH], ACT.Copy, scale=QKH ** -0.5)
                q.then_inc(emptied[b.bank], 1)
                mark().then_inc(qscale_done, 1)
                act.wait_ge(gt_done, l + 1)
                act.wait_ge(b_done, l + 1)
                act.activation(ta[:, :, :], gt[:, :, :], ACT.Square).then_inc(gsq_done, 1)

                def exponential(t, h):
                    lead, n = TILES[t]
                    keys = lead + n
                    act.activation(scores[t][0:n, h, 0:keys], scores[t][0:n, h, 0:keys], ACT.Exp,
                                   bias=small[0:n, t, 1, h:h + 1], accum_out=small[0:n, t, 2, h:h + 1]).then_inc(exp_done, 1)

                def turned(t, h):
                    n = TILES[t][1]
                    k0 = tiles(l).index(t)
                    b = B[l, "p", t, h]
                    act.wait_ge(filled, b.ready())
                    if h >= 2:
                        act.wait_ge(pv_done, (NH - 1) * (len(tiles(0)) * l + k0) + h - 1)
                    q = act.activation(pT[0:NMETA, 1, 0:n], ps[0:NMETA, b.bank, 0:n], ACT.Copy)
                    if t:
                        q = act.activation(pT[:, 1, P:(t + 1) * P], ps[:, b.bank, P:(t + 1) * P], ACT.Copy)
                    q.then_inc(emptied[b.bank], 1)

                def out_high(t):
                    lead, n = TILES[t]
                    b = B[l, "ot", t]
                    act.wait_ge(filled, b.ready())
                    for c in range(CH):
                        act.activation(mx[:, 0, c, lead:lead + n], ps[:, b.bank, c * P:c * P + n], ACT.Copy,
                                       scale=col("attn_out_g", l, c)).then_inc(mixhi, 1)

                def rn_high():
                    for c in range(CH):
                        act.wait_ge(rg_done, CH * l + c + 1)
                        act.activation(rnh[:, c, c0:T], tb[:, c, c0:T], ACT.Copy).then_inc(mixhi, 1)

                tl = tiles(l)
                for k0, t in enumerate(tl):
                    act.wait_ge(sc_done, len(tiles(0)) * l + k0 + 1)
                    for h in range(NH):
                        exponential(t, h)
                        if k0 and h % 2:
                            turned(tl[k0 - 1], h)
                            if t == 2:
                                mix(l, N_IN + h // 2)
                    if k0 == 0:
                        act.wait_ge(ginner, l + 1)
                        act.activation(ta[:, :, :], ta[:, :, :], ACT.Tanh, scale=0.7978845608028654).then_inc(gtanh, 1)
                    elif k0 == 1:
                        act.wait_ge(rnn_done, l + 1)
                        act.activation(ta[:, :, :], xc[:, :, :], ACT.Square).then_inc(squares, 1)
                    if t == 2 and l == 0:
                        out_high(0)
                    if t == 2:
                        root_rows(B[l, "rnss"], 1)
                t = tl[-1]
                out_high(1)
                for h in range(1, NH, 2):
                    turned(t, h)
                    if h == 3:
                        rn_high()
                out_high(2)
                for m in range(KD):
                    chunk(2 * l + 1, m, c0, split_it=l == 0)
                    if m < SPL:
                        mix(l, N_IN + SPL + m)
                    if m >= SPL and l == 0:
                        ff(m - SPL)
                if l == 0:
                    act.wait_ge(n2_filled, 1)
                    act.activation(rr[0:1, :], ps[0:1, 4, 0:T], ACT.Sqrt, bias=eps[0:1, :]).then_inc(rows_root, 1)
                    act.wait_ge(n2_filled, 2)
                    act.activation(rsb[:, :], ps[:, 4, 0:T], ACT.Copy).then_inc(rsb_done, 1)

                    def tanh_gate(k):
                        act.wait_ge(gs_done, k)
                        act.activation(tff[:, :, :], gsf[:, :, :], ACT.Tanh, scale=0.5).then_inc(sgff, 1)

                    with act.Fori(0, 5) as i:
                        for g in range(2):
                            j = SPL + 4 * g
                            ff(j, i, 4)
                            ff(j + 1, i, 4)
                            tanh_gate(2 * i + g + 1)
                            ff(j + 2, i, 4)
                            ff(j + 3, i, 4)
                            act.wait_ge(aff_done, 2 * i + g + 1)
                            act.activation(ahi[:, bass.ds(4 * i + 2 * g, 2), :], aff[:, :, :], ACT.Copy).then_inc(ahi_done, 1)
                    ff(44)
                    ff(45)
                    tanh_gate(11)
                    ff(46)
                    ff(47)
                    act.wait_ge(aff_done, 11)
                    act.activation(ahi[:, 20:22, :], aff[:, :, :], ACT.Copy).then_inc(ahi_done, 1)
                    for m in range(KD):
                        if m < KD - 2:
                            ff(48 + 2 * m)
                            ff(49 + 2 * m)
                            chunk(2, m, 0)

            act.wait_ge(top_done, 1)
            act.activation(rtmp[:, 1, 0:2], rtmp[:, 0, 0:2], ACT.Exp).then_inc(topx, 1)
            for t in range(2):
                for hf in range(2):
                    b = B["ut", t, hf]
                    act.wait_ge(filled, b.ready())
                    act.wait_ge(rstd_done, POWERS[1, "n2"])
                    act.activation(uhi[:, :, :].rearrange("p k t -> p (k t)")[:, t * D + hf * 512:t * D + hf * 512 + 512],
                                   ps[:, b.bank, :], ACT.Copy, scale=rv[:, t + 3:t + 4]).then_inc(tok_hi, 1)
            for t in range(2):
                for hf in range(2):
                    take(B["ht", t, hf], acc[:, t, hf * 512:hf * 512 + 512], cols=slice(0, 512))

            def experts(p):
                e0 = NE * p
                base = [(XB[b] * NE + 4) * p for b in range(2)]
                def tokens(low, n_full):
                    for q in range(2):
                        bk = 1 - q
                        act.wait_ge(xr_full[bk], n_full[bk])
                        act.activation((xel if low else xeh)[:, 4 * q:4 * q + 4, :],
                                       ps[:, 6 + bk, :].rearrange("p (k n) -> p k n", k=4), ACT.Copy).then_inc(xr_free[bk], 1)

                def result(n_used):
                    act.wait_ge(w_used, n_used)
                    act.activation(yhi[:, :], ps[:, 4:6, :].rearrange("p b n -> p (b n)"), ACT.Copy).then_inc(yhi_done, 1)

                tokens(False, [base[0] + 1, base[1] + 1])
                tokens(True, [base[0] + 2, base[1] + 2])
                base = [b + 2 for b in base]
                with act.Fori(0, NE) as e:
                    n0 = [base[bk] + XB[bk] * e for bk in range(2)]
                    used = W0 + EP * (e + e0)

                    def w(*js):
                        for j in js:
                            land, src = expert_piece(j)
                            split(MOES0 + j + EP * e0, land + PER_EXPERT * e0, src, e, PER_EXPERT)

                    def sigmoid(hf, width):
                        act.wait_ge(w_used, used + 8 * hf + 4)
                        act.activation(sg[:, 0:2 * width].rearrange("p (b n) -> p b n", b=2), ps[:, 0:2, 0:width],
                                       ACT.Tanh, scale=0.5).then_inc(sg_done, 1)

                    def turned(k0, bks):
                        for bk, cnt, blk in bks:
                            act.wait_ge(xr_full[bk], n0[bk] + blk)
                            act.activation(heh[:, k0:k0 + cnt, :], ps[:, 6 + bk, 0:cnt * P].rearrange("p (k n) -> p k n", k=cnt),
                                           ACT.Copy).then_inc(xr_hi[bk], 1)
                            k0 += cnt

                    w(0, 1, 2)
                    result(used)
                    w(3, 4, 5, 6)
                    sigmoid(0, HALF_A // 2)
                    w(7, 8, 9, 10, 11, 12, 13, 14)
                    sigmoid(1, HALF_B // 2)
                    w(15)
                    turned(0, TURN_A)
                    w(16, 17, 18)
                    act.wait_ge(w_used, used + 16)
                    tokens(False, [n0[0] + 5, n0[1] + 4])
                    w(19, 20)
                    tokens(True, [n0[0] + 6, n0[1] + 5])
                    w(21, 22)
                    turned(6, TURN_B)
                    w(23)
                result(W0 + EP * (NE + e0))

            experts(0)
            act.wait_ge(flag_done, 1)
            more = act.value_load(flag[0:1, 0:1], min_val=0, max_val=1)
            with act.If(more > 0):
                experts(1)
            with act.Else():
                act.nop()
            act.nop()

        @block.vector
        def _(dve):
            ch = Chain(dve, d_link)
            link = ch.link

            dve.memset(vrow[:, :], 0.0).then_inc(zeroed, 1)
            dve.memset(gdiag[:, :, :, :], 0.0).then_inc(zeroed, 1)
            dve.memset(rt[:, :, :], 1.0)
            dve.memset(rv[:, :], 1.0)
            dve.memset(one[:, :], 1.0)
            dve.memset(spt[:, :, :], 0.0)
            dve.memset(scr[:, :], 0.0)
            dve.memset(small[:, :, :, :], 0.0)
            dve.memset(eps[:, :], EPS)
            dve.memset(mhalf[:, :], -0.5).then_inc(ready0, 1)
            dve.wait_ge(ready0, 1)

            def lo(s, land, src, i=0, chunks=0):
                dve.wait_ge(hi_done, s + 1 + 2 * chunks * i)
                dve.tensor_tensor(placed(wlo, s, src), src, placed(whi, s, src).bitcast(F32), ALU.subtract).then_inc(lo_done, 1)

            def mix(l, *js):
                for j in js:
                    lo(SPLIT0[l] + j, *mix_piece(l, j))

            def ff(c, i=0, chunks=0):
                lo(FFS0 + c, *ff_piece(c), i, chunks)

            def rows(l, name, n):
                dve.wait_ge(rows_root, ROWS_DONE[l, name])
                dve.reciprocal(rr[0:n, :], rr[0:n, :]).then_inc(rows_done, 1)

            def low_chunk(phase, c, c0):
                l, g = divmod(phase, 2)
                dve.wait_ge(uhi_done, KD * phase + c + 1)
                dve.scalar_tensor_tensor(ulo[:, c, c0:T], hT[:, c, c0:T], col(("norm_mix_g", "norm_ffn_g")[g], l, c),
                                         uhi[:, c, c0:T].bitcast(F32), ALU.mult, ALU.subtract).then_inc(ulo_done, 1)

            for c in range(KD):
                b = B["x", c]
                dve.wait_ge(filled, b.ready())
                dve.tensor_copy(hT[:, c, :], bank(b)).then_inc(emptied[b.bank], 1)
                dve.engine_nop().then_inc(h_done, 1)
            mix(0, *range(SPL))
            b = B["vec"]
            dve.wait_ge(filled, b.ready())
            dve.tensor_copy(vec[:, :], ps[:, b.bank, 0:P]).then_inc(emptied[b.bank], 1)
            dve.wait_ge(emptied[b.bank], b.before + 1)
            dve.engine_nop().then_inc(vec_done, 1)
            for c in range(KD):
                low_chunk(0, c, 0)
            n = DEPTH * CH
            fa, fi, fl_ = ROWS["b_a"][0], ROWS["b_i"][0], ROWS["lru_lambda"][0]
            dve.tensor_scalar(hba[:, :], vec[:, fa:fa + n], 0.5, None, ALU.mult)
            dve.tensor_scalar(hbi[:, :], vec[:, fi:fi + n], 0.5, None, ALU.mult).then_inc(hba_done, 1)
            link(dve.tensor_scalar(spt[:, 0, :], vec[:, fl_:fl_ + n], -1.0, None, ALU.mult))
            dve.tensor_tensor(spt[:, 0, :], spt[:, 0, :], vec[:, fl_:fl_ + n], ALU.max).then_inc(splus, 1)
            r = slice(NOPE, QKH)
            dve.wait_ge(con_in, 16)
            dve.wait_ge(pos_in, 16)
            dve.tensor_copy(rope[r, 0, 0:NMETA], con[r, C_IOTA:C_IOTA + NMETA])
            link(dve.tensor_copy(rope[r, 0, NMETA:T], posi[r, :]))
            link(dve.tensor_scalar(rope[r, 0, NMETA:T], rope[r, 0, NMETA:T], float(NMETA), None, ALU.add))
            link(dve.tensor_scalar(rope[r, 0, :], rope[r, 0, :], con[r, C_FREQ:C_FREQ + 1], None, ALU.mult))
            magic = 12582912.0
            link(dve.tensor_scalar(rope[r, 1, :], rope[r, 0, :], 0.15915494309189535, magic, ALU.mult, ALU.add))
            link(dve.tensor_scalar(rope[r, 1, :], rope[r, 1, :], magic, None, ALU.subtract))
            for part in (6.28125, 0.0019350051879882812, 3.019916050561733e-07):
                link(dve.scalar_tensor_tensor(rope[r, 0, :], rope[r, 1, :], -part, rope[r, 0, :], ALU.mult, ALU.add))
            pi = 3.1415925
            dve.tensor_scalar(rope[r, 2, :], rope[r, 0, :], pi, -pi, ALU.min, ALU.max).then_inc(angle, 1)
            dve.wait_ge(angle, 1)
            link(dve.tensor_scalar(rope[r, 3, :], rope[r, 2, :], -1.0, None, ALU.mult))
            link(dve.tensor_tensor(rope[r, 3, :], rope[r, 3, :], rope[r, 2, :], ALU.max))
            dve.tensor_scalar(rope[r, 3, :], rope[r, 3, :], -1.0, 1.5707963267948966, ALU.mult, ALU.add).then_inc(angle, 1)
            e, z, z2, w = spt[:, 1, :], spt[:, 2, :], spt[:, 3, :], spt[:, 0, :]
            dve.wait_ge(splus_e, 1)
            link(dve.tensor_scalar(z, e, 2.0, None, ALU.add))
            link(dve.reciprocal(z, z))
            link(dve.tensor_tensor(z, z, e, ALU.mult))
            link(dve.tensor_tensor(z2, z, z, ALU.mult))
            link(dve.tensor_scalar(w, z2, 1.0 / 17, 1.0 / 15, ALU.mult, ALU.add))
            for k in (13, 11, 9, 7, 5, 3, 1):
                link(dve.tensor_tensor(w, w, z2, ALU.mult))
                link(dve.tensor_scalar(w, w, 1.0 / k, None, ALU.add))
            link(dve.tensor_tensor(w, w, z, ALU.mult))
            link(dve.tensor_scalar(e, vec[:, fl_:fl_ + n], -1.0, 0.0, ALU.mult, ALU.max))
            link(dve.scalar_tensor_tensor(e, w, 2.0, e, ALU.mult, ALU.add))
            dve.tensor_scalar(sp4[:, :], e, 4.0, None, ALU.mult)
            dve.tensor_scalar(nsp4[:, :], e, -4.0, None, ALU.mult).then_inc(vec_done, 1)
            dve.wait_ge(sine, 2)

            for l in range(DEPTH):
                c0 = first_token(l)
                if l:
                    mix(l, 2, 3)
                rows(l, "n1", 1)
                dve.wait_ge(rsb_done, 2 * l + 1)

                def scaled(name, c):
                    b = B[l, name, c]
                    r = slice(NOPE, QKH) if name == "kr" else slice(0, P)
                    dst = {"q": cq[:, c % QC, :], "kv": ckv[:, c % KVC, :], "kr": kr[r, 0, :], "xr": xr[:, c, CONV - 1:],
                           "gt": gt[:, c, :]}[name]
                    dve.wait_ge(filled, b.ready())
                    dve.tensor_tensor(dst, bank(b, r), rsb[r, :], ALU.mult).then_inc(emptied[b.bank], 1)
                    dve.wait_ge(emptied[b.bank], b.before + 1)

                for k, (name, c) in enumerate(IN_BLOCKS[:N_IN - CH]):
                    if (name, c) == ("xr", 0):
                        link(dve.memset(xr[:, :, 0:CONV - 1], 0.0))
                    scaled(name, c)
                    if name != "xr":
                        dve.engine_nop().then_inc(cq_raw, 1)
                    mix(l, k + SPL)
                    if (name, c) == ("xr", 1):
                        rows(l, "lat", 2)
                    if (name, c) == ("xr", 2):
                        for bc, lat, g, cs in (("cqbc", cq, "q_norm_g", QC), ("kvbc", ckv, "kv_norm_g", KVC)):
                            b = B[l, bc]
                            dve.wait_ge(filled, b.ready())
                            for m in range(cs):
                                dve.scalar_tensor_tensor(lat[:, m, :], lat[:, m, :], col(g, l, m), bank(b), ALU.mult,
                                                         ALU.mult).then_inc(lat_done, 1)
                            dve.engine_nop().then_inc(emptied[b.bank], 1)
                    if name == "xr":
                        cw = [vec[:, ROWS["conv_w"][0] + (l * CONV + j) * CH + c:][:, 0:1] for j in range(CONV)]
                        link(dve.tensor_scalar(xc[:, c, :], xr[:, c, 0:T], cw[0], col("conv_b", l, c), ALU.mult, ALU.add))
                        for j in range(1, CONV):
                            q = dve.scalar_tensor_tensor(xc[:, c, :], xr[:, c, j:j + T], cw[j], xc[:, c, :], ALU.mult, ALU.add)
                            if j < CONV - 1:
                                link(q)
                        q.then_inc(xc_done, 1)
                r = slice(NOPE, QKH)
                dve.tensor_scalar(kr[r, 1, :], kr[r, 0, :], col("k_head_g", l, 0, r), None, ALU.mult).then_inc(krg_done, 1)
                decay = xr[:, :, 0:T]
                dve.wait_ge(th_done, CH * (l + 1))
                link(dve.tensor_tensor(gt[:, :, :], decay, decay, ALU.mult))
                dve.scalar_tensor_tensor(ta[:, :, :], gt[:, :, :], 1.0, ta[:, :, :], ALU.add, ALU.mult).then_inc(s_done, 1)
                dve.wait_ge(ti_done, l + 1)
                dve.wait_ge(xc_done, CH * (l + 1))
                link(dve.scalar_tensor_tensor(tb[:, :, :], tb[:, :, :], 1.0, xc[:, :, :], ALU.add, ALU.mult))
                b = B[l, "krr"]
                dve.wait_ge(filled, b.ready())
                dve.wait_ge(krsq_done, l + 1)
                dve.tensor_tensor(kr[r, 0, :], bank(b, r), sinT[r, :], ALU.mult).then_inc(emptied[b.bank], 1)
                link(dve.tensor_tensor(kr[r, 1, :], kr[r, 1, :], cosT[r, :], ALU.mult))
                dve.wait_ge(emptied[b.bank], b.before + 1)
                link(dve.tensor_tensor(kr[r, 1, :], kr[r, 0, :], kr[r, 1, :], ALU.add))
                for h in range(NH):
                    b = B[l, "qr", h]
                    dve.wait_ge(filled, b.ready())
                    dve.tensor_tensor(ksq[r, h, :], bank(b, r), sinT[r, :], ALU.mult).then_inc(emptied[b.bank], 1)
                    q = dve.tensor_tensor(qT[r, h, :], qT[r, h, :], cosT[r, :], ALU.mult)
                link(q)
                dve.tensor_tensor(qT[r, :, :], qT[r, :, :], ksq[r, :, :], ALU.add).then_inc(qrot_done, 1)
                dve.wait_ge(root_done, l + 1)
                dve.tensor_tensor(tb[:, :, :], tb[:, :, :], ta[:, :, :], ALU.mult).then_inc(b_done, 1)
                dve.wait_ge(b_done, l + 1)
                rows(l, "qk", 2 * NH)
                for c in range(CH):
                    q = dve.tensor_tensor_scan(xc[:, c, :], decay[:, c, :], tb[:, c, :], 0.0, ALU.mult, ALU.add)
                scaled("gt", 0)
                for h in range(NH):
                    b = B[l, "kbc", h]
                    dve.wait_ge(filled, b.ready())
                    if h == 0:
                        dve.wait_ge(ksq_done, l + 1)
                    n = slice(0, NOPE)
                    dve.scalar_tensor_tensor(kT[n, h, :], kT[n, h, :], col("k_head_g", l, 0, n), bank(b, n), ALU.mult, ALU.mult)
                    dve.tensor_tensor(kT[r, h, :], kr[r, 1, :], bank(b, r), ALU.mult).then_inc(emptied[b.bank], 1)
                for c in range(1, CH):
                    scaled("gt", c)
                dve.engine_nop().then_inc(gt_done, 1)

                dve.wait_ge(qscale_done, l + 1)

                def maxima(t):
                    lead, n = TILES[t]
                    keys = lead + n
                    m0 = C_MASK + T - P - lead
                    for h in range(NH):
                        b = B[l, "s", t, h]
                        dve.wait_ge(filled, b.ready())
                        q = dve.tensor_tensor_reduce(out=scores[t][0:n, h, 0:keys], in0=ps[0:n, b.bank, 0:keys],
                                                     in1=con[0:n, m0:m0 + keys], scale=rt[0:n, t, h:h + 1],
                                                     scalar=-3e38, op0=ALU.add, op1=ALU.max,
                                                     accum_out=small[0:n, t, 0, h:h + 1])
                        q.then_inc(emptied[b.bank], 1)
                    dve.wait_ge(emptied[b.bank], b.before + 1)
                    dve.tensor_scalar(small[0:n, t, 1, :], small[0:n, t, 0, :], -1.0, None, ALU.mult).then_inc(sc_done, 1)

                def turned(t, h):
                    n = TILES[t][1]
                    b = B[l, "p", t, h]
                    dve.wait_ge(filled, b.ready())
                    if h >= 2:
                        dve.wait_ge(pv_done, (NH - 1) * (len(tiles(0)) * l + tiles(l).index(t)) + h - 1)
                    q = dve.tensor_copy(pT[0:NMETA, 0, 0:n], ps[0:NMETA, b.bank, 0:n])
                    if t:
                        q = dve.tensor_copy(pT[:, 0, P:(t + 1) * P], ps[:, b.bank, P:(t + 1) * P])
                    q.then_inc(emptied[b.bank], 1)

                def averages(t):
                    n = TILES[t][1]
                    o = osb[0:n, t % 2, :]
                    dve.wait_ge(exp_done, NH * (len(tiles(0)) * l + tiles(l).index(t) + 1))
                    link(dve.reciprocal(small[0:n, t, 3, :], small[0:n, t, 2, :]))
                    b = B[l, "o", t]
                    dve.wait_ge(filled, b.ready())
                    dve.tensor_tensor(o.rearrange("p (h d) -> p h d", h=NH), ps[0:n, b.bank, :].rearrange("p (h d) -> p h d", h=NH),
                                      small[0:n, t, 3, :].rearrange("p (h o) -> p h o", o=1).to_broadcast([n, NH, VH]), ALU.mult)\
                       .then_inc(emptied[b.bank], 1)
                    dve.wait_ge(emptied[b.bank], b.before + 1)
                    junk = kr[0:n, :, :].rearrange("p a t -> p (a t)")[:, 0:DH2]
                    link(dve.tensor_tensor_reduce(out=junk, in0=o, in1=o, scale=1.0, scalar=0.0, op0=ALU.mult, op1=ALU.add,
                                                  accum_out=small[0:n, t, 4, 1:2]))
                    dve.tensor_scalar(rv[0:n, t:t + 1], small[0:n, t, 4, 1:2], 1.0 / DH2, EPS, ALU.mult, ALU.add)\
                       .then_inc(var_done, 1)

                def normed(t):
                    n = TILES[t][1]
                    dve.wait_ge(rstd_done, POWERS[l, ("att", t)])
                    dve.tensor_scalar(osb[0:n, t % 2, :], osb[0:n, t % 2, :], rv[0:n, t:t + 1], None, ALU.mult)\
                       .then_inc(on_done, 1)

                high = {}
                at = MIXHI[l]
                for what in [t for t in tiles(l) if t < 2] + ["rn", 2]:
                    at += CH
                    high[what] = at

                def out_low(t):
                    lead, n = TILES[t]
                    b = B[l, "ot", t]
                    dve.wait_ge(filled, b.ready())
                    dve.wait_ge(mixhi, high[t])
                    for c in range(CH):
                        q = dve.scalar_tensor_tensor(mx[:, 1, c, lead:lead + n], ps[:, b.bank, c * P:c * P + n],
                                                     col("attn_out_g", l, c), mx[:, 0, c, lead:lead + n].bitcast(F32),
                                                     ALU.mult, ALU.subtract)
                    q.then_inc(emptied[b.bank], 1)

                def rn_scaled(cs):
                    b = B[l, "rnbc"]
                    dve.wait_ge(filled, b.ready())
                    for c in cs:
                        dve.scalar_tensor_tensor(tb[:, c, c0:T], xc[:, c, c0:T], col("rnn_out_g", l, c),
                                                 bank(b, cols=slice(c0, T)), ALU.mult, ALU.mult).then_inc(rg_done, 1)

                def rn_low():
                    for c in range(CH):
                        dve.wait_ge(mixhi, high["rn"] - CH + c + 1)
                        q = dve.tensor_tensor(rnl[:, c, c0:T], tb[:, c, c0:T], rnh[:, c, c0:T].bitcast(F32), ALU.subtract)
                    q.then_inc(rnlo, 1)

                def gelu_inner():
                    dve.wait_ge(gsq_done, l + 1)
                    link(dve.tensor_scalar(ta[:, :, :], ta[:, :, :], 0.044715, 1.0, ALU.mult, ALU.add))
                    dve.tensor_tensor(ta[:, :, :], ta[:, :, :], gt[:, :, :], ALU.mult).then_inc(ginner, 1)

                def gelu_times():
                    dve.wait_ge(gtanh, l + 1)
                    link(dve.scalar_tensor_tensor(ta[:, :, :], ta[:, :, :], 1.0, gt[:, :, :], ALU.add, ALU.mult))
                    dve.scalar_tensor_tensor(xc[:, :, :], ta[:, :, :], 0.5, xc[:, :, :], ALU.mult, ALU.mult).then_inc(rnn_done, 1)

                tl = tiles(l)
                maxima(tl[0])
                maxima(tl[1])
                gelu_inner()
                if l == 0:
                    for h in range(0, NH, 2):
                        turned(0, h)
                        if h == 2:
                            gelu_times()
                    averages(0)
                    maxima(2)
                    normed(0)
                for h in range(0, NH, 2):
                    turned(1, h)
                    if l and h == 2:
                        gelu_times()
                    mix(l, N_IN + h // 2)
                if l == 0:
                    out_low(0)
                averages(1)
                rows(l, "rnn", 1)
                normed(1)
                out_low(1)
                for h in range(0, NH, 2):
                    turned(2, h)
                    if h < 4:
                        rn_scaled((h, h + 1))
                    if h == 2:
                        dve.engine_nop().then_inc(emptied[B[l, "rnbc"].bank], 1)
                    if h == 4:
                        rn_low()
                averages(2)
                normed(2)
                out_low(2)
                dve.engine_nop().then_inc(mixlo, 1)
                for m in range(KD):
                    b = B[l, "wo", m]
                    dve.wait_ge(filled, b.ready())
                    dve.tensor_tensor(hT[:, m, c0:T], hT[:, m, c0:T], bank(b, cols=slice(c0, T)), ALU.add)\
                       .then_inc(emptied[b.bank], 1)
                    dve.wait_ge(emptied[b.bank], b.before + 1)
                    dve.engine_nop().then_inc(h_done, 1)
                    if l == 0:
                        low_chunk(1, m, c0)
                    else:
                        dve.tensor_scalar(u32[:, m, c0:T], hT[:, m, c0:T], col("norm_ffn_g", l, m), None, ALU.mult)\
                           .then_inc(u_done, 1)
                    if m < SPL:
                        mix(l, N_IN + SPL + m)
                    elif l == 0:
                        ff(m - SPL)
                if l == 0:
                    rows(0, "n2", 1)

                    def group(banks, k, gate_at, m, lows):
                        dve.wait_ge(filled, gate_at)
                        for q in range(2):
                            dve.tensor_tensor(gsf[:, q, :], ps[:, banks[q], 0:T], rsb[:, :], ALU.mult)\
                               .then_inc(emptied[banks[q]], 1)
                        dve.engine_nop().then_inc(gs_done, 1)
                        lows()
                        dve.wait_ge(sgff, k + 1)
                        dve.wait_ge(alo_done, k + 1)
                        dve.wait_ge(gs_done, k + 1)
                        link(dve.scalar_tensor_tensor(aff[:, :, :], tff[:, :, :], 1.0, gsf[:, :, :], ALU.add, ALU.mult))
                        dve.wait_ge(filled, gate_at + 2)
                        for q in range(2):
                            dve.scalar_tensor_tensor(aff[:, q, :], aff[:, q, :], 0.5, ps[:, banks[2 + q], 0:T], ALU.mult, ALU.mult)\
                               .then_inc(emptied[banks[2 + q]], 1)
                        dve.engine_nop().then_inc(aff_done, 1)
                        dve.wait_ge(ahi_done, k + 1)
                        dve.tensor_tensor(alo[:, bass.ds(m, 2), :], aff[:, :, :], ahi[:, bass.ds(m, 2), :].bitcast(F32),
                                          ALU.subtract).then_inc(alo_done, 1)

                    dve.wait_ge(rsb_done, 2)
                    dve.engine_nop().then_inc(alo_done, 1)
                    with ch.loop(5, 2) as i:
                        for g, banks in enumerate(([0, 1, 2, 3], [4, 5, 6, 7])):
                            j = SPL + 4 * g
                            ff(j, i, 4)
                            ff(j + 1, i, 4)
                            group(banks, 2 * i + g, FFB + 2 + 4 * g + 8 * i, 4 * i + 2 * g,
                                  lambda: (ff(j + 2, i, 4), ff(j + 3, i, 4)))
                    ff(44)
                    ff(45)
                    group([0, 1, 2, 3], 10, FFB + 42, 20, lambda: (ff(46), ff(47)))
                    for m in range(KD):
                        i, q = divmod(m, 4)
                        b = B["dn", q]
                        dve.wait_ge(filled, b.ready(i))
                        link(dve.tensor_tensor(gsf[:, m % 2, :], bank(b), rsb[:, :], ALU.mult))
                        dve.engine_nop().then_inc(emptied[b.bank], 1)
                        dve.tensor_tensor(hT[:, m, :], hT[:, m, :], gsf[:, m % 2, :], ALU.add).then_inc(h_done, 1)
                        dve.wait_ge(h_done, 2 * KD + m + 1)
                        if m < KD - 2:
                            ff(48 + 2 * m)
                            ff(49 + 2 * m)
                        if m == KD - 2:
                            lo(SPLIT0[1], *mix_piece(1, 0))
                            lo(SPLIT0[1] + 1, *mix_piece(1, 1))
                        low_chunk(2, m, 0)

            b = B[1, "n2ss"]
            dve.wait_ge(filled, b.ready())
            dve.tensor_scalar(rv[:, 3:5], ps[:, b.bank, 0:2], 1.0 / D, EPS, ALU.mult, ALU.add).then_inc(var_done, 1)
            dve.engine_nop().then_inc(emptied[b.bank], 1)
            b = B["lg"]
            dve.wait_ge(filled, b.ready())
            dve.memset(sel[:, :, :], 0.0)
            dve.memset(gate[:, :, :], 0.0)
            dve.memset(pos[:, :, :], 0.0)
            dve.tensor_copy(identr[:, :], ident)
            dve.wait_ge(rstd_done, POWERS[1, "n2"])
            for t in range(2):
                q = dve.tensor_scalar(lgt[:, t, :], ps[:, b.bank, t * NE:(t + 1) * NE], rv[:, t + 3:t + 4], None, ALU.mult)
            link(q)
            dve.engine_nop().then_inc(emptied[b.bank], 1)
            for t in range(2):
                q = dve.max(top[:, t, :], lgt[:, t, :])
            link(q)
            for t in range(2):
                q = dve.max_index(topi[:, t, :], top[:, t, :], lgt[:, t, :])
            link(q)
            link(dve.tensor_copy(topf[:, :, :], topi[:, :, :]))
            for t in range(2):
                q = dve.tensor_tensor(rtmp[:, 0, t:t + 1], top[:, t, 1:2], top[:, t, 0:1], ALU.subtract)
            q.then_inc(top_done, 1)
            dve.wait_ge(topx, 1)
            link(dve.tensor_scalar(rtmp[:, 2, 0:2], rtmp[:, 1, 0:2], 1.0, None, ALU.add))
            link(dve.reciprocal(rtmp[:, 2, 0:2], rtmp[:, 2, 0:2]))
            link(dve.tensor_tensor(rtmp[:, 3, 0:2], rtmp[:, 2, 0:2], rtmp[:, 1, 0:2], ALU.mult))
            e8 = con[:, C_E8:C_E8 + NE]
            for t in range(2):
                dve.tensor_scalar(rtmp[:, 4, :], e8, topf[:, t, 0:1], None, ALU.is_equal)
                link(dve.tensor_scalar(rtmp[:, 5, :], e8, topf[:, t, 1:2], None, ALU.is_equal))
                dve.tensor_tensor(sel[:, t, 0:NE], rtmp[:, 4, :], rtmp[:, 5, :], ALU.add)
                link(dve.tensor_scalar(rtmp[:, 4, :], rtmp[:, 4, :], rtmp[:, 2, t:t + 1], None, ALU.mult))
                link(dve.scalar_tensor_tensor(gate[:, t, 1:NE + 1], rtmp[:, 5, :], rtmp[:, 3, t:t + 1], rtmp[:, 4, :],
                                              ALU.mult, ALU.add))
            dve.engine_nop().then_inc(sel_done, 1)
            for t in range(2):
                for hf in range(2):
                    b = B["ut", t, hf]
                    n = 2 * t + hf
                    dve.wait_ge(tok_hi, n + 1)
                    v = slice(t * D + hf * 512, t * D + hf * 512 + 512)
                    dve.scalar_tensor_tensor(ulo[:, :, :].rearrange("p k t -> p (k t)")[:, v], ps[:, b.bank, :],
                                             rv[:, t + 3:t + 4], uhi[:, :, :].rearrange("p k t -> p (k t)")[:, v].bitcast(F32),
                                             ALU.mult, ALU.subtract)\
                       .then_inc(emptied[b.bank], 1)
            b = B["cum"]
            dve.wait_ge(filled, b.ready())
            for t in range(2):
                dve.tensor_copy(pos[:, t, 0:NE], ps[:, b.bank, t * NE:t * NE + NE])
            link(dve.tensor_reduce(rtmp[:, 0, 0:1], ps[:, b.bank, 2 * NE:3 * NE], AX.X, ALU.max))
            dve.engine_nop().then_inc(emptied[b.bank], 1)
            dve.tensor_scalar(flag[:, :], rtmp[:, 0, 0:1], float(P), None, ALU.is_gt).then_inc(flag_done, 1)
            dve.engine_nop().then_inc(tok_lo, 1)
            dve.memset(onehT[:, :, :].bitcast(F32), 0.0)
            dve.memset(ylo[:, :].bitcast(F32), 0.0)
            for t in range(2):
                for hf in range(2):
                    b = B["ht", t, hf]
                    dve.wait_ge(emptied[b.bank], b.before + 1)
            dve.memset(yhi[:, :].bitcast(F32), 0.0)
            dve.engine_nop().then_inc(hact_done, 1)
            dve.engine_nop().then_inc(gate_read, 1)

            def hot(e, p):
                for t in range(2):
                    q = dve.tensor_scalar(onehot[:, t, :], con[:, C_IOTA + P * p:C_IOTA + P * p + P],
                                          pos[:, t, bass.ds(e, 1)], sel[:, t, bass.ds(e, 1)], ALU.is_equal, ALU.mult)
                q.then_inc(hot_done, 1)

            def experts(p):
                e0 = NE * p
                hot(0, p)
                base = [(XB[b] * NE + 4) * p for b in range(2)]
                hbase = [XH[b] * NE * p for b in range(2)]
                base = [b + 2 for b in base]

                def add_expert(t, n_full, gcol):
                    for bk in range(2):
                        dve.wait_ge(xr_full[bk], n_full[bk])
                        v = slice(bk * 512, bk * 512 + 512)
                        dve.scalar_tensor_tensor(acc[:, t, v], ps[:, 6 + bk, :], gate[:, t, bass.ds(gcol, 1)],
                                                 acc[:, t, v], ALU.mult, ALU.add).then_inc(xr_free[bk], 1)

                def result(n_y):
                    dve.wait_ge(yhi_done, n_y)
                    dve.tensor_tensor(ylo[:, :], ps[:, 4:6, :].rearrange("p b n -> p (b n)"), yhi[:, :].bitcast(F32),
                                      ALU.subtract).then_inc(ylo_done, 1)

                with dve.Fori(0, NE) as e:
                    n0 = [base[bk] + XB[bk] * e for bk in range(2)]
                    used = W0 + EP * (e + e0)
                    two = "p (b n) -> p b n"

                    def w(*js):
                        for j in js:
                            land, src = expert_piece(j)
                            lo(MOES0 + j + EP * e0, land + PER_EXPERT * e0, src, e, PER_EXPERT)

                    def turned(k0, bks, k):
                        for bk, cnt, blk in bks:
                            dve.wait_ge(xr_hi[bk], hbase[bk] + k + XH[bk] * e)
                            dve.tensor_tensor(hel[:, k0:k0 + cnt, :], ps[:, 6 + bk, 0:cnt * P].rearrange("p (k n) -> p k n", k=cnt),
                                              heh[:, k0:k0 + cnt, :].bitcast(F32), ALU.subtract).then_inc(xr_free[bk], 1)
                            k0 += cnt

                    def silu(hf, width):
                        dve.wait_ge(sg_done, 2 * (e + e0) + hf + 1)
                        dve.scalar_tensor_tensor(act1[:, 0:2 * width].rearrange(two, b=2), sg[:, 0:2 * width].rearrange(two, b=2),
                                                 1.0, ps[:, 0:2, 0:width], ALU.add, ALU.mult).then_inc(gate_read, 1)

                    def times_up(hf, width):
                        dve.wait_ge(w_used, used + 8 * hf + 8)
                        dve.wait_ge(gate_read, 2 * (e + e0) + hf + 2)
                        half = slice(HALF_A * hf, HALF_A * hf + 2 * width)
                        dve.scalar_tensor_tensor(hact[:, half].rearrange(two, b=2), act1[:, 0:2 * width].rearrange(two, b=2), 0.5,
                                                 ps[:, 2:4, 0:width], ALU.mult, ALU.mult).then_inc(hact_done, 1)

                    w(0, 1, 2)
                    result((NE + 1) * p + e + 1)
                    w(3, 4, 5, 6)
                    silu(0, HALF_A // 2)
                    add_expert(0, [n0[0] + 1, n0[1] + 1], e)
                    w(7, 8, 9)
                    add_expert(1, [n0[0] + 2, n0[1] + 2], e)
                    w(10)
                    times_up(0, HALF_A // 2)
                    w(11)
                    dve.wait_ge(xr_full[0], n0[0] + 3)
                    dve.tensor_copy(onehT[:, :, :], ps[:, 6, 0:2 * P].rearrange("p (t n) -> p t n", t=2)).then_inc(xr_free[0], 1)
                    hot(e + 1, p)
                    w(12, 13, 14)
                    silu(1, HALF_B // 2)
                    w(15)
                    turned(0, TURN_A, 1)
                    w(16, 17, 18)
                    times_up(1, HALF_B // 2)
                    w(19, 20, 21, 22)
                    turned(6, TURN_B, 2)
                    w(23)
                result((NE + 1) * (p + 1))
                for t in range(2):
                    add_expert(t, [base[bk] + XB[bk] * NE + t + 1 for bk in range(2)], NE)

            experts(0)
            more = dve.value_load(flag[0:1, 0:1], min_val=0, max_val=1)
            with dve.If(more > 0):
                experts(1)
            with dve.Else():
                dve.nop()
            dve.nop()
            dve.engine_nop().then_inc(acc_done, 1)

        @block.tensor
        def _(pe):
            pe.wait_ge(ready0, 1)
            pe.wait_ge(con_in, 16)
            pe.wait_ge(x_in, 32)
            for c in range(KD):
                b = B["x", c]
                fill(pe, b)
                for t, (lead, n) in enumerate(TILES):
                    q = pe.transpose(ps[:, b.bank, lead:lead + n], xin[0:n, t, c * P:(c + 1) * P], ident[0:n, 0:n])
                q.then_inc(filled, 1)
            pe.wait_ge(vec_in, 16 * len(ROWS))
            b = B["vec"]
            fill(pe, b)
            pe.transpose(ps[:, b.bank, 0:P], vrow[:, :], ident).then_inc(filled, 1)

            def ones(rows, n):
                return one[rows, :].to_broadcast([rows.stop - rows.start, n])

            def sums(bk, src, parts):
                for i, (c, r, (at, n)) in enumerate(parts):
                    q = pe.matmul(ps[0:n, bk, 0:T], con[r, at:at + n], src(c)[r, :], start=(i == 0), stop=(i == len(parts) - 1))
                return q

            def spread(bk, row, rows, width=P):
                return pe.matmul(ps[0:width, bk, 0:T], ident[0:rows, row:row + 1].to_broadcast([rows, width]), rr[0:rows, :],
                                 start=True, stop=True)

            def chunk_ready(s, i=0, per=0):
                pe.wait_ge(lo_done, s + 1 + per * i)

            def dense_block(b, s, ks, n, c0, x_of, row0=0, start=True, stop=True, wait_x=None):
                chunk_ready(s)
                for kk in ks:
                    if wait_x is not None:
                        pe.wait_ge(ulo_done, wait_x + kk + 1)
                    at = (kk - row0) * n
                    w = (whi[:, s % SPL, at:at + n], wlo[:, s % SPL, at:at + n])
                    q = matmul3(pe, ps[0:n, b.bank, c0:T], w, x_of(kk, slice(c0, T)), start and kk == ks[0], stop and kk == ks[-1])
                return q

            def normed_in(kk, cols):
                return uhi[:, kk, cols], ulo[:, kk, cols]

            def dense_in(kk, cols):
                return ahi[:, kk, cols], alo[:, kk, cols]

            for l in range(DEPTH):
                c0 = first_token(l)
                def w_in_block(k):
                    name, c = IN_BLOCKS[k]
                    b = B[l, name, c]
                    fill(pe, b)
                    dense_block(b, SPLIT0[l] + k, range(KD), W_IN_PIECES[k][2], 0, normed_in,
                                wait_x=2 * KD * l if k == 0 else None).then_inc(filled, 1)

                for k, (name, c) in enumerate(IN_BLOCKS[:N_IN - CH]):
                    w_in_block(k)
                    if k == 0:
                        b = B[l, "n1ss"]
                        fill(pe, b)
                        pe.wait_ge(nsq_done, 2 * KD * l + KD)
                        sums(b.bank, lambda c: u32[:, c, :], [(c, slice(0, P), (C_D, 1)) for c in range(KD)]).then_inc(filled, 1)
                    if k == 2:
                        b = B[l, "n1bc"]
                        fill(pe, b)
                        pe.wait_ge(rows_done, ROWS_DONE[l, "n1"])
                        spread(b.bank, 0, 1).then_inc(filled, 1)
                    if (name, c) == ("xr", 0):
                        b = B[l, "latss"]
                        fill(pe, b)
                        pe.wait_ge(squares, 3 * l + 2)
                        parts = [(c, slice(0, P), (C_LATQ if c < QC else C_LATK, 2)) for c in range(QC + KVC)]
                        sums(b.bank, lambda c: u32[:, c, :], parts).then_inc(filled, 1)
                    if (name, c) == ("xr", 2):
                        pe.wait_ge(rows_done, ROWS_DONE[l, "lat"])
                        for row, bc in enumerate(("cqbc", "kvbc")):
                            b = B[l, bc]
                            fill(pe, b)
                            spread(b.bank, row, 2).then_inc(filled, 1)

                def queries(hs):
                    n = MIX0[l] + UQ
                    wq = raw[:, n % RAW, 0:QC * NH * QKH].rearrange("p (k c) -> p k c", k=QC)
                    pe.wait_ge(landed[n % RAW], 16 * (n // RAW + 1))
                    pe.wait_ge(lat_done, 5 * l + 3)
                    for h in hs:
                        b = B[l, "uq", h]
                        fill(pe, b)
                        for k in range(QC):
                            q = pe.matmul(bank(b, slice(0, QKH)), wq[:, k, h * QKH:(h + 1) * QKH], cq[:, k, :],
                                          start=(k == 0), stop=(k == QC - 1))
                        q.then_inc(filled, 1)

                queries(range(NH // 2))
                pe.wait_ge(gdiag_in, 64 * (l + 1))
                for kind, name in enumerate(("wa", "wi")):
                    for c in range(CH):
                        b = B[l, name, c]
                        fill(pe, b)
                        pe.wait_ge(xc_done, CH * l + c + 1)
                        pe.matmul(bank(b), gdiag[:, kind, c, :], xc[:, c, :], start=True, stop=True).then_inc(filled, 1)
                queries(range(NH // 2, NH))
                r = slice(NOPE, QKH)
                rot = con[r, C_ROT:C_ROT + ROPE]
                b = B[l, "krr"]
                fill(pe, b)
                pe.wait_ge(krg_done, l + 1)
                pe.matmul(bank(b, r), rot, kr[r, 1, :], start=True, stop=True).then_inc(filled, 1)
                n = MIX0[l] + UKV
                wkv = raw[:, n % RAW, 0:KVC * NH * (NOPE + VH)].rearrange("p (k c) -> p k c", k=KVC)
                pe.wait_ge(landed[n % RAW], 16 * (n // RAW + 1))
                pe.wait_ge(lat_done, 5 * l + 5)
                for h in range(NH):
                    b = B[l, "kn", h]
                    fill(pe, b)
                    for k in range(KVC):
                        at = h * (NOPE + VH)
                        q = pe.matmul(bank(b, slice(0, NOPE)), wkv[:, k, at:at + NOPE], ckv[:, k, :],
                                      start=(k == 0), stop=(k == KVC - 1))
                    q.then_inc(filled, 1)
                for h in range(NH):
                    b = B[l, "qr", h]
                    fill(pe, b)
                    u = B[l, "uq", h]
                    pe.wait_ge(emptied[u.bank], u.before + 1)
                    pe.matmul(bank(b, r), rot, qT[r, h, :], start=True, stop=True).then_inc(filled, 1)
                for t, (lead, m) in enumerate(TILES):
                    b = B[l, "v", t]
                    fill(pe, b)
                    for k in range(KVC):
                        wv = wkv[:, k, :].rearrange("p (h d) -> p h d", h=NH)[:, :, NOPE:]
                        q = pe.matmul(ps[0:m, b.bank, :].rearrange("p (h d) -> p h d", h=NH), ckv[:, k, lead:lead + m], wv,
                                      start=(k == 0), stop=(k == KVC - 1))
                    q.then_inc(filled, 1)
                b = B[l, "qkss"]
                fill(pe, b)
                pe.wait_ge(ksq_done, l + 1)
                pe.wait_ge(krsq_done, l + 1)
                parts = [(h, slice(0, QKH), (C_HEAD + 15 - h, 2 * NH)) for h in range(NH)]
                parts += [(NH + h, slice(0, NOPE), (C_HEAD + 15 - NH - h, 2 * NH)) for h in range(NH)]
                parts += [(2 * NH, r, (C_KR, 2 * NH))]

                def source(c):
                    return u32[:, c, :] if c < NH else ksq[:, c - NH, :] if c < 2 * NH else kr[:, 2, :]

                sums(b.bank, source, parts).then_inc(filled, 1)
                w_in_block(N_IN - CH)
                pe.wait_ge(rows_done, ROWS_DONE[l, "qk"])
                b = B[l, "qrt"]
                fill(pe, b)
                for t, (lead, n) in enumerate(TILES):
                    q = pe.transpose(ps[0:n, b.bank, NH * t:NH * t + NH], rr[0:NH, lead:lead + n], ident[0:NH, 0:NH])
                q.then_inc(filled, 1)
                for h in range(NH):
                    b = B[l, "kbc", h]
                    fill(pe, b)
                    spread(b.bank, NH + h, 2 * NH, QKH).then_inc(filled, 1)
                for k in range(N_IN - CH + 1, N_IN):
                    w_in_block(k)

                pe.wait_ge(qrot_done, l + 1)

                def score(t):
                    lead, n = TILES[t]
                    for h in range(NH):
                        b = B[l, "s", t, h]
                        fill(pe, b)
                        kb = B[l, "kbc", h]
                        pe.wait_ge(emptied[kb.bank], kb.before + 1)
                        pe.matmul(ps[0:n, b.bank, 0:lead + n], qT[0:QKH, h, lead:lead + n], kT[0:QKH, h, 0:lead + n],
                                  start=True, stop=True).then_inc(filled, 1)

                def values(t):
                    lead, n = TILES[t]
                    turn = len(tiles(0)) * l + tiles(l).index(t)
                    fill(pe, B[l, "o", t])
                    for h in range(NH + 1):
                        if h < NH:
                            b = B[l, "p", t, h]
                            fill(pe, b)
                            pe.wait_ge(exp_done, NH * turn + h + 1)
                            for j in range(t + 1):
                                kl, kn = TILES[j]
                                q = pe.transpose(ps[0:kn, b.bank, j * P:j * P + n], scores[t][0:n, h, kl:kl + kn], ident[0:n, 0:n])
                            q.then_inc(filled, 1)
                        if h:
                            g = h - 1
                            b = B[l, "p", t, g]
                            pe.wait_ge(emptied[b.bank], b.before + 1)
                            for j in range(t + 1):
                                kn = TILES[j][1]
                                q = pe.matmul(ps[0:n, B[l, "o", t].bank, g * VH:(g + 1) * VH], pT[0:kn, g % 2, j * P:j * P + n],
                                              vt[0:kn, j, g * VH:(g + 1) * VH], start=(j == 0), stop=(j == t))
                            q.then_inc(pv_done if g < NH - 1 else filled, 1)

                def out_turned(t):
                    n = TILES[t][1]
                    b = B[l, "ot", t]
                    fill(pe, b)
                    pe.wait_ge(on_done, len(tiles(0)) * l + tiles(l).index(t) + 1)
                    for c in range(CH):
                        q = pe.transpose(ps[:, b.bank, c * P:c * P + n], osb[0:n, t % 2, c * P:(c + 1) * P], ident[0:n, 0:n])
                    q.then_inc(filled, 1)

                for what, t in ATTENTION[l][:-1]:
                    if what == "scores":
                        score(t)
                    elif what == "values":
                        values(t)
                    elif what == "out":
                        out_turned(t)
                    elif what == "rnss":
                        b = B[l, "rnss"]
                        fill(pe, b)
                        pe.wait_ge(squares, 3 * (l + 1))
                        sums(b.bank, lambda c: ta[:, c, :], [(c, slice(0, P), (C_DH2, 1)) for c in range(CH)]).then_inc(filled, 1)
                    else:
                        b = B[l, "rnbc"]
                        fill(pe, b)
                        pe.wait_ge(rows_done, ROWS_DONE[l, "rnn"])
                        spread(b.bank, 0, 1).then_inc(filled, 1)
                halves = range(4)
                pe.wait_ge(rnlo, l + 1)
                for m in halves:
                    b = B[l, "wo", m]
                    fill(pe, b)
                    dense_block(b, SPLIT0[l] + N_IN + m, range(CH, KD), P, c0, mix_in, stop=False)
                out_turned(2)
                pe.wait_ge(mixlo, l + 1)
                for m in range(KD):
                    b = B[l, "wo", m]
                    if m not in halves:
                        fill(pe, b)
                    dense_block(b, SPLIT0[l] + N_IN + m, range(CH) if m in halves else range(KD), P, c0, mix_in,
                                start=m not in halves).then_inc(filled, 1)
                if l == 1:
                    b = B[l, "n2ss"]
                    fill(pe, b)
                    pe.matmul(ps[0:1, b.bank, 511:512], one[:, :], one[:, :], start=True, stop=True).then_inc(w_used, W0)
                    pe.wait_ge(nsq_done, 4 * KD)
                    for t in range(2):
                        lead, n = TILES[t + 1]
                        for k in range(KD):
                            q = pe.matmul(ps[:, b.bank, t:t + 1], qT[:, k, lead:lead + n], one[:, :], start=(k == 0),
                                          stop=(k == KD - 1))
                    q.then_inc(filled, 1)
                else:
                    def group(banks, s, per, i, emp):
                        for m in range(4):
                            chunk_ready(s + m, i, per)
                            pe.wait_ge(emptied[banks[m]], emp[m])
                            for kk in range(KD):
                                if m == 0 and not per:
                                    pe.wait_ge(ulo_done, KD + kk + 1)
                                sl = (s + m) % SPL
                                at = kk * P
                                q = matmul3(pe, ps[:, banks[m], 0:T], (whi[:, sl, at:at + P], wlo[:, sl, at:at + P]),
                                            (uhi[:, kk, :], ulo[:, kk, :]), kk == 0, kk == KD - 1)
                            q.then_inc(filled, 1)
                            if not per and m < 2:
                                if m == 0:
                                    pe.wait_ge(emptied[4], B["ff", 0].before)
                                    pe.wait_ge(nsq_done, 2 * KD)
                                    sums(4, lambda c: u32[:, c, :], [(c, slice(0, P), (C_D, 1)) for c in range(KD)])\
                                        .then_inc(n2_filled, 1)
                                else:
                                    pe.wait_ge(rows_done, ROWS_DONE[0, "n2"])
                                    spread(4, 0, 1).then_inc(n2_filled, 1)

                    group([0, 1, 2, 3], FFS0, 0, 0, [B["ff0", q].before for q in range(4)])
                    pe.wait_ge(rsb_done, 2)
                    with pe.Fori(0, 5) as i:
                        group([4, 5, 6, 7], FFS0 + 4, 8, i, [B["ff", q].emptied(i) for q in range(4)])
                        group([0, 1, 2, 3], FFS0 + 8, 8, i, [B["ff", q].emptied(i) for q in range(4, 8)])
                    def down(m, hf):
                        b = B["dn", m % 4]
                        k0 = hf * FC // 2
                        return dense_block(b, FFS0 + 44 + 2 * m + hf, range(k0, k0 + FC // 2), P, 0, dense_in, row0=k0,
                                           start=hf == 0, stop=hf == 1)

                    pe.wait_ge(alo_done, 7)
                    for m in range(2):
                        b = B["dn", m]
                        pe.wait_ge(emptied[b.bank], b.emptied(0))
                        down(m, 0)
                    pe.wait_ge(alo_done, 12)
                    for m in range(KD):
                        i, q = divmod(m, 4)
                        if m >= 2:
                            b = B["dn", q]
                            pe.wait_ge(emptied[b.bank], b.emptied(i))
                            down(m, 0)
                        down(m, 1).then_inc(filled, 1)

            b = B["lg"]
            fill(pe, b)
            pe.wait_ge(rw_in, 16)
            pe.wait_ge(u_done, KD)
            for t in range(2):
                lead, n = TILES[t + 1]
                for k in range(KD):
                    q = pe.matmul(ps[:, b.bank, t * NE:(t + 1) * NE], u32[:, k, lead:lead + n], rw[:, k, :],
                                  start=(k == 0), stop=(k == KD - 1))
            q.then_inc(filled, 1)
            for name, src in (("ut", u32), ("ht", hT)):
                for t in range(2):
                    lead, n = TILES[t + 1]
                    for hf in range(2):
                        b = B[name, t, hf]
                        fill(pe, b)
                        for c in range(4):
                            q = pe.transpose(ps[:, b.bank, c * P:(c + 1) * P], src[:, 4 * hf + c, lead:lead + n], ident)
                        q.then_inc(filled, 1)
            b = B["cum"]
            fill(pe, b)
            pe.wait_ge(sel_done, 1)
            before = con[:, C_LT:C_LT + P]
            every = one[:, :].to_broadcast([P, P])
            pe.matmul(ps[:, b.bank, 0:NE], before, sel[:, 0, 0:NE], start=True, stop=True)
            pe.matmul(ps[:, b.bank, NE:2 * NE], every, sel[:, 0, 0:NE], start=True, stop=False)
            pe.matmul(ps[:, b.bank, NE:2 * NE], before, sel[:, 1, 0:NE], start=False, stop=True)
            pe.matmul(ps[:, b.bank, 2 * NE:3 * NE], every, sel[:, 0, 0:NE], start=True, stop=False)
            pe.matmul(ps[:, b.bank, 2 * NE:3 * NE], every, sel[:, 1, 0:NE], start=False, stop=True).then_inc(filled, 1)

            tokh = uhi[:, :, :].rearrange("p k t -> p (k t)")
            tokl = ulo[:, :, :].rearrange("p k t -> p (k t)")
            pe.wait_ge(tok_lo, 1)
            for hf in range(2):
                b = B["ht", 1, hf]
                pe.wait_ge(emptied[b.bank], b.before + 1)
            for b in (4, 5, 6, 7):
                pe.wait_ge(emptied[b], pl.before[b])

            def experts(p):
                e0 = NE * p
                base = [(XB[b] * NE + 4) * p for b in range(2)]

                def room(bk, k):
                    if isinstance(k, int) and k == 0:
                        return
                    pe.wait_ge(xr_free[bk], k)

                def gather(part, blk7, blk6):
                    for q, (bk, k) in enumerate(((1, blk7), (0, blk6))):
                        room(bk, k - 1)
                        for c in range(4):
                            at = (4 * q + c) * P
                            for t in range(2):
                                m = pe.matmul(ps[:, 6 + bk, c * P:(c + 1) * P], part[:, t * D + at:t * D + at + P],
                                              onehot[:, t, :], start=(t == 0), stop=(t == 1))
                        m.then_inc(xr_full[bk], 1)

                def combine(t, blk6, blk7):
                    for hf in range(2):
                        room(hf, (blk6, blk7)[hf] - 1)
                        v = slice(hf * 512, hf * 512 + 512)
                        pe.matmul(ps[:, 6 + hf, :], onehT[:, t, :], yhi[:, v], start=True, stop=False)
                        pe.matmul(ps[:, 6 + hf, :], onehT[:, t, :], ylo[:, v], start=False, stop=True)\
                          .then_inc(xr_full[hf], 1)

                pe.wait_ge(hot_done, (NE + 1) * p + 1)
                gather(tokh, base[1] + 1, base[0] + 1)
                gather(tokl, base[1] + 2, base[0] + 2)
                base = [b + 2 for b in base]
                with pe.Fori(0, NE) as e:
                    n0 = [base[b] + XB[b] * e for b in range(2)]

                    def weights(j):
                        pe.wait_ge(lo_done, MOES0 + j + 1 + EP * (e + e0))
                        return j % SPL

                    def hidden(hf, kind, width, js):
                        for c in js:
                            sl = weights(8 * hf + 4 * kind + c)
                            if c == 0:
                                pe.wait_ge((gate_read, hact_done)[kind], 2 * (e + e0) + hf + 1)
                            for k in range(2):
                                kk = 2 * c + k
                                for xs, ws in ((xeh, (whi, wlo)), (xel, (whi,))):
                                    for w in ws:
                                        for n in range(2):
                                            at = k * 2 * width + n * width
                                            q = pe.matmul(ps[:, 2 * kind + n, 0:width], xs[:, kk, :], w[:, sl, at:at + width],
                                                          start=(kk == 0 and xs is xeh and w is whi),
                                                          stop=(kk == KD - 1 and xs is xel), skip_group_check=True)
                            q.then_inc(w_used, 1)

                    def turn(k0, bks):
                        for bk, cnt, blk in bks:
                            room(bk, n0[bk] + blk - 1)
                            for j in range(cnt):
                                at = (k0 + j) * P
                                q = pe.transpose(ps[:, 6 + bk, j * P:(j + 1) * P], hact[:, at:at + P], ident)
                            q.then_inc(xr_full[bk], 1)
                            k0 += cnt

                    def down(*js):
                        for j in js:
                            sl = weights(j)
                            c, n = divmod(j - 16, 2)
                            for k in range(2 if c == 3 else 3):
                                kk = 3 * c + k
                                for xs, w in ((heh, whi), (heh, wlo), (hel, whi)):
                                    at = k * 512
                                    q = pe.matmul(ps[:, 4 + n, :], xs[:, kk, :], w[:, sl, at:at + 512],
                                                  start=(kk == 0 and xs is heh and w is whi),
                                                  stop=(kk == FEC - 1 and xs is hel), skip_group_check=True)
                            q.then_inc(w_used, 1)

                    for bk in range(2):
                        pe.wait_ge(xr_free[bk], n0[bk])
                    hidden(0, 0, HALF_A // 2, range(4))
                    pe.wait_ge(ylo_done, (NE + 1) * p + e + 1)
                    combine(0, n0[0] + 1, n0[1] + 1)
                    hidden(0, 1, HALF_A // 2, (0, 1))
                    combine(1, n0[0] + 2, n0[1] + 2)
                    hidden(0, 1, HALF_A // 2, (2, 3))
                    room(0, n0[0] + 2)
                    for t in range(2):
                        q = pe.matmul(ps[:, 6, t * P:(t + 1) * P], onehot[:, t, :], identr[:, :], start=True, stop=True)
                    q.then_inc(xr_full[0], 1)
                    hidden(1, 0, HALF_B // 2, range(4))
                    pe.wait_ge(hact_done, 2 * (e + e0) + 2)
                    turn(0, TURN_A)
                    hidden(1, 1, HALF_B // 2, range(4))
                    pe.wait_ge(hot_done, (NE + 1) * p + e + 2)
                    gather(tokh, n0[1] + 4, n0[0] + 5)
                    pe.wait_ge(xr_free[1], n0[1] + 3)
                    pe.wait_ge(xr_free[0], n0[0] + 4)
                    down(16)
                    gather(tokl, n0[1] + 5, n0[0] + 6)
                    down(17, 18)
                    pe.wait_ge(hact_done, 2 * (e + e0) + 3)
                    turn(6, TURN_B)
                    down(19)
                    pe.wait_ge(xr_free[1], n0[1] + 6)
                    pe.wait_ge(xr_free[0], n0[0] + 7)
                    down(20, 21, 22, 23)
                pe.wait_ge(ylo_done, (NE + 1) * (p + 1))
                for t in range(2):
                    combine(t, base[0] + XB[0] * NE + t + 1, base[1] + XB[1] * NE + t + 1)

            experts(0)
            pe.wait_ge(flag_done, 1)
            more = pe.value_load(flag[0:1, 0:1], min_val=0, max_val=1)
            with pe.If(more > 0):
                experts(1)
            with pe.Else():
                pe.nop()
            pe.nop()


_INS = ["x", "positions", "meta_tokens", "norm_mix_g", "w_in", "q_norm_g", "w_uq", "kv_norm_g", "w_ukv", "q_head_g",
        "k_head_g", "conv_w", "conv_b", "w_a", "b_a", "w_i", "b_i", "lru_lambda", "attn_out_g", "rnn_out_g", "w_out",
        "norm_ffn_g", "ffn_w_gate", "ffn_w_up", "ffn_w_down", "router_w", "moe_w_gate", "moe_w_up", "moe_w_down"]


def kernel(**inputs):
    import concourse.bacc as _bacc
    from concourse.bass_utils import run_bass_kernel_spmd as _run

    nc = _bacc.Bacc("TRN2", target_bir_lowering=False, num_devices=1)
    arrays, aps = {}, {}
    given = {name: np.ascontiguousarray(inputs[name]) for name in _INS}
    given["constants"] = constants()
    for name, a in given.items():
        arrays[f"in_{name}_dram"] = a
        aps[name] = nc.dram_tensor(f"in_{name}_dram", a.shape, mybir.dt.from_np(a.dtype), kind="ExternalInput").ap()
    out = nc.dram_tensor("out_0_dram", (1, SEQ, D), F32, kind="ExternalOutput").ap()
    build(nc, aps, out)
    r = _run(nc, [arrays], core_ids=[0])
    return r.results[0]["out_0_dram"]
```
